# Optimizing a Trainium2 kernel written in Bass

```python
import jax, jax.numpy as jnp
from jax import lax
import numpy as np

D_MODEL = 1024
BATCH = 1
SEQ = 512
DEPTH = 2
DEC_BATCH = 1
DEC_SEQ = 256
PAST_LEN = 128

N_MIXERS = 2
N_A = (DEPTH + 1) // 2
N_B = DEPTH // 2
CHUNK = 64
EPS = 1e-6

MLSTM_HEADS = 4
MLSTM_QK = D_MODEL // 2
MLSTM_V = D_MODEL
MLSTM_DK = MLSTM_QK // MLSTM_HEADS
MLSTM_DV = MLSTM_V // MLSTM_HEADS
MLSTM_IN = 2 * MLSTM_QK + 2 * MLSTM_V + 4 * MLSTM_HEADS
M_INIT = -1e30

GLA_HEADS = 4
GLA_K = D_MODEL // 2
GLA_V = D_MODEL
GLA_DK = GLA_K // GLA_HEADS
GLA_DV = GLA_V // GLA_HEADS
GLA_RANK = 16
GLA_TAU = 16.0
GLA_IN = 2 * GLA_K + 2 * GLA_V + 2 * GLA_RANK

D_FF = ((8 * D_MODEL // 3 + 255) // 256) * 256

kernel_name = "bidir_mlstm_gla_hybrid_encoder"

def _rmsnorm(x, g):
    xf = x.astype(jnp.float32)
    y = xf * lax.rsqrt(jnp.mean(xf * xf, axis=-1, keepdims=True) + EPS)
    return (y * g.astype(jnp.float32)).astype(x.dtype)

def _heads(a, n_heads):
    b, t, _ = a.shape
    return a.reshape(b, t, n_heads, -1).transpose(0, 2, 1, 3)

def _merge_heads(a):
    b, n, t, d = a.shape
    return a.transpose(0, 2, 1, 3).reshape(b, t, n * d)

def _to_chunks(a):
    b, h, t = a.shape[:3]
    a = a.reshape((b, h, t // CHUNK, CHUNK) + a.shape[3:])
    return jnp.moveaxis(a, 2, 0)

def _from_chunks(a):
    a = jnp.moveaxis(a, 0, 2)
    return a.reshape(a.shape[:2] + (a.shape[2] * a.shape[3],) + a.shape[4:])

def _flip(a):
    return jnp.flip(a, axis=2)

def _mlstm_scan(q, k, v, ig, lf):
    bsz, nh, _, dk = q.shape
    dv = v.shape[-1]
    causal = jnp.tril(jnp.ones((CHUNK, CHUNK), dtype=bool))

    def step(carry, inp):
        C, n, m = carry
        qc, kc, vc, ic, fc = inp
        b = jnp.cumsum(fc, axis=-1)
        dmat = jnp.where(causal, b[..., :, None] - b[..., None, :] + ic[..., None, :], -jnp.inf)
        m_inter = b + m[..., None]
        m_t = jnp.maximum(m_inter, jnp.max(dmat, axis=-1))
        w_inter = jnp.exp(m_inter - m_t)
        s = jnp.einsum('bhtd,bhjd->bhtj', qc, kc) * jnp.exp(dmat - m_t[..., None])
        num = (w_inter[..., None] * jnp.einsum('bhtd,bhdv->bhtv', qc, C)
               + jnp.einsum('bhtj,bhjv->bhtv', s, vc))
        den = w_inter * jnp.einsum('bhtd,bhd->bht', qc, n) + jnp.sum(s, axis=-1)
        hc = num / jnp.maximum(jnp.abs(den), jnp.exp(-m_t))[..., None]
        g_last = b[..., -1]
        wk_log = g_last[..., None] - b + ic
        m_new = jnp.maximum(g_last + m, jnp.max(wk_log, axis=-1))
        w_c = jnp.exp(g_last + m - m_new)
        kw = kc * jnp.exp(wk_log - m_new[..., None])[..., None]
        C = w_c[..., None, None] * C + jnp.einsum('bhjd,bhjv->bhdv', kw, vc)
        n = w_c[..., None] * n + jnp.sum(kw, axis=-2)
        return (C, n, m_new), hc

    init = (jnp.zeros((bsz, nh, dk, dv), jnp.float32),
            jnp.zeros((bsz, nh, dk), jnp.float32),
            jnp.full((bsz, nh), M_INIT, jnp.float32))
    _, hs = lax.scan(step, init, (_to_chunks(q), _to_chunks(k), _to_chunks(v),
                                  _to_chunks(ig), _to_chunks(lf)))
    return _from_chunks(hs)

def _gla_scan(q, k, v, lg):
    bsz, nh, _, dk = q.shape
    dv = v.shape[-1]
    causal = jnp.tril(jnp.ones((CHUNK, CHUNK), dtype=bool))

    def step(S, inp):
        qc, kc, vc, gc = inp
        bc = jnp.cumsum(gc, axis=-2)
        qe = qc * jnp.exp(bc)
        ke = kc * jnp.exp(-bc)
        a = jnp.where(causal, jnp.einsum('bhtd,bhjd->bhtj', qe, ke), 0.0)
        o = jnp.einsum('bhtd,bhdv->bhtv', qe, S) + jnp.einsum('bhtj,bhjv->bhtv', a, vc)
        b_last = bc[..., -1, :]
        kd = kc * jnp.exp(b_last[..., None, :] - bc)
        S = jnp.exp(b_last)[..., None] * S + jnp.einsum('bhjd,bhjv->bhdv', kd, vc)
        return S, o

    init = jnp.zeros((bsz, nh, dk, dv), jnp.float32)
    _, os_ = lax.scan(step, init, (_to_chunks(q), _to_chunks(k), _to_chunks(v), _to_chunks(lg)))
    return _from_chunks(os_)

def _mlstm_mixer(h, w_in, b_gate, head_g, w_out):
    bsz, t, _ = h.shape
    f32 = jnp.float32
    proj = h @ w_in
    q, k, v, o, gt = jnp.split(proj, [MLSTM_QK, 2 * MLSTM_QK, 2 * MLSTM_QK + MLSTM_V,
                                      2 * MLSTM_QK + 2 * MLSTM_V], axis=-1)
    q = _heads(q, MLSTM_HEADS).astype(f32) * (MLSTM_DK ** -0.5)
    k = _heads(k, MLSTM_HEADS).astype(f32)
    v = _heads(v, MLSTM_HEADS).astype(f32)
    gt = (gt + b_gate).astype(f32).reshape(bsz, t, 4, MLSTM_HEADS).transpose(2, 0, 3, 1)
    ig_f, fg_f, ig_b, fg_b = gt[0], gt[1], gt[2], gt[3]
    h_f = _mlstm_scan(q, k, v, ig_f, jax.nn.log_sigmoid(fg_f))
    h_b = _flip(_mlstm_scan(_flip(q), _flip(k), _flip(v), _flip(ig_b),
                            _flip(jax.nn.log_sigmoid(fg_b))))
    hs = _rmsnorm(h_f + h_b, head_g.reshape(MLSTM_HEADS, 1, MLSTM_DV))
    y = _merge_heads(hs) * jax.nn.sigmoid(o.astype(f32))
    return y.astype(h.dtype) @ w_out

def _gla_mixer(h, w_in, w_a2, b_a, head_g, w_out):
    f32 = jnp.float32
    proj = h @ w_in
    q, k, v, r, a_f, a_b = jnp.split(proj, [GLA_K, 2 * GLA_K, 2 * GLA_K + GLA_V,
                                            2 * GLA_K + 2 * GLA_V,
                                            2 * GLA_K + 2 * GLA_V + GLA_RANK], axis=-1)
    q = _heads(q, GLA_HEADS).astype(f32) * (GLA_DK ** -0.5)
    k = _heads(k, GLA_HEADS).astype(f32)
    v = _heads(v, GLA_HEADS).astype(f32)
    lg_f = jax.nn.log_sigmoid((a_f @ w_a2[0] + b_a[0]).astype(f32)) / GLA_TAU
    lg_b = jax.nn.log_sigmoid((a_b @ w_a2[1] + b_a[1]).astype(f32)) / GLA_TAU
    lg_f = _heads(lg_f, GLA_HEADS)
    lg_b = _heads(lg_b, GLA_HEADS)
    o_f = _gla_scan(q, k, v, lg_f)
    o_b = _flip(_gla_scan(_flip(q), _flip(k), _flip(v), _flip(lg_b)))
    os_ = _rmsnorm(o_f + o_b, head_g.reshape(GLA_HEADS, 1, GLA_DV))
    y = _merge_heads(os_) * jax.nn.silu(r.astype(f32))
    return y.astype(h.dtype) @ w_out

def _swiglu(h, w_gu, w_down):
    g, u = jnp.split(h @ w_gu, 2, axis=-1)
    return (jax.nn.silu(g) * u) @ w_down

def _trunk(x, norm_mix_g, norm_ffn_g, norm_final_g,
           mlstm_w_in, mlstm_b_gate, mlstm_head_g, mlstm_w_out,
           gla_w_in, gla_w_a2, gla_b_a, gla_head_g, gla_w_out,
           ffn_w_gu, ffn_w_down):
    for i in range(DEPTH):
        h = _rmsnorm(x, norm_mix_g[i])
        j = i // N_MIXERS
        if i % N_MIXERS == 0:
            x = x + _mlstm_mixer(h, mlstm_w_in[j], mlstm_b_gate[j], mlstm_head_g[j], mlstm_w_out[j])
        else:
            x = x + _gla_mixer(h, gla_w_in[j], gla_w_a2[j], gla_b_a[j], gla_head_g[j], gla_w_out[j])
        h = _rmsnorm(x, norm_ffn_g[i])
        x = x + _swiglu(h, ffn_w_gu[i], ffn_w_down[i])
    return _rmsnorm(x, norm_final_g)

def setup_inputs(seed: int = 0) -> dict:
    key = jax.random.key(seed)
    ks = jax.random.split(key, 20)
    f32 = jnp.float32
    nrm = lambda k, s, sc: jax.random.normal(k, s, f32) * sc
    gate_offset = jnp.repeat(jnp.array([0.0, 3.0, 0.0, 3.0], f32), MLSTM_HEADS)
    return {
        "x_prompt": nrm(ks[0], (BATCH, SEQ, D_MODEL), 1.0),
        "x_sample": nrm(ks[1], (DEC_BATCH, DEC_SEQ, D_MODEL), 1.0),
        "norm_mix_g": 1.0 + nrm(ks[2], (DEPTH, D_MODEL), 0.02),
        "norm_ffn_g": 1.0 + nrm(ks[3], (DEPTH, D_MODEL), 0.02),
        "norm_final_g": 1.0 + nrm(ks[4], (D_MODEL,), 0.02),
        "mlstm_w_in": nrm(ks[5], (N_A, D_MODEL, MLSTM_IN), D_MODEL ** -0.5),
        "mlstm_b_gate": gate_offset + nrm(ks[6], (N_A, 4 * MLSTM_HEADS), 0.1),
        "mlstm_head_g": 1.0 + nrm(ks[7], (N_A, MLSTM_V), 0.02),
        "mlstm_w_out": nrm(ks[8], (N_A, MLSTM_V, D_MODEL), MLSTM_V ** -0.5),
        "gla_w_in": nrm(ks[9], (N_B, D_MODEL, GLA_IN), D_MODEL ** -0.5),
        "gla_w_a2": nrm(ks[10], (N_B, 2, GLA_RANK, GLA_K), GLA_RANK ** -0.5),
        "gla_b_a": nrm(ks[11], (N_B, 2, GLA_K), 0.1),
        "gla_head_g": 1.0 + nrm(ks[12], (N_B, GLA_V), 0.02),
        "gla_w_out": nrm(ks[13], (N_B, GLA_V, D_MODEL), GLA_V ** -0.5),
        "ffn_w_gu": nrm(ks[14], (DEPTH, D_MODEL, 2 * D_FF), D_MODEL ** -0.5),
        "ffn_w_down": nrm(ks[15], (DEPTH, D_FF, D_MODEL), D_FF ** -0.5),
    }

def reference(x_prompt, x_sample, norm_mix_g, norm_ffn_g, norm_final_g,
              mlstm_w_in, mlstm_b_gate, mlstm_head_g, mlstm_w_out,
              gla_w_in, gla_w_a2, gla_b_a, gla_head_g, gla_w_out,
              ffn_w_gu, ffn_w_down):
    y_prompt = _trunk(x_prompt, norm_mix_g, norm_ffn_g, norm_final_g,
                      mlstm_w_in, mlstm_b_gate, mlstm_head_g, mlstm_w_out,
                      gla_w_in, gla_w_a2, gla_b_a, gla_head_g, gla_w_out,
                      ffn_w_gu, ffn_w_down)
    y_sample = _trunk(x_sample, norm_mix_g, norm_ffn_g, norm_final_g,
                      mlstm_w_in, mlstm_b_gate, mlstm_head_g, mlstm_w_out,
                      gla_w_in, gla_w_a2, gla_b_a, gla_head_g, gla_w_out,
                      ffn_w_gu, ffn_w_down)
    return (y_prompt, y_sample)


_drawn_inputs = setup_inputs


def setup_inputs(seed=0):
    import zlib

    import numpy as np

    out = dict(_drawn_inputs(seed))
    spreads = {}
    factors = {'norm_ffn_g': 2.774,
     'norm_final_g': 2.872,
     'mlstm_head_g': 3.997,
     'gla_b_a': 2.954,
     'gla_head_g': 6.312}
    for name, (base, spread) in spreads.items():
        noise = np.random.default_rng([zlib.crc32(name.encode()), seed]).standard_normal(out[name].shape)
        drawn = base * np.exp(spread * noise) if base else spread * noise
        out[name] = __import__('jax').numpy.asarray(drawn.astype(out[name].dtype))
    for name, factor in factors.items():
        out[name] = (out[name] * factor).astype(out[name].dtype)
    return out
```

```python
from contextlib import ExitStack

import concourse.bass as bass
from concourse import mybir

F32 = mybir.dt.float32
F32R = mybir.dt.float32r
ALU = mybir.AluOpType
ACT = mybir.ActivationFunctionType

P = 128
SEQS = (512, 256)
T = sum(SEQS)
HT = T // 2
TT = T // P
D = 1024
KC = D // P
NH = 4
DK = 128
DV = 256
QK = NH * DK
DFF = 2816
W = 256
EPS = 1e-6
M_INIT = -1e30
GLA_TAU = 16.0
RANK = 16
PIVOT = P // 2 - 1
BLOCKS = (8, 8, 6)
PAIRS = 25
PQ, PK, PV_, PO, POUT = 0, 1, 2, 4, 6
PGU, PDN = (8, 14, 20), (12, 18, 23)
FFP = sum(BLOCKS) // 2
NORM_S = (0, 32, 48, 80)
Y_S = (16, 64)
FIRST_T = (0, 0, 0, 0, 4, 4)
LAST_T = (3, 3, 3, 3, 5, 5)
OUTS = [(0, 0), (0, 1), (0, 2), (0, 3), (1, 3), (1, 2), (1, 1), (1, 0), (0, 4), (0, 5), (1, 5), (1, 4)]
PIECES = [[(0, j) for j in range(4)], [(1, j) for j in range(4)], [(0, 4), (0, 5), (1, 4), (1, 5)]]
UPD = ((0, 1, 2, 4), (3, 2, 1, 5))


def span(d, j):
    if d == 0:
        return j * P, (LAST_T[j] + 1 - j) * P
    return FIRST_T[j] * P, (j + 1 - FIRST_T[j]) * P


def offsets():
    out, at = {}, [0, 0]
    for d in range(2):
        for j in range(TT):
            out[d, j] = at[d]
            at[d] += span(d, j)[1]
    assert at[0] == at[1]
    return out, at[0]


OFF, PW = offsets()


def build(nc, x_prompt, x_sample, norm_mix_g, norm_ffn_g, norm_final_g,
          mlstm_w_in, mlstm_b_gate, mlstm_head_g, mlstm_w_out,
          gla_w_in, gla_w_a2, gla_b_a, gla_head_g, gla_w_out,
          ffn_w_gu, ffn_w_down, y_prompt, y_sample):
    w_in = [w[0].rearrange("(k p) n -> p k n", p=P) for w in (mlstm_w_in, gla_w_in)]
    w_out = [w[0].rearrange("(k p) n -> p k n", p=P) for w in (mlstm_w_out, gla_w_out)]
    w_gu = [ffn_w_gu[i].rearrange("(k p) n -> p k n", p=P) for i in range(2)]
    w_dn = [ffn_w_down[i].rearrange("(k p) n -> p k n", p=P) for i in range(2)]

    with ExitStack() as ctx:
        def sb(name, shape, dt=F32, to=ctx):
            return to.enter_context(nc.sbuf_tensor(name, shape, dt))

        def sem(name):
            return ctx.enter_context(nc.semaphore(name))

        xT = sb("xT", [P, KC, T])
        raw = [sb(f"raw{s}", [P, KC, W]) for s in range(2)]
        w_hi = [sb(f"w_hi{s}", [P, KC, W], F32R) for s in range(2)]
        w_lo = [sb(f"w_lo{s}", [P, KC, W], F32R) for s in range(2)]
        ht = sb("ht", [P, 4, HT])
        with ExitStack() as r:
            hs_g1 = sb("hs_g1", [P, TT, DV], F32, r)
            junk = sb("junk", [P, DV], F32, r)
        rstd = sb("rstd", [P, 2, HT])
        sq_sum = sb("sq_sum", [P, 2, HT])
        sq_new = sb("sq_new", [P, HT])
        rows = sb("rows", [64, T])
        cols = sb("cols", [P, TT, 100])
        ones = sb("ones", [P, P])
        ident = sb("ident", [P, P])
        vec_rows = sb("vec_rows", [64, P])
        vec = sb("vec", [P, 64])
        gate_bias = sb("gate_bias", [P, 1])
        gate_raw = sb("gate_raw", [P, KC, 2 * RANK])
        w_a2 = sb("w_a2", [48, QK])
        head_sq = sb("head_sq", [P, 2, TT])
        head_rstd = sb("head_rstd", [P, 2, TT])
        den = sb("den", [P, 2])
        eps_col = sb("eps_col", [P, 1])

        with ExitStack() as r:
            h_hi = sb("h_hi", [P, KC, T], F32R, r)
            h_lo = sb("h_lo", [P, KC, T], F32R, r)
        with ExitStack() as r:
            decay = sb("decay", [P, 2, 2, PW], F32, r)
            hs_m = sb("hs_m", [P, 2, TT, DV], F32, r)
        region_h = ctx.enter_context(ExitStack())
        qe = sb("qe", [P, 2, 2, T], F32, region_h)
        ke = sb("ke", [P, 2, 2, T], F32, region_h)
        bsum = sb("bsum", [P, 2, T], F32, region_h)
        a_sb = sb("a_sb", [P, 2, 2, 2, P], F32, region_h)
        k_tok = sb("k_tok", [P, 2, 4, P], F32, region_h)
        state = sb("state", [P, 2, DV], F32, region_h)
        s_piv = sb("s_piv", [P, 2, 4, DV], F32, region_h)
        hs_g = [sb("hs_g0", [P, TT, DV], F32, region_h), hs_g1]
        piv = sb("piv", [P, 2, 3, TT], F32, region_h)
        epiv = sb("epiv", [P, 2, 3, TT], F32, region_h)

        HR = 2 * T + TT * (DV + 1)
        with ExitStack() as r:
            xs = sb("xs", [P, TT, D], F32, r)
        with ExitStack() as r:
            y_parts = sb("y_parts", [P, NH, HR], F32R, r)
        with ExitStack() as r:
            a_hi = sb("a_hi", [P, 8, T], F32R, r)
            a_lo = sb("a_lo", [P, 8, T], F32R, r)
        with ExitStack() as r:
            y_fin = sb("y_fin", [P, KC, T], F32, r)
            y_tok = sb("y_tok", [P, TT, D], F32, r)
        qkv = sb("qkv", [P, NH, HR])

        with ExitStack() as r:
            g_hi = sb("g_hi", [P, KC, P], F32R, r)
            g_lo = sb("g_lo", [P, KC, P], F32R, r)
            with ExitStack() as r2:
                g_pre = sb("g_pre", [100, T], F32, r2)
                g_soft = sb("g_soft", [100, T], F32, r2)
                g_log = sb("g_log", [64, T], F32, r2)
                g_cum = sb("g_cum", [64, T], F32, r2)
                g_cols = sb("g_cols", [P, T], F32, r2)
            with ExitStack() as r2:
                sg = sb("sg", [P, 4, HT], F32, r2)
                at = sb("at", [P, 4, HT], F32, r2)
        o_gate = sb("o_gate", [P, KC, T])

        bank = [ctx.enter_context(nc.psum_tensor(f"bank{i}", [P, 512], F32)) for i in range(8)]

        q_of = [qkv[:, h, 0:T] for h in range(NH)]
        k_of = [qkv[:, h, T:2 * T] for h in range(NH)]
        v_all = qkv[:, :, 2 * T:HR].rearrange("p h (t n) -> p h t n", t=TT)
        y_hi = [y_parts[:, c // 2, (c % 2) * T:(c % 2 + 1) * T] for c in range(KC)]
        y_lo = [y_parts[:, c // 2, (2 + c % 2) * T:(3 + c % 2) * T] for c in range(KC)]
        gain = [vec[:, 8 * e:8 * e + 8] for e in range(5)]
        head_g = [vec[:, 40:48], vec[:, 48:56]]
        b_a = vec[:, 56:64]

        x_loaded = [sem(f"x_loaded{t}") for t in range(TT)]
        vec_loaded, bias_loaded, a2_loaded = sem("vec_loaded"), sem("bias_loaded"), sem("a2_loaded")
        gate_w_loaded = sem("gate_w_loaded")
        raw_loaded = [sem(f"raw_loaded{s}") for s in range(2)]
        y_stored = sem("y_stored")
        consts = sem("consts")
        vec_t, vec_ready = sem("vec_t"), sem("vec_ready")
        w_hi_ready, w_lo_ready = sem("w_hi_ready"), sem("w_lo_ready")
        mm_done = sem("mm_done")
        taken = [sem(f"taken{s}") for s in range(2)]
        x_t, x_taken = sem("x_t"), sem("x_taken")
        sq_mul, sq_acc = sem("sq_mul"), sem("sq_acc")
        ss_done, ln_done, rstd_done = sem("ss_done"), sem("ln_done"), sem("rstd_done")
        ht_ready, hi_ready, lo_ready = sem("ht_ready"), sem("hi_ready"), sem("lo_ready")
        gw_zero, gw_hi, gw_lo = sem("gw_zero"), sem("gw_hi"), sem("gw_lo")
        gate_mm, gate_rows = sem("gate_mm"), sem("gate_rows")
        gate_act, gate_dve = sem("gate_act"), sem("gate_dve")
        cols_t, cols_ready = sem("cols_t"), sem("cols_ready")
        v_ones = sem("v_ones")
        a_hi_done, a_ready = sem("a_hi_done"), sem("a_ready")
        st_ready, cm_ready, exp_done, mask_done, p_ready = (
            sem("st_ready"), sem("cm_ready"), sem("exp_done"), sem("mask_done"), sem("p_ready"))
        pv_ready, den_step, fin_done = sem("pv_ready"), sem("den_step"), sem("fin_done")
        hsq_done, hln_done, hrstd_done, hsn_done, tr_ready = (
            sem("hsq_done"), sem("hln_done"), sem("hrstd_done"), sem("hsn_done"), sem("tr_ready"))
        z_ready, z_taken, z_abs, z_exp, z_ln, lg_ready = (
            sem("z_ready"), sem("z_taken"), sem("z_abs"), sem("z_exp"), sem("z_ln"), sem("lg_ready"))
        scanned, piv_ready, epiv_ready, centred, e_ready, qk_ready = (
            sem("scanned"), sem("piv_ready"), sem("epiv_ready"), sem("centred"), sem("e_ready"), sem("qk_ready"))
        a_mm, a_taken, a_masked = sem("a_mm"), sem("a_taken"), sem("a_masked")
        kt_ready, kt_taken, u_ready, state_step, u_taken, piv_state = (
            sem("kt_ready"), sem("kt_taken"), sem("u_ready"), sem("state_step"), sem("u_taken"), sem("piv_state"))
        o_mm, o_taken = sem("o_mm"), sem("o_taken")
        fin_t = sem("fin_t")
        fin_copied = [sem(f"fin_copied{i}") for i in range(2)]

        halves = [slice(0, HT), slice(HT, T)]
        block = ctx.enter_context(nc.Block())

        @block.sync
        def _(sp):
            def load_x(t):
                src = x_prompt[0, t * P:(t + 1) * P, :] if t < 4 else x_sample[0, (t - 4) * P:(t - 3) * P, :]
                sp.dma_start(xs[:, t, :], src).then_inc(x_loaded[t], 16)

            load_x(0)
            load_x(1)
            load_x(2)
            srcs = [norm_mix_g[0], norm_ffn_g[0], norm_mix_g[1], norm_ffn_g[1], norm_final_g,
                    mlstm_head_g[0], gla_head_g[0]]
            for i, src in enumerate(srcs):
                sp.dma_start(vec_rows[8 * i:8 * i + 8, :], src.rearrange("(c p) -> c p", p=P)).then_inc(vec_loaded, 16)
            sp.dma_start(vec_rows[56:64, :], gla_b_a[0].rearrange("d (h p) -> (d h) p", p=P)).then_inc(vec_loaded, 16)

            def load_w(q, s, src, wait=True):
                if wait:
                    sp.wait_ge(w_lo_ready, 2 * q + s - 1)
                sp.dma_start(raw[s][:, 0:src.shape[1], :], src).then_inc(raw_loaded[s], 16)

            for s in range(2):
                load_w(0, s, w_in[0][:, :, s * W:(s + 1) * W], wait=False)
            sp.dma_start(gate_raw[:, :, 0:16], w_in[0][:, :, 3072:3088]).then_inc(gate_w_loaded, 16)
            load_x(3)
            load_x(4)
            load_x(5)
            sp.wait_ge(consts, 4)
            for at_p, c in ((0, 0), (32, 8), (64, 4), (96, 12)):
                sp.dma_start(gate_bias[at_p:at_p + 4, :],
                             mlstm_b_gate[0, c:c + 4].rearrange("(p a) -> p a", a=1)).then_inc(bias_loaded, 16)
            for d in range(2):
                sp.dma_start(w_a2[32 * d:32 * d + RANK, :], gla_w_a2[0, d]).then_inc(a2_loaded, 16)

            for L in range(2):
                q0 = PAIRS * L
                with sp.Fori(1 - L, 6) as i:
                    for s in range(2):
                        load_w(i + q0, s, w_in[L][:, :, bass.ds(i * (2 * W) + s * W, W)])
                with sp.Fori(0, 2) as i:
                    for s in range(2):
                        load_w(i + q0 + POUT, s, w_out[L][:, :, bass.ds(i * (2 * W) + s * W, W)])
                if L == 0:
                    sp.wait_ge(gw_lo, 2)
                    sp.dma_start(gate_raw[:, :, :], w_in[1][:, :, 3072:3104]).then_inc(gate_w_loaded, 16)
                for b, nb in enumerate(BLOCKS):
                    c0 = sum(BLOCKS[:b])
                    with sp.Fori(0, nb // 2) as i:
                        for s in range(2):
                            load_w(i + q0 + PGU[b], s, w_gu[L][:, :, bass.ds(i * W + (s * DFF + c0 * P), W)])
                    with sp.Fori(0, 2) as i:
                        for s in range(2):
                            load_w(i + q0 + PDN[b], s, w_dn[L][:, c0:c0 + nb, bass.ds(i * (2 * W) + s * W, W)])

            for t in range(TT):
                for hf in range(2):
                    sp.wait_ge(fin_copied[hf], t + 1)
                dst = y_prompt[0, t * P:(t + 1) * P, :] if t < 4 else y_sample[0, (t - 4) * P:(t - 3) * P, :]
                sp.dma_start(dst, y_tok[:, t, :]).then_inc(y_stored, 16)
            sp.wait_ge(y_stored, 16 * TT)

        @block.tensor
        def _(pe):
            def mm(out, lhsT, rhs, start, stop):
                return nc.tensor.matmul(out, lhsT, rhs, start=start, stop=stop)

            def group(out, wh, wl, rh, rl, half, kdim, before=None):
                for k in range(kdim):
                    if before is not None:
                        before(k)
                    r0, r1 = rh(k)[:, halves[half]], rl(k)[:, halves[half]]
                    mm(out, wh(k), r0, k == 0, False)
                    mm(out, wh(k), r1, False, False)
                    last = mm(out, wl(k), r0, False, k == kdim - 1)
                return last

            h_parts = (lambda k: h_hi[:, k, :]), (lambda k: h_lo[:, k, :])
            y_parts_ = (lambda k: y_hi[k]), (lambda k: y_lo[k])
            a_parts = (lambda k: a_hi[:, k, :]), (lambda k: a_lo[:, k, :])

            def tile_begin(q, s):
                pe.wait_ge(w_lo_ready, 2 * q + s + 1)
                pe.wait_ge(taken[s], 4 * q)

            def tile_group(s, g, parts, kdim, before=None):
                half, m = g // 2, g % 2
                cs = slice(m * P, (m + 1) * P)
                last = group(bank[4 * s + g][:, 0:HT], lambda k: w_hi[s][:, k, cs], lambda k: w_lo[s][:, k, cs],
                             *parts, half, kdim, before)
                last.then_inc(mm_done, 1)
                return last

            def tile_seq(q, s, parts, kdim, before=(None,) * 4, hook=None):
                hook = hook or {}
                tile_begin(q, s)
                for g in range(4):
                    last = tile_group(s, g, parts, kdim, before[g])
                    if g in hook:
                        hook[g]()

            def sum_squares(e, half):
                if e == 0:
                    pe.wait_ge(sq_acc, 8 * (half + 1))
                else:
                    pe.wait_ge(sq_acc, 16 * e + 14 + 2 * half)
                mm(bank[3 * half][:, 0:HT], ones[:, :], sq_sum[:, half, :], True, True).then_inc(ss_done, 1)

            def parts_of(e, half):
                def before(k):
                    pe.wait_ge(lo_ready, NORM_S[e] + 8 * half + k + 1)
                return before

            pe.wait_ge(consts, 4)
            pe.wait_ge(vec_loaded, 16 * 8)
            nc.tensor.transpose(bank[7][:, 0:64], vec_rows[:, :], ident[0:64, 0:64]).then_inc(vec_t, 1)

            def x_chunks(half):
                for t in range(3):
                    pe.wait_ge(x_loaded[3 * half + t], 16)
                for c in range(KC):
                    j = 8 * half + c
                    if j == 7:
                        pe.wait_ge(vec_ready, 1)
                    if j >= 8:
                        pe.wait_ge(x_taken, j - 7)
                    for t in range(3):
                        last = nc.tensor.transpose(bank[j % 8][:, t * P:(t + 1) * P],
                                                   xs[:, 3 * half + t, c * P:(c + 1) * P], ident[:, :])
                    last.then_inc(x_t, 1)

            x_chunks(0)
            sum_squares(0, 0)
            pe.wait_ge(ln_done, 1)
            x_chunks(1)

            def mlstm(q0):
                q1 = q0 + POUT
                pe.wait_ge(taken[0], 4 * q1)
                pe.wait_ge(taken[1], 4 * q1)

                def scores(h):
                    if h:
                        pe.wait_ge(p_ready, 12 * h)
                    if h >= 2:
                        pe.wait_ge(ht_ready, Y_S[0] + 4 * (h - 1))
                    for j in range(TT):
                        first, last_t = FIRST_T[j] * P, (LAST_T[j] + 1) * P
                        out = bank[j][:, :] if j < 4 else bank[4][:, (j - 4) * 256:(j - 3) * 256]
                        mm(out, k_of[h][:, j * P:(j + 1) * P], q_of[h][:, first:last_t], True, True
                           ).then_inc(st_ready, 1)

                def maxima(h, piece):
                    n = 3 * h + piece
                    if n:
                        pe.wait_ge(exp_done, 4 * n)
                    for d, cs, at_c in ([(0, slice(0, 512), 0)], [(1, slice(0, 512), 0)],
                                        [(0, slice(512, T), 0), (1, slice(512, T), 256)])[piece]:
                        r = 32 * d + h
                        last = mm(bank[5][:, at_c:at_c + cs.stop - cs.start],
                                  ident[0:36, r:r + 1].to_broadcast([36, P]), rows[0:36, cs], True, True)
                    last.then_inc(cm_ready, 1)

                def output(h, i):
                    d, t = OUTS[i]
                    n = 12 * h + i
                    if n >= 2:
                        pe.wait_ge(fin_done, n - 1)
                    pe.wait_ge(p_ready, 12 * h + (t + 1 if i < 4 else 8 if i < 8 else 12))
                    js = range(FIRST_T[t], t + 1) if d == 0 else range(t, LAST_T[t] + 1)
                    for j in js:
                        at_c = OFF[d, j] + t * P - span(d, j)[0]
                        last = mm(bank[6 + n % 2][:, 0:DV + 1], decay[:, h % 2, d, at_c:at_c + P],
                                  v_all[:, h, j, :], j == js[0], j == js[-1])
                    last.then_inc(pv_ready, 1)

                def turn(h, g, b):
                    half, cc = g // 2, g % 2
                    pe.wait_ge(hsn_done, TT * (h + 1))
                    for t in range(3):
                        last = nc.tensor.transpose(bank[b][:, t * P:(t + 1) * P],
                                                   hs_m[:, h % 2, 3 * half + t, cc * P:(cc + 1) * P], ident[:, :])
                    last.then_inc(tr_ready, 1)

                pe.wait_ge(v_ones, 1)
                scores(0)
                for piece in range(3):
                    maxima(0, piece)
                for h in range(NH):
                    for i in range(12):
                        output(h, i)
                        if h + 1 < NH and i % 4 == 0:
                            maxima(h + 1, i // 4)
                        if h and i in (5, 9):
                            pe.wait_ge(p_ready, 12 * (h + 1))
                            turn(h - 1, (i - 5) // 2, (i - 5) // 2)
                            turn(h - 1, (i - 5) // 2 + 1, (i - 5) // 2 + 1)
                    if h + 1 < NH:
                        scores(h + 1)
                pe.wait_ge(fin_done, 12 * NH)
                for g in range(4):
                    turn(NH - 1, g, 4 + g)
                pe.wait_ge(ht_ready, Y_S[0] + 4 * (NH - 1))

            def gla(q0):
                q1 = q0 + POUT
                pe.wait_ge(taken[0], 4 * q1)
                pe.wait_ge(taken[1], 4 * q1)
                pe.wait_ge(a2_loaded, 32)

                def gate_logits(h, d):
                    for half in range(2):
                        n = 4 * h + 2 * d + half
                        if n >= 2:
                            pe.wait_ge(z_taken, n - 1)
                        if h >= 3:
                            pe.wait_ge(ht_ready, Y_S[1] + 4 * (h - 2))
                        p = slice(32 * d, 32 * d + RANK)
                        mm(bank[half][:, 0:HT], w_a2[p, h * DK:(h + 1) * DK], rows[p, halves[half]], True, True
                           ).then_inc(z_ready, 1)

                def chunk_scores(h, g):
                    n = 3 * h + g
                    if n >= 2:
                        pe.wait_ge(a_taken, n - 1)
                    if h and g == 2 or h >= 2:
                        pe.wait_ge(ht_ready, Y_S[1] + 4 * (h if g == 2 else h - 1))
                    for i in range(2):
                        for d in range(2):
                            ts = slice((2 * g + i) * P, (2 * g + i + 1) * P)
                            last = mm(bank[2 + n % 2][:, (2 * i + d) * P:(2 * i + d + 1) * P],
                                      ke[:, h % 2, d, ts], qe[:, h % 2, d, ts], True, True)
                    last.then_inc(a_mm, 1)

                def keys_by_token(h, d):
                    n = 2 * h + d
                    if n >= 1:
                        pe.wait_ge(kt_taken, n)
                    if h and d == 0:
                        pe.wait_ge(o_taken, 3 * h - 1)
                    for i, t in enumerate(UPD[d]):
                        last = nc.tensor.transpose(bank[4][:, i * P:(i + 1) * P],
                                                   ke[:, h % 2, d, t * P:(t + 1) * P], ident[:, :])
                    last.then_inc(kt_ready, 1)

                def updates(h, d):
                    n = 2 * h + d
                    pe.wait_ge(kt_taken, n + 1)
                    if n:
                        pe.wait_ge(u_taken, 4 * n)
                    for i, t in enumerate(UPD[d]):
                        last = mm(bank[5 + i // 2][:, (i % 2) * DV:(i % 2 + 1) * DV], k_tok[:, d, i, :],
                                  v_all[:, h, t, 0:DV], True, True)
                    last.then_inc(u_ready, 1)

                def outputs(h, g):
                    n = 3 * h + g
                    b = (7, 4, 7)[g]
                    pe.wait_ge(a_masked, 2 * n + 2)
                    if g == 0:
                        pe.wait_ge(piv_state, 8 * (h + 1))
                        if h:
                            pe.wait_ge(o_taken, 3 * h)
                    if g == 1:
                        pe.wait_ge(kt_taken, 2 * h + 2)
                    if g == 2:
                        pe.wait_ge(o_taken, 3 * h + 1)
                    for i in range(2):
                        t = 2 * g + i
                        ts = slice(t * P, (t + 1) * P)
                        ops = [(a_sb[:, n % 2, i, d, :], v_all[:, h, t, 0:DV]) for d in range(2)]
                        if t != FIRST_T[t]:
                            ops.append((qe[:, h % 2, 0, ts], s_piv[:, 0, UPD[0].index(t - 1), :]))
                        if t != LAST_T[t]:
                            ops.append((qe[:, h % 2, 1, ts], s_piv[:, 1, UPD[1].index(t + 1), :]))
                        for k, (a, b_) in enumerate(ops):
                            last = mm(bank[b][:, i * DV:(i + 1) * DV], a, b_, k == 0, k == len(ops) - 1)
                    last.then_inc(o_mm, 1)

                def turn(h, g, b):
                    half, cc = g // 2, g % 2
                    pe.wait_ge(hsn_done, TT * (NH + h + 1))
                    for t in range(3):
                        last = nc.tensor.transpose(bank[b][:, t * P:(t + 1) * P],
                                                   hs_g[h % 2][:, 3 * half + t, cc * P:(cc + 1) * P], ident[:, :])
                    last.then_inc(tr_ready, 1)

                gate_logits(0, 0)
                gate_logits(0, 1)
                for h in range(NH):
                    pe.wait_ge(qk_ready, 4 * (h + 1))
                    chunk_scores(h, 0)
                    chunk_scores(h, 1)
                    if h + 1 < NH:
                        gate_logits(h + 1, 0)
                        gate_logits(h + 1, 1)
                    for d in range(2):
                        keys_by_token(h, d)
                    for d in range(2):
                        updates(h, d)
                    if h:
                        pe.wait_ge(a_taken, 3 * h + 2)
                        pe.wait_ge(z_taken, 4 * min(h + 2, NH))
                        for g in range(4):
                            turn(h - 1, g, (2, 3, 0, 1)[g])
                    outputs(h, 0)
                    chunk_scores(h, 2)
                    outputs(h, 1)
                    outputs(h, 2)
                pe.wait_ge(o_taken, 3 * NH)
                for g in range(4):
                    turn(NH - 1, g, 4 + g)

            for L in range(2):
                q0 = PAIRS * L
                e = 2 * L
                if L == 0:
                    pe.wait_ge(x_taken, 16)
                pe.wait_ge(gw_lo, L + 2)

                def gates(half):
                    group(bank[4 + half][:, 0:HT], lambda k: g_hi[:, k, :], lambda k: g_lo[:, k, :],
                          *h_parts, half, KC, parts_of(e, half)).then_inc(gate_mm, 1)

                gates(0)
                sum_squares(e, 1)
                tile_begin(q0, 0)
                tile_group(0, 0, h_parts, KC)
                tile_group(0, 1, h_parts, KC)
                gates(1)
                tile_group(0, 2, h_parts, KC)
                tile_group(0, 3, h_parts, KC)
                pe.wait_ge(gate_rows, 2 * L + 2)
                tile_seq(q0, 1, h_parts, KC)
                for s in range(2):
                    tile_seq(q0 + PK, s, h_parts, KC)
                with pe.Fori(0, 2) as i:
                    for s in range(2):
                        tile_begin(i + q0 + PV_, s)
                        for t in range(TT):
                            out = bank[4 * s + t // 2][:, (t % 2) * W:(t % 2 + 1) * W]
                            ts = slice(t * P, (t + 1) * P)
                            for k in range(KC):
                                mm(out, h_hi[:, k, ts], w_hi[s][:, k, :], k == 0, False)
                                mm(out, h_lo[:, k, ts], w_hi[s][:, k, :], False, False)
                                last = mm(out, h_hi[:, k, ts], w_lo[s][:, k, :], False, k == KC - 1)
                            if t % 2 == 1:
                                last.then_inc(mm_done, 2 if t == TT - 1 else 1)
                if L == 0:
                    pe.wait_ge(gate_act, 4)
                    for t in range(TT):
                        last = nc.tensor.transpose(bank[3 + 4 * (t // 3)][:, (t % 3) * 100:(t % 3 + 1) * 100],
                                                   g_cols[0:100, t * P:(t + 1) * P], ident[0:100, 0:100])
                    last.then_inc(cols_t, 1)
                    pe.wait_ge(cols_ready, 2)
                with pe.Fori(0, 2) as i:
                    for s in range(2):
                        tile_seq(i + q0 + PO, s, h_parts, KC)
                (mlstm if L == 0 else gla)(q0)

                def y_before(half):
                    def before(k):
                        pe.wait_ge(lo_ready, Y_S[L] + 4 * (k // 2) + 2 * half + k % 2 + 1)
                    return before

                q = q0 + POUT
                tile_seq(q, 0, y_parts_, KC, (y_before(0), None, y_before(1), None))
                pe.wait_ge(ht_ready, Y_S[L] + 4 * NH)
                tile_seq(q, 1, y_parts_, KC)

                def first_sum(q, e):
                    pe.wait_ge(taken[0], 4 * (q + 1))
                    sum_squares(e, 0)

                tile_seq(q + 1, 0, y_parts_, KC)
                tile_seq(q + 1, 1, y_parts_, KC, hook={2: lambda: first_sum(q + 1, e + 1)})

                for b, nb in enumerate(BLOCKS):
                    n_pairs = nb // 2
                    start = 0
                    if b == 0:
                        tile_seq(q0 + PGU[0], 0, h_parts, KC, (parts_of(e + 1, 0), None, parts_of(e + 1, 1), None),
                                 hook={0: lambda: sum_squares(e + 1, 1)})
                        tile_seq(q0 + PGU[0], 1, h_parts, KC)
                        start = 1
                    with pe.Fori(start, n_pairs) as i:
                        for s in range(2):
                            tile_seq(i + q0 + PGU[b], s, h_parts, KC)

                    f0 = 4 * (FFP * L + sum(BLOCKS[:b]) // 2) + 4

                    def a_before(half):
                        def before(k):
                            pe.wait_ge(a_ready, f0 + 4 * (k // 2) + 2 * half + k % 2 + 1)
                        return before

                    q = q0 + PDN[b]
                    if b < 2:
                        with pe.Fori(0, 2) as i:
                            pe.wait_ge(a_ready, f0 + 4 * n_pairs - 3)
                            tile_seq(i + q, 0, a_parts, nb, (a_before(0), None, a_before(1), None))
                            tile_seq(i + q, 1, a_parts, nb)
                    else:
                        tile_seq(q, 0, a_parts, nb, (a_before(0), None, a_before(1), None))
                        tile_seq(q, 1, a_parts, nb)
                        tile_seq(q + 1, 0, a_parts, nb)
                        tile_seq(q + 1, 1, a_parts, nb, hook={2: lambda: first_sum(q + 1, e + 2)})

            sum_squares(4, 1)
            for t in range(TT):
                for hf in range(2):
                    n = 2 * t + hf
                    pe.wait_ge(ht_ready, 96 + 8 * (t // 3) + 4 * hf + 4)
                    if n == 0:
                        pe.wait_ge(taken[1], 8 * PAIRS)
                    if t:
                        pe.wait_ge(fin_copied[hf], t)
                    for c in range(4):
                        last = nc.tensor.transpose(bank[4 + n % 2][:, c * P:(c + 1) * P],
                                                   y_fin[:, 4 * hf + c, t * P:(t + 1) * P], ident[:, :])
                    last.then_inc(fin_t, 1)

        @block.scalar
        def _(act):
            def split(q, s, wait=True):
                act.wait_ge(raw_loaded[s], 16 * (q + 1))
                if wait:
                    act.wait_ge(mm_done, 8 * q + (4 * s - 4))
                nc.scalar.copy(w_hi[s][:, :, :], raw[s][:, :, :]).then_inc(w_hi_ready, 1)

            def high(s, out):
                act.wait_ge(ht_ready, s + 1)
                nc.scalar.copy(out, ht[:, s % 4, :]).then_inc(hi_ready, 1)

            def norm(e):
                for half in range(2):
                    act.wait_ge(ss_done, 2 * e + half + 1)
                    nc.scalar.activation(rstd[:, half, :], bank[3 * half][:, 0:HT], ACT.Ln,
                                         bias=eps_col[:, 0:1], scale=1.0 / D).then_inc(ln_done, 1)
                    act.wait_ge(ln_done, 2 * e + half + 1)
                    nc.scalar.activation(rstd[:, half, :], rstd[:, half, :], ACT.Exp, scale=-0.5).then_inc(rstd_done, 1)
                    for c in range(KC if e < 4 else 0):
                        high(NORM_S[e] + 8 * half + c, h_hi[:, c, halves[half]])

            def y_high(L, h, g):
                high(Y_S[L] + 4 * h + g, y_hi[2 * h + g % 2][:, halves[g // 2]])

            def take(q, s, g):
                act.wait_ge(mm_done, 8 * q + (4 * s + g + 1))
                return bank[4 * s + g][:, 0:HT]

            def head_norm(L, h, hs, order, taken):
                for n, t in enumerate(order):
                    taken(t)
                    nc.scalar.activation(junk[:, :], hs[:, t, :], ACT.Square,
                                         accum_out=head_sq[:, h % 2, t:t + 1]).then_inc(hsq_done, 1)
                    act.wait_ge(hsq_done, TT * (NH * L + h) + n + 1)
                act.wait_ge(hsq_done, TT * (NH * L + h + 1))
                nc.scalar.activation(head_rstd[:, h % 2, :], head_sq[:, h % 2, :], ACT.Ln,
                                     bias=eps_col[:, 0:1], scale=1.0 / DV).then_inc(hln_done, 1)
                act.wait_ge(hln_done, NH * L + h + 1)
                nc.scalar.activation(head_rstd[:, h % 2, :], head_rstd[:, h % 2, :], ACT.Exp,
                                     scale=-0.5).then_inc(hrstd_done, 1)

            def mlstm():
                act.wait_ge(cols_ready, 2)

                def decays(h, piece):
                    n = 3 * h + piece
                    act.wait_ge(cm_ready, n + 1)
                    if h >= 2:
                        act.wait_ge(pv_ready, 12 * (h - 1))
                    for d, j in PIECES[piece]:
                        t0, w = span(d, j)
                        c0 = t0 if piece < 2 else t0 - 512 + 256 * d
                        nc.scalar.activation(decay[:, h % 2, d, OFF[d, j]:OFF[d, j] + w], bank[5][:, c0:c0 + w],
                                             ACT.Exp, bias=cols[:, j, 32 * d + h:32 * d + h + 1],
                                             scale=-1.0).then_inc(exp_done, 1)

                for piece in range(3):
                    decays(0, piece)
                for h in range(NH):
                    if h + 1 < NH:
                        decays(h + 1, 0)
                        decays(h + 1, 1)
                    if h:
                        y_high(0, h - 1, 0)
                        y_high(0, h - 1, 1)
                    if h + 1 < NH:
                        decays(h + 1, 2)
                    if h:
                        y_high(0, h - 1, 2)
                        y_high(0, h - 1, 3)
                    order = (3, 2, 1, 0, 5, 4)
                    if h >= 2:
                        act.wait_ge(hsn_done, TT * (h - 1))
                    head_norm(0, h, hs_m[:, h % 2], order,
                              lambda t: act.wait_ge(fin_done, 12 * h + OUTS.index((1, t)) + 1))
                for g in range(4):
                    y_high(0, NH - 1, g)

            def gla():
                def take_scores(h, g):
                    n = 3 * h + g
                    act.wait_ge(a_mm, n + 1)
                    if n >= 2:
                        act.wait_ge(o_mm, n - 1)
                    nc.scalar.copy(a_sb[:, n % 2], bank[2 + n % 2][:, :]).then_inc(a_taken, 1)

                def take_keys(h, d):
                    n = 2 * h + d
                    act.wait_ge(kt_ready, n + 1)
                    if h:
                        act.wait_ge(u_ready, n - 1)
                    nc.scalar.copy(k_tok[:, d], bank[4][:, :]).then_inc(kt_taken, 1)

                def softplus(h):
                    sl = h % 2
                    for d in range(2):
                        act.wait_ge(z_taken, 4 * h + 2 * d + 2)
                        nc.scalar.activation(qe[:, sl, d, :], ke[:, sl, d, :], ACT.Abs).then_inc(z_abs, 1)
                    for d in range(2):
                        act.wait_ge(z_abs, 2 * h + d + 1)
                        nc.scalar.activation(qe[:, sl, d, :], qe[:, sl, d, :], ACT.Exp, scale=-1.0).then_inc(z_exp, 1)
                    for d in range(2):
                        act.wait_ge(z_exp, 2 * h + d + 1)
                        nc.scalar.activation(qe[:, sl, d, :], qe[:, sl, d, :], ACT.Ln,
                                             bias=ones[:, 0:1]).then_inc(z_ln, 1)

                def exponentials(h):
                    sl = h % 2
                    for d in range(2):
                        act.wait_ge(piv_ready, 6 * h + 3 * d + 3)
                        nc.scalar.activation(epiv[:, d], piv[:, d], ACT.Exp, scale=1.0 / GLA_TAU).then_inc(epiv_ready, 1)
                    for d in range(2):
                        act.wait_ge(centred, 2 * h + d + 1)
                        nc.scalar.activation(qe[:, sl, d, :], bsum[:, d, :], ACT.Exp,
                                             scale=1.0 / GLA_TAU).then_inc(e_ready, 1)
                        nc.scalar.activation(ke[:, sl, d, :], bsum[:, d, :], ACT.Exp,
                                             scale=-1.0 / GLA_TAU).then_inc(e_ready, 1)

                softplus(0)
                exponentials(0)
                for h in range(NH):
                    take_scores(h, 0)
                    take_scores(h, 1)
                    take_keys(h, 0)
                    take_keys(h, 1)
                    if h + 1 < NH:
                        softplus(h + 1)
                    if h:
                        for g in range(4):
                            y_high(1, h - 1, g)
                    take_scores(h, 2)
                    if h + 1 < NH:
                        act.wait_ge(u_taken, 8 * (h + 1))
                        act.wait_ge(piv_state, 8 * (h + 1))
                        exponentials(h + 1)
                    if h >= 2:
                        act.wait_ge(hsn_done, TT * (NH + h - 1))
                    head_norm(1, h, hs_g[h % 2], range(TT), lambda t: act.wait_ge(o_taken, 3 * h + t // 2 + 1))
                for g in range(4):
                    y_high(1, NH - 1, g)

            act.wait_ge(consts, 4)
            split(0, 0, wait=False)
            act.wait_ge(gate_w_loaded, 16)
            act.wait_ge(gw_zero, 1)
            for a in range(2):
                src = gate_raw[:, :, 8 * a:8 * a + 8].rearrange("p k (b r) -> p k b r", b=2)
                dst = g_hi[:, :, :].rearrange("p k (b a r) -> p k b a r", b=2, a=2)[:, :, :, a, 0:4]
                nc.scalar.copy(dst, src).then_inc(gw_hi, 1)
            norm(0)
            for L in range(2):
                q0 = PAIRS * L
                for kind in range(2):
                    q = q0 + kind
                    for s in range(2):
                        if s == 0:
                            split(q, 1, wait=q > 0)
                        else:
                            split(q + 1, 0)
                        for g in range(4):
                            h = 2 * s + g % 2
                            src = take(q, s, g)
                            dst = (k_of if kind else q_of)[h][:, halves[g // 2]]
                            ins = nc.scalar.mul(dst, src, 1.0 if kind else float(DK) ** -0.5)
                            ins.then_inc(taken[s], 1)
                if L == 0:
                    act.wait_ge(gate_rows, 2)
                    nc.scalar.activation(g_soft[64:100, :], g_pre[64:100, :], ACT.Abs).then_inc(gate_act, 1)
                    act.wait_ge(gate_act, 1)
                    nc.scalar.activation(g_soft[64:100, :], g_soft[64:100, :], ACT.Exp, scale=-1.0).then_inc(gate_act, 1)
                    act.wait_ge(gate_act, 2)
                    nc.scalar.activation(g_soft[64:100, :], g_soft[64:100, :], ACT.Ln,
                                         bias=ones[64:100, 0:1]).then_inc(gate_act, 1)
                    act.wait_ge(gate_dve, 11)
                    nc.scalar.activation(g_cols[64:100, :], g_log[0:36, :], ACT.Exp, scale=-1.0).then_inc(gate_act, 1)
                with act.Fori(0, 2) as i:
                    for s in range(2):
                        q = i + q0 + PV_
                        if s == 0:
                            split(q, 1)
                        else:
                            split(q + 1, 0)
                        for g in range(3):
                            act.wait_ge(mm_done, 8 * q + (4 * s + g + 1 + (g == 2)))
                            dst = v_all[:, bass.ds(i * 2 + s, 1), 2 * g:2 * g + 2, 0:DV]
                            src = bank[4 * s + g][:, :].rearrange("p (a t n) -> p a t n", a=1, t=2)
                            nc.scalar.copy(dst, src).then_inc(taken[s], 2 if g == 2 else 1)
                if L == 0:
                    act.wait_ge(cols_ready, 2)
                with act.Fori(0, 2) as i:
                    for s in range(2):
                        q = i + q0 + PO
                        if s == 0:
                            split(q, 1)
                        else:
                            split(q + 1, 0)
                        for g in range(4):
                            src = take(q, s, g)
                            dst = o_gate[:, bass.ds(i * 4 + (2 * s + g % 2), 1), halves[g // 2]]
                            nc.scalar.activation(dst, src, ACT.Silu if L else ACT.Sigmoid).then_inc(taken[s], 1)
                (gla if L else mlstm)()
                for i in range(2):
                    split(q0 + POUT + i, 1)
                    split(q0 + POUT + i + 1, 0)
                norm(2 * L + 1)
                for b, nb in enumerate(BLOCKS):
                    with act.Fori(0, nb // 2) as i:
                        q = i + q0 + PGU[b]
                        split(q, 1)
                        for g in range(4):
                            act.wait_ge(taken[1], 4 * q + (g - 3))
                            src = take(q, 0, g)
                            nc.scalar.activation(sg[:, g, :], src, ACT.Silu).then_inc(taken[0], 1)
                        split(q + 1, 0)
                    if L == 0 and b == 0:
                        act.wait_ge(gate_w_loaded, 32)
                        act.wait_ge(gw_zero, 2)
                        src = gate_raw[:, :, :].rearrange("p k (b r) -> p k b r", b=2)
                        dst = g_hi[:, :, :].rearrange("p k (b r) -> p k b r", b=4)[:, :, 0:2, 0:RANK]
                        nc.scalar.copy(dst, src).then_inc(gw_hi, 1)
                    if b < 2:
                        with act.Fori(0, 2) as i:
                            split(i + q0 + PDN[b], 1)
                            split(i + q0 + PDN[b] + 1, 0)
                    else:
                        for i in range(2):
                            split(q0 + PDN[b] + i, 1)
                            if L == 0 or i == 0:
                                split(q0 + PDN[b] + i + 1, 0)
                norm(2 * L + 2)
            for t in range(TT):
                act.wait_ge(fin_t, 2 * t + 1)
                nc.scalar.copy(y_tok[:, t, 0:512], bank[4][:, :]).then_inc(fin_copied[0], 1)

        @block.vector
        def _(dve):
            V = nc.vector

            def split(q, s):
                dve.wait_ge(w_hi_ready, 2 * q + s + 1)
                V.tensor_tensor(w_lo[s][:, :, :], raw[s][:, :, :], w_hi[s][:, :, :].bitcast(F32),
                                ALU.subtract).then_inc(w_lo_ready, 1)

            def ring(s):
                if s >= 4:
                    dve.wait_ge(lo_ready, s - 3)

            def norm_half(e, half):
                dve.wait_ge(rstd_done, 2 * e + half + 1)
                for c in range(KC):
                    if e < 4:
                        s = NORM_S[e] + 8 * half + c
                        ring(s)
                        out = ht[:, s % 4, :]
                    else:
                        out = y_fin[:, c, halves[half]]
                    V.scalar_tensor_tensor(out=out, in0=xT[:, c, halves[half]], scalar=gain[e][:, c:c + 1],
                                           in1=rstd[:, half, :], op0=ALU.mult, op1=ALU.mult).then_inc(ht_ready, 1)

            def add_residual(q, s, g, c):
                dve.wait_ge(mm_done, 8 * q + (4 * s + g + 1))
                dve.wait_ge(taken[s], 4 * q + g)
                hs = halves[g // 2]
                if isinstance(c, int):
                    x, src = xT[:, c, hs], bank[4 * s + g][:, 0:HT]
                else:
                    x = xT[:, bass.ds(c, 1), hs]
                    src = bank[4 * s + g][:, 0:HT].rearrange("p (a n) -> p a n", a=1)
                V.tensor_tensor(x, x, src, ALU.add).then_inc(taken[s], 1)

            def y_take(L, h, g, b):
                s = Y_S[L] + 4 * h + g
                c = 2 * h + g % 2
                dve.wait_ge(tr_ready, 16 * L + 4 * h + g + 1)
                ring(s)
                V.scalar_tensor_tensor(out=ht[:, s % 4, :], in0=bank[b][:, 0:HT], scalar=head_g[L][:, c:c + 1],
                                       in1=o_gate[:, c, halves[g // 2]], op0=ALU.mult,
                                       op1=ALU.mult).then_inc(ht_ready, 1)

            def mlstm():
                row = (lambda d, h: 32 * d + h)

                def weights(h, k, piece):
                    n = 12 * h + 4 * piece + k
                    d, j = PIECES[piece][k]
                    t0, w = span(d, j)
                    dve.wait_ge(mask_done, n + 1)
                    dve.wait_ge(st_ready, TT * h + (4 if piece < 2 else 6))
                    first = FIRST_T[j] * P
                    src = bank[j][:, t0 - first:t0 - first + w] if j < 4 else \
                        bank[4][:, (j - 4) * 256 + t0 - first:(j - 4) * 256 + t0 - first + w]
                    at_d = decay[:, h % 2, d, OFF[d, j]:OFF[d, j] + w]
                    V.tensor_tensor(at_d, at_d, src, ALU.mult).then_inc(p_ready, 1)

                def finish(h, i):
                    d, t = OUTS[i]
                    n = 12 * h + i
                    b = bank[6 + n % 2]
                    dve.wait_ge(pv_ready, n + 1)
                    if n:
                        dve.wait_ge(fin_done, n)
                    r = 64 + row(d, h)
                    V.tensor_scalar(den[:, 0:1], b[:, DV:DV + 1], -1.0, cols[:, t, r:r + 1], ALU.mult, ALU.max
                                    ).then_inc(den_step, 1)
                    dve.wait_ge(den_step, 3 * n + 1)
                    V.tensor_scalar(den[:, 0:1], b[:, DV:DV + 1], den[:, 0:1], None, ALU.max).then_inc(den_step, 1)
                    dve.wait_ge(den_step, 3 * n + 2)
                    V.reciprocal(den[:, 1:2], den[:, 0:1]).then_inc(den_step, 1)
                    dve.wait_ge(den_step, 3 * n + 3)
                    out = hs_m[:, h % 2, t, :]
                    if d == 0:
                        V.tensor_scalar(out, b[:, 0:DV], den[:, 1:2], None, ALU.mult).then_inc(fin_done, 1)
                    else:
                        V.scalar_tensor_tensor(out=out, in0=b[:, 0:DV], scalar=den[:, 1:2], in1=out,
                                               op0=ALU.mult, op1=ALU.add).then_inc(fin_done, 1)

                for h in range(NH):
                    for piece in range(3):
                        for k in range(4):
                            weights(h, k, piece)
                    for i in range(12):
                        finish(h, i)
                        if h and i in (5, 9):
                            for g in range((i - 5) // 2, (i - 5) // 2 + 2):
                                y_take(0, h - 1, g, g)
                for g in range(4):
                    y_take(0, NH - 1, g, 4 + g)

            def gla():
                b_t = [bsum[:, d, :].rearrange("p (c t) -> p c t", t=P) for d in range(2)]

                def logits(h):
                    for d in range(2):
                        for half in range(2):
                            n = 4 * h + 2 * d + half
                            dve.wait_ge(z_ready, n + 1)
                            if h >= 2:
                                dve.wait_ge(o_mm, 3 * (h - 1))
                            V.tensor_scalar(ke[:, h % 2, d, halves[half]], bank[half][:, 0:HT],
                                            b_a[:, 4 * d + h:4 * d + h + 1], None, ALU.add).then_inc(z_taken, 1)

                def log_gates(h, d):
                    sl = h % 2
                    dve.wait_ge(z_ln, 2 * h + d + 1)
                    V.scalar_tensor_tensor(out=qe[:, sl, d, :], in0=ke[:, sl, d, :], scalar=0.0, in1=qe[:, sl, d, :],
                                           op0=ALU.min, op1=ALU.subtract).then_inc(lg_ready, 1)
                    dve.wait_ge(lg_ready, 2 * h + d + 1)
                    if h:
                        dve.wait_ge(e_ready, 4 * h)
                    for t in range(TT):
                        lo = t * P
                        if d == 0:
                            ts = slice(lo, lo + P)
                        else:
                            ts = slice(lo + P - 1, lo - 1 if t else None, -1)
                        V.tensor_tensor_scan(bsum[:, d, ts], ones[:, :], qe[:, sl, d, ts], 0.0,
                                             ALU.mult, ALU.add).then_inc(scanned, 1)

                def pivots(h, d):
                    dve.wait_ge(scanned, TT * (2 * h + d + 1))
                    if h:
                        dve.wait_ge(epiv_ready, 2 * h)
                    end = P - 1 if d == 0 else 0
                    n = 6 * h + 3 * d
                    V.tensor_copy(piv[:, d, 0, :], b_t[d][:, :, PIVOT]).then_inc(piv_ready, 1)
                    V.tensor_copy(piv[:, d, 1, :], b_t[d][:, :, end]).then_inc(piv_ready, 1)
                    dve.wait_ge(piv_ready, n + 2)
                    V.tensor_tensor(piv[:, d, 2, :], piv[:, d, 1, :], piv[:, d, 0, :], ALU.subtract
                                    ).then_inc(piv_ready, 1)
                    c = piv[:, d, 0, :].rearrange("p (c a) -> p c a", a=1).to_broadcast([P, TT, P])
                    V.tensor_tensor(b_t[d], b_t[d], c, ALU.subtract).then_inc(centred, 1)

                def states(h, d):
                    dve.wait_ge(u_ready, 2 * h + d + 1)
                    dve.wait_ge(epiv_ready, 2 * h + 2)
                    st = state[:, d, :]
                    for i, t in enumerate(UPD[d]):
                        n = 4 * (2 * h + d) + i
                        u = bank[5 + i // 2][:, (i % 2) * DV:(i % 2 + 1) * DV]
                        if n:
                            dve.wait_ge(u_taken, n)
                            dve.wait_ge(piv_state, n)
                        if i in (0, 3):
                            V.tensor_scalar(st, u, epiv[:, d, 2, t:t + 1], None, ALU.mult).then_inc(u_taken, 1)
                        else:
                            V.tensor_scalar(st, st, epiv[:, d, 1, t:t + 1], None, ALU.mult).then_inc(state_step, 1)
                            dve.wait_ge(state_step, 2 * (2 * h + d) + i)
                            V.scalar_tensor_tensor(out=st, in0=u, scalar=epiv[:, d, 2, t:t + 1], in1=st,
                                                   op0=ALU.mult, op1=ALU.add).then_inc(u_taken, 1)

                def take_outputs(h, g):
                    n = 3 * h + g
                    dve.wait_ge(o_mm, n + 1)
                    if h >= 2:
                        dve.wait_ge(tr_ready, 16 + 4 * (h - 1))
                    src = bank[(7, 4, 7)[g]][:, :].rearrange("p (t n) -> p t n", t=2)
                    V.tensor_copy(hs_g[h % 2][:, 2 * g:2 * g + 2, :], src).then_inc(o_taken, 1)

                logits(0)
                for d in range(2):
                    log_gates(0, d)
                for d in range(2):
                    pivots(0, d)
                for h in range(NH):
                    if h + 1 < NH:
                        logits(h + 1)
                    for d in range(2):
                        states(h, d)
                    if h:
                        for g in range(4):
                            y_take(1, h - 1, g, (2, 3, 0, 1)[g])
                    if h + 1 < NH:
                        log_gates(h + 1, 0)
                    take_outputs(h, 0)
                    if h + 1 < NH:
                        log_gates(h + 1, 1)
                        for d in range(2):
                            pivots(h + 1, d)
                    take_outputs(h, 1)
                    take_outputs(h, 2)
                for g in range(4):
                    y_take(1, NH - 1, g, 4 + g)

            V.memset(ones[:, :], 1.0).then_inc(consts, 1)
            V.memset(eps_col[:, :], EPS).then_inc(consts, 1)
            dve.wait_ge(vec_t, 1)
            V.tensor_copy(vec[:, :], bank[7][:, 0:64]).then_inc(vec_ready, 1)
            dve.wait_ge(vec_ready, 1)
            for half in range(2):
                for c in range(KC):
                    j = 8 * half + c
                    dve.wait_ge(x_t, j + 1)
                    V.tensor_copy(xT[:, c, halves[half]], bank[j % 8][:, 0:HT]).then_inc(x_taken, 1)
                if half == 0:
                    split(0, 0)
                    for a in range(2):
                        dve.wait_ge(gw_hi, a + 1)
                        src = gate_raw[:, :, 8 * a:8 * a + 8].rearrange("p k (b r) -> p k b r", b=2)
                        hi = g_hi[:, :, :].rearrange("p k (b a r) -> p k b a r", b=2, a=2)[:, :, :, a, 0:4]
                        lo = g_lo[:, :, :].rearrange("p k (b a r) -> p k b a r", b=2, a=2)[:, :, :, a, 0:4]
                        V.tensor_tensor(lo, src, hi.bitcast(F32), ALU.subtract).then_inc(gw_lo, 1)
                    norm_half(0, 0)
            norm_half(0, 1)
            for L in range(2):
                q0 = PAIRS * L
                split(q0, 1)
                for half in range(2):
                    dve.wait_ge(gate_mm, 2 * L + half + 1)
                    if L == 0:
                        dve.wait_ge(bias_loaded, 64)
                        V.tensor_scalar(g_pre[0:100, halves[half]], bank[4 + half][0:100, 0:HT],
                                        gate_bias[0:100, 0:1], None, ALU.add).then_inc(gate_rows, 1)
                    else:
                        V.tensor_copy(rows[0:48, halves[half]], bank[4 + half][0:48, 0:HT]).then_inc(gate_rows, 1)
                split(q0 + 1, 0)
                split(q0 + 1, 1)
                split(q0 + 2, 0)
                if L == 0:
                    n = 0

                    def step(ins):
                        ins.then_inc(gate_dve, 1)

                    one = ones[0:36, 0:1]
                    dve.wait_ge(gate_act, 3)
                    step(V.scalar_tensor_tensor(out=g_log[0:36, :], in0=g_pre[64:100, :], scalar=0.0,
                                                in1=g_soft[64:100, :], op0=ALU.min, op1=ALU.subtract))
                    dve.wait_ge(gate_dve, 1)
                    for p in (slice(0, 36), slice(32, 36)):
                        for n_s, (a, b) in enumerate(((0, SEQS[0]), (SEQS[0], T))):
                            ts = slice(a, b) if p.start == 0 else slice(b - 1, a - 1 if a else None, -1)
                            step(V.tensor_tensor_scan(g_cum[p, ts], ones[p, 0:1].to_broadcast([p.stop - p.start, b - a]),
                                                      g_log[p, ts], 0.0, ALU.mult, ALU.add))
                        dve.wait_ge(gate_dve, 3 if p.start == 0 else 5)
                    dve.wait_ge(gw_zero, 1)
                    step(V.tensor_tensor(g_cols[0:36, :], g_pre[0:36, :], g_cum[0:36, :], ALU.subtract))
                    dve.wait_ge(gate_dve, 6)
                    for p in (slice(0, 36), slice(32, 36)):
                        for a, b in ((0, SEQS[0]), (SEQS[0], T)):
                            ts = slice(a, b) if p.start == 0 else slice(b - 1, a - 1 if a else None, -1)
                            step(V.tensor_tensor_scan(rows[p, ts], ones[p, 0:1].to_broadcast([p.stop - p.start, b - a]),
                                                      g_cols[p, ts], M_INIT, ALU.mult, ALU.max))
                        dve.wait_ge(gate_dve, 8 if p.start == 0 else 10)
                    step(V.tensor_tensor(g_log[0:36, :], g_cum[0:36, :], rows[0:36, :], ALU.add))
                    V.memset(v_all[:, :, :, DV:DV + 1], 1.0).then_inc(v_ones, 1)
                with dve.Fori(0, 2) as i:
                    split(i + q0 + PV_, 1)
                    split(i + q0 + PV_ + 1, 0)
                if L == 0:
                    dve.wait_ge(cols_t, 1)
                    for k in range(2):
                        V.tensor_copy(cols[:, 3 * k:3 * k + 3, :],
                                      bank[3 + 4 * k][:, 0:300].rearrange("p (t r) -> p t r", t=3)).then_inc(cols_ready, 1)
                with dve.Fori(0, 2) as i:
                    split(i + q0 + PO, 1)
                    split(i + q0 + PO + 1, 0)
                (gla if L else mlstm)()

                def last_pair(q, c, e, more):
                    split(q, 1)
                    for g in range(4):
                        add_residual(q, 0, g, c + g % 2)
                    if more:
                        split(q + 1, 0)
                    for g in range(3):
                        add_residual(q, 1, g, c + 2 + g % 2)
                    norm_half(e, 0)
                    add_residual(q, 1, 3, c + 3)
                    norm_half(e, 1)

                def pair(q, c):
                    split(q, 1)
                    for g in range(4):
                        add_residual(q, 0, g, c + g % 2)
                    split(q + 1, 0)
                    for g in range(4):
                        add_residual(q, 1, g, c + (2 + g % 2))

                pair(q0 + POUT, 0)
                last_pair(q0 + POUT + 1, 4, 2 * L + 1, True)
                for b, nb in enumerate(BLOCKS):
                    with dve.Fori(0, nb // 2) as i:
                        q = i + q0 + PGU[b]
                        f = i + (FFP * L + sum(BLOCKS[:b]) // 2)
                        split(q, 1)
                        split(q + 1, 0)
                        for g in range(4):
                            dve.wait_ge(mm_done, 8 * q + (4 + g + 1))
                            dve.wait_ge(taken[0], 4 * q + (g + 1))
                            dve.wait_ge(a_ready, 4 * f + (g + 1))
                            V.tensor_tensor(at[:, g, :], sg[:, g, :], bank[4 + g][:, 0:HT], ALU.mult
                                            ).then_inc(taken[1], 1)
                    if L == 0 and b == 0:
                        dve.wait_ge(gw_hi, 3)
                        src = gate_raw[:, :, :].rearrange("p k (b r) -> p k b r", b=2)
                        hi = g_hi[:, :, :].rearrange("p k (b r) -> p k b r", b=4)[:, :, 0:2, 0:RANK]
                        lo = g_lo[:, :, :].rearrange("p k (b r) -> p k b r", b=4)[:, :, 0:2, 0:RANK]
                        V.tensor_tensor(lo, src, hi.bitcast(F32), ALU.subtract).then_inc(gw_lo, 1)
                    if b < 2:
                        with dve.Fori(0, 2) as i:
                            pair(i + q0 + PDN[b], i * 4)
                    else:
                        pair(q0 + PDN[b], 0)
                        last_pair(q0 + PDN[b] + 1, 4, 2 * L + 2, L == 0)
            for t in range(TT):
                dve.wait_ge(fin_t, 2 * t + 2)
                V.tensor_copy(y_tok[:, t, 512:D], bank[5][:, :]).then_inc(fin_copied[1], 1)

        @block.gpsimd
        def _(pool):
            G = nc.gpsimd

            sq_steps = [1]

            def square(src, first, half, n):
                if first:
                    G.tensor_tensor(sq_sum[:, half, :], src, src, ALU.mult).then_inc(sq_acc, 1)
                    return
                pool.wait_ge(sq_acc, n)
                G.tensor_tensor(sq_new[:, :], src, src, ALU.mult).then_inc(sq_mul, 1)
                sq_steps[0] += 1
                pool.wait_ge(sq_mul, sq_steps[0])
                G.tensor_tensor(sq_sum[:, half, :], sq_sum[:, half, :], sq_new[:, :], ALU.add).then_inc(sq_acc, 1)

            def low(s, out, hi):
                pool.wait_ge(hi_ready, s + 1)
                G.tensor_tensor(out, ht[:, s % 4, :], hi.bitcast(F32), ALU.subtract).then_inc(lo_ready, 1)

            def norm_low(e, half):
                for c in range(KC if e < 4 else 0):
                    low(NORM_S[e] + 8 * half + c, h_lo[:, c, halves[half]], h_hi[:, c, halves[half]])

            def y_low(L, h, g):
                c, hs = 2 * h + g % 2, halves[g // 2]
                low(Y_S[L] + 4 * h + g, y_lo[c][:, hs], y_hi[c][:, hs])

            def squares(q, e):
                for n in range(16):
                    i, s, g = n // 8, n // 4 % 2, n % 4
                    c = 4 * i + 2 * s + g % 2
                    if n == 15:
                        norm_low(e, 0)
                    if c == 0:
                        pool.wait_ge(ss_done, 2 * (e - 1) + g // 2 + 1)
                    pool.wait_ge(taken[s], 4 * (q + i) + g + 1)
                    square(xT[:, c, halves[g // 2]], c == 0, g // 2, 16 * e + n)
                norm_low(e, 1)

            def head_scale(L, h, hs, order):
                pool.wait_ge(hrstd_done, NH * L + h + 1)
                for t in order:
                    G.tensor_scalar(hs[:, t, :], hs[:, t, :], head_rstd[:, h % 2, t:t + 1], None, ALU.mult
                                    ).then_inc(hsn_done, 1)

            def causal(ap, d, tiles, done):
                sign = 1 if d == 0 else -1
                pat = [[sign, P]] if tiles == 1 else [[0, tiles], [sign, P]]
                G.affine_select(out=ap, in_=ap, pattern=pat, compare_op=ALU.is_ge, fill=0.0, base=0,
                                channel_multiplier=-sign).then_inc(done, 1)

            def mlstm():
                def masks(h, piece):
                    for k, (d, j) in enumerate(PIECES[piece]):
                        pool.wait_ge(exp_done, 12 * h + 4 * piece + k + 1)
                        c = OFF[d, j] + (0 if d == 0 else span(d, j)[1] - P)
                        causal(decay[:, h % 2, d, c:c + P], d, 1, mask_done)

                for piece in range(3):
                    masks(0, piece)
                for h in range(NH):
                    if h + 1 < NH:
                        masks(h + 1, 0)
                        masks(h + 1, 1)
                    if h:
                        y_low(0, h - 1, 0)
                        y_low(0, h - 1, 1)
                    if h + 1 < NH:
                        masks(h + 1, 2)
                    if h:
                        y_low(0, h - 1, 2)
                        y_low(0, h - 1, 3)
                    head_scale(0, h, hs_m[:, h % 2], range(TT))
                for g in range(4):
                    y_low(0, NH - 1, g)

            def gla():
                def scale_qk(h):
                    for d in range(2):
                        for i, (part, of) in enumerate(((qe, q_of), (ke, k_of))):
                            pool.wait_ge(e_ready, 4 * h + 2 * d + i + 1)
                            p = part[:, h % 2, d, :]
                            G.tensor_tensor(p, p, of[h], ALU.mult).then_inc(qk_ready, 1)

                def masks(h, g):
                    n = 3 * h + g
                    pool.wait_ge(a_taken, n + 1)
                    for d in range(2):
                        causal(a_sb[:, n % 2, :, d, :], d, 2, a_masked)

                def pivot_states(h):
                    if h:
                        pool.wait_ge(o_mm, 3 * h)
                    for d in range(2):
                        for i in range(4):
                            pool.wait_ge(u_taken, 4 * (2 * h + d) + i + 1)
                            nxt = UPD[d][i] + (1 if d == 0 else -1)
                            G.tensor_scalar(s_piv[:, d, i, :], state[:, d, :], epiv[:, d, 0, nxt:nxt + 1], None,
                                            ALU.mult).then_inc(piv_state, 1)

                scale_qk(0)
                for h in range(NH):
                    masks(h, 0)
                    masks(h, 1)
                    pivot_states(h)
                    if h:
                        for g in range(4):
                            y_low(1, h - 1, g)
                    masks(h, 2)
                    if h + 1 < NH:
                        scale_qk(h + 1)
                    head_scale(1, h, hs_g[h % 2], range(TT))
                for g in range(4):
                    y_low(1, NH - 1, g)

            G.memset(ident[:, :], 0.0).then_inc(sq_mul, 1)
            pool.wait_ge(sq_mul, 1)
            G.affine_select(out=ident[:, :], in_=ident[:, :], compare_op=ALU.not_equal, fill=1.0, base=0,
                            pattern=[[-1, P]], channel_multiplier=1).then_inc(consts, 1)
            G.memset(gate_bias[:, :], 0.0).then_inc(consts, 1)
            G.memset(den[:, :], 0.0).then_inc(a_ready, 4)
            G.memset(g_cols[:, :], 0.0)
            G.memset(g_hi[:, :, :].bitcast(mybir.dt.uint32), 0)
            G.memset(g_lo[:, :, :].bitcast(mybir.dt.uint32), 0).then_inc(gw_zero, 1)
            for half in range(2):
                for c in range(KC):
                    n = 8 * half + c
                    pool.wait_ge(x_taken, n + 1)
                    square(xT[:, c, halves[half]], c == 0, half, n)
                norm_low(0, half)
            for L in range(2):
                q0 = PAIRS * L
                (gla if L else mlstm)()
                squares(q0 + POUT, 2 * L + 1)
                for b, nb in enumerate(BLOCKS):
                    with pool.Fori(0, nb // 2) as i:
                        q = i + q0 + PGU[b]
                        f = i + (FFP * L + sum(BLOCKS[:b]) // 2)
                        for g in range(4):
                            c = bass.ds(i * 2 + g % 2, 1)
                            hs = halves[g // 2]
                            src = at[:, g:g + 1, :]
                            pool.wait_ge(taken[1], 4 * q + (g + 1))
                            G.tensor_copy(a_hi[:, c, hs], src).then_inc(a_hi_done, 1)
                            pool.wait_ge(a_hi_done, 4 * f + (g + 1))
                            G.tensor_tensor(a_lo[:, c, hs], src, a_hi[:, c, hs].bitcast(F32),
                                            ALU.subtract).then_inc(a_ready, 1)
                    if L == 0 and b == 0:
                        G.memset(g_hi[:, :, :].bitcast(mybir.dt.uint32), 0)
                        G.memset(g_lo[:, :, :].bitcast(mybir.dt.uint32), 0).then_inc(gw_zero, 1)
                squares(q0 + PDN[2], 2 * L + 2)


_INS = ["x_prompt", "x_sample", "norm_mix_g", "norm_ffn_g", "norm_final_g", "mlstm_w_in", "mlstm_b_gate",
        "mlstm_head_g", "mlstm_w_out", "gla_w_in", "gla_w_a2", "gla_b_a", "gla_head_g", "gla_w_out",
        "ffn_w_gu", "ffn_w_down"]
_OUTS = [(1, SEQS[0], D), (1, SEQS[1], D)]


def kernel(**inputs):
    import numpy as _np
    import concourse.bacc as _bacc
    from concourse.bass_utils import run_bass_kernel_spmd as _run

    nc = _bacc.Bacc("TRN2", target_bir_lowering=False, num_devices=1, dynamic_dma_scratch_size=1024)
    arrays, args = {}, []
    for name in _INS:
        a = _np.ascontiguousarray(inputs[name])
        arrays[f"in_{name}_dram"] = a
        args.append(nc.dram_tensor(f"in_{name}_dram", a.shape, mybir.dt.from_np(a.dtype), kind="ExternalInput").ap())
    for i, shape in enumerate(_OUTS):
        args.append(nc.dram_tensor(f"out_{i}_dram", shape, F32, kind="ExternalOutput").ap())
    build(nc, *args)
    r = _run(nc, [arrays], core_ids=[0])
    return tuple(r.results[0][f"out_{i}_dram"] for i in range(len(_OUTS)))
```

```python
from contextlib import ExitStack

import concourse.bass as bass
from concourse import mybir

F32 = mybir.dt.float32
F32R = mybir.dt.float32r
ALU = mybir.AluOpType
ACT = mybir.ActivationFunctionType

P = 128
SEQS = (512, 256)
T = sum(SEQS)
HT = T // 2
TT = T // P
D = 1024
KC = D // P
NH = 4
DK = 128
DV = 256
QK = NH * DK
DFF = 2816
W = 256
EPS = 1e-6
M_INIT = -1e30
GLA_TAU = 16.0
RANK = 16
PIVOT = P // 2 - 1
BLOCKS = (8, 8, 6)
PAIRS = 25
PQ, PK, PV_, PO, POUT = 0, 1, 2, 4, 6
PGU, PDN = (8, 14, 20), (12, 18, 23)
FFP = sum(BLOCKS) // 2
NORM_S = (0, 32, 48, 80)
Y_S = (16, 64)
FIRST_T = (0, 0, 0, 0, 4, 4)
LAST_T = (3, 3, 3, 3, 5, 5)
OUTS = [(0, 0), (0, 1), (0, 2), (0, 3), (1, 3), (1, 2), (1, 1), (1, 0), (0, 4), (0, 5), (1, 5), (1, 4)]
TURN_AT, SCORES_AT = (4, 6), 7
OUT_BANKS = [b if b == 4 or h % 2 == 0 else 13 - b
             for h in range(NH) for b in (6, 7, 4, 6, 7, 4, 6, 7, 4, 6, 7, 6)]
PIECES = [[(0, j) for j in range(4)], [(1, j) for j in range(4)], [(0, 4), (0, 5), (1, 4), (1, 5)]]
UPD = ((0, 1, 2, 4), (3, 2, 1, 5))
TURN = (3, 2, 4, 7)


def span(d, j):
    if d == 0:
        return j * P, (LAST_T[j] + 1 - j) * P
    return FIRST_T[j] * P, (j + 1 - FIRST_T[j]) * P


def offsets():
    out, at = {}, [0, 0]
    for d in range(2):
        for j in range(TT):
            out[d, j] = at[d]
            at[d] += span(d, j)[1]
    assert at[0] == at[1]
    return out, at[0]


OFF, PW = offsets()


def build(nc, x_prompt, x_sample, norm_mix_g, norm_ffn_g, norm_final_g,
          mlstm_w_in, mlstm_b_gate, mlstm_head_g, mlstm_w_out,
          gla_w_in, gla_w_a2, gla_b_a, gla_head_g, gla_w_out,
          ffn_w_gu, ffn_w_down, y_prompt, y_sample):
    w_in = [w[0].rearrange("(k p) n -> p k n", p=P) for w in (mlstm_w_in, gla_w_in)]
    w_out = [w[0].rearrange("(k p) n -> p k n", p=P) for w in (mlstm_w_out, gla_w_out)]
    w_gu = [ffn_w_gu[i].rearrange("(k p) n -> p k n", p=P) for i in range(2)]
    w_dn = [ffn_w_down[i].rearrange("(k p) n -> p k n", p=P) for i in range(2)]

    with ExitStack() as ctx:
        def sb(name, shape, dt=F32, to=ctx):
            return to.enter_context(nc.sbuf_tensor(name, shape, dt))

        def sem(name):
            return ctx.enter_context(nc.semaphore(name))

        xT = sb("xT", [P, KC, T])
        raw = [sb(f"raw{s}", [P, KC, W]) for s in range(2)]
        w_hi = [sb(f"w_hi{s}", [P, KC, W], F32R) for s in range(2)]
        w_lo = [sb(f"w_lo{s}", [P, KC, W], F32R) for s in range(2)]
        ht = sb("ht", [P, 4, HT])
        with ExitStack() as r:
            hs_g1 = sb("hs_g1", [P, TT, DV], F32, r)
            junk = sb("junk", [P, DV], F32, r)
        with ExitStack() as r:
            b0_sum = sb("b0_sum", [P, 2, T], F32, r)
        rstd = sb("rstd", [P, 2, HT])
        sq_sum = sb("sq_sum", [P, 2, HT])
        sq_new = sb("sq_new", [P, HT])
        with ExitStack() as r:
            rows_g = sb("rows_g", [96, T], F32R, r)
        rows_m = sb("rows_m", [100, T], F32R)
        sel = sb("sel", [100, 36], F32R)
        ones = sb("ones", [P, P])
        ident = sb("ident", [P, P])
        with ExitStack() as r:
            vec_rows = sb("vec_rows", [64, P], F32, r)
            cols = sb("cols", [P, TT, 100], F32, r)
            gate_raw = sb("gate_raw", [P, KC, 2 * RANK], F32, r)
        w_a2 = sb("w_a2", [96, 2, QK], F32R)
        vec = sb("vec", [P, 64])
        gate_bias = sb("gate_bias", [P, 1])
        head_sq = sb("head_sq", [P, 2, TT])
        head_rstd = sb("head_rstd", [P, 2, TT])
        den = sb("den", [P, 2, 2])
        eps_col = sb("eps_col", [P, 1])

        with ExitStack() as r:
            h_hi = sb("h_hi", [P, KC, T], F32R, r)
            h_lo = sb("h_lo", [P, KC, T], F32R, r)
        with ExitStack() as r:
            decay = sb("decay", [P, 2, 2, PW], F32, r)
            hs_m = sb("hs_m", [P, 2, TT, DV], F32, r)
        region_h = ctx.enter_context(ExitStack())
        qe = sb("qe", [P, 2, 2, T], F32, region_h)
        ke = sb("ke", [P, 2, 2, T], F32, region_h)
        bsum = sb("bsum", [P, 2, T], F32, region_h)
        k_tok = sb("k_tok", [P, 2, 4, P], F32, region_h)
        state = sb("state", [P, 2, DV], F32, region_h)
        s_piv = sb("s_piv", [P, 2, 4, DV], F32, region_h)
        hs_g = [sb("hs_g0", [P, TT, DV], F32, region_h), hs_g1]
        a_sb = sb("a_sb", [P, 3, 2, 2, P], F32, region_h)
        piv = sb("piv", [P, 2, TT], F32, region_h)
        step_log = sb("step_log", [P, 2, 2, TT - 1], F32, region_h)
        step_exp = sb("step_exp", [P, 2, TT - 1], F32, region_h)

        HR = 2 * T + TT * (DV + 1)
        with ExitStack() as r:
            xs = sb("xs", [P, TT, D], F32, r)
        with ExitStack() as r:
            y_parts = sb("y_parts", [P, NH, HR], F32R, r)
        with ExitStack() as r:
            a_hi = sb("a_hi", [P, 8, T], F32R, r)
            a_lo = sb("a_lo", [P, 8, T], F32R, r)
        with ExitStack() as r:
            y_fin = sb("y_fin", [P, KC, T], F32, r)
            y_tok = sb("y_tok", [P, TT, D], F32, r)
        qkv = sb("qkv", [P, NH, HR])

        with ExitStack() as r:
            g_hi = sb("g_hi", [P, KC, P], F32R, r)
            g_lo = sb("g_lo", [P, KC, P], F32R, r)
            with ExitStack() as r2:
                g_pre = sb("g_pre", [100, T], F32, r2)
                g_soft = sb("g_soft", [100, T], F32, r2)
                g_log = sb("g_log", [64, T], F32, r2)
                g_cum = sb("g_cum", [64, T], F32, r2)
                g_cols = sb("g_cols", [P, T], F32, r2)
            with ExitStack() as r2:
                sg = sb("sg", [P, 4, HT], F32, r2)
                at = sb("at", [P, 4, HT], F32, r2)
                w_a2_raw = sb("w_a2_raw", [96, 2, QK], F32, r2)
        o_gate = sb("o_gate", [P, KC, T])

        bank = [ctx.enter_context(nc.psum_tensor(f"bank{i}", [P, 512], F32)) for i in range(8)]

        q_of = [qkv[:, h, 0:T] for h in range(NH)]
        k_of = [qkv[:, h, T:2 * T] for h in range(NH)]
        v_all = qkv[:, :, 2 * T:HR].rearrange("p h (t n) -> p h t n", t=TT)
        y_hi = [y_parts[:, c // 2, (c % 2) * T:(c % 2 + 1) * T] for c in range(KC)]
        y_lo = [y_parts[:, c // 2, (2 + c % 2) * T:(3 + c % 2) * T] for c in range(KC)]
        gain = [vec[:, 8 * e:8 * e + 8] for e in range(5)]
        head_g = [vec[:, 40:48], vec[:, 48:56]]
        b_a = vec[:, 56:64]

        x_loaded = [sem(f"x_loaded{t}") for t in range(TT)]
        vec_loaded, bias_loaded, a2_loaded = sem("vec_loaded"), sem("bias_loaded"), sem("a2_loaded")
        gate_w_loaded = sem("gate_w_loaded")
        raw_loaded = [sem(f"raw_loaded{s}") for s in range(2)]
        y_stored = sem("y_stored")
        consts = sem("consts")
        vec_t, vec_ready = sem("vec_t"), sem("vec_ready")
        w_hi_ready, w_lo_ready = sem("w_hi_ready"), sem("w_lo_ready")
        mm_done = sem("mm_done")
        taken = [sem(f"taken{s}") for s in range(2)]
        x_t, x_taken = sem("x_t"), sem("x_taken")
        sq_mul, sq_acc = sem("sq_mul"), sem("sq_acc")
        ss_done, ln_done, rstd_done = sem("ss_done"), sem("ln_done"), sem("rstd_done")
        ht_ready, hi_ready, lo_ready = sem("ht_ready"), sem("hi_ready"), sem("lo_ready")
        gw_zero, gw_hi, gw_lo = sem("gw_zero"), sem("gw_hi"), sem("gw_lo")
        gate_mm, gate_rows = sem("gate_mm"), sem("gate_rows")
        gate_act, gate_dve = sem("gate_act"), sem("gate_dve")
        cols_t, cols_ready = sem("cols_t"), sem("cols_ready")
        v_ones = sem("v_ones")
        a_hi_done, a_ready = sem("a_hi_done"), sem("a_ready")
        st_ready, cm_ready, exp_done, mask_done, p_ready = (
            sem("st_ready"), sem("cm_ready"), sem("exp_done"), sem("mask_done"), sem("p_ready"))
        pv_ready, den_step, fin_done = sem("pv_ready"), sem("den_step"), sem("fin_done")
        hsq_done, hln_done, hrstd_done, hsn_done, tr_ready = (
            sem("hsq_done"), sem("hln_done"), sem("hrstd_done"), sem("hsn_done"), sem("tr_ready"))
        z_ready, z_taken, z_abs, z_exp, z_ln, lg_ready = (
            sem("z_ready"), sem("z_taken"), sem("z_abs"), sem("z_exp"), sem("z_ln"), sem("lg_ready"))
        scanned, piv_ready, step_ready, centred, e_ready, qk_ready = (
            sem("scanned"), sem("piv_ready"), sem("step_ready"), sem("centred"), sem("e_ready"), sem("qk_ready"))
        a_mm, a_taken, a_masked, a_summed = sem("a_mm"), sem("a_taken"), sem("a_masked"), sem("a_summed")
        a2_zero, a2_split, rows_hi = sem("a2_zero"), sem("a2_split"), sem("rows_hi")
        kt_ready, kt_taken, u_ready, first_state, state_step = (
            sem("kt_ready"), sem("kt_taken"), sem("u_ready"), sem("first_state"), sem("state_step"))
        o_mm = sem("o_mm")
        fin_t = sem("fin_t")
        fin_copied = [sem(f"fin_copied{i}") for i in range(2)]

        halves = [slice(0, HT), slice(HT, T)]
        block = ctx.enter_context(nc.Block())

        @block.sync
        def _(sp):
            def load_x(t):
                src = x_prompt[0, t * P:(t + 1) * P, :] if t < 4 else x_sample[0, (t - 4) * P:(t - 3) * P, :]
                sp.dma_start(xs[:, t, :], src).then_inc(x_loaded[t], 16)

            load_x(0)
            load_x(1)
            load_x(2)
            srcs = [norm_mix_g[0], norm_ffn_g[0], norm_mix_g[1], norm_ffn_g[1], norm_final_g,
                    mlstm_head_g[0], gla_head_g[0]]
            for i, src in enumerate(srcs):
                sp.dma_start(vec_rows[8 * i:8 * i + 8, :], src.rearrange("(c p) -> c p", p=P)).then_inc(vec_loaded, 16)
            sp.dma_start(vec_rows[56:64, :], gla_b_a[0].rearrange("d (h p) -> (d h) p", p=P)).then_inc(vec_loaded, 16)

            def load_w(q, s, src, wait=True):
                if wait:
                    sp.wait_ge(w_lo_ready, 2 * q + s - 1)
                sp.dma_start(raw[s][:, 0:src.shape[1], :], src).then_inc(raw_loaded[s], 16)

            for s in range(2):
                load_w(0, s, w_in[0][:, :, s * W:(s + 1) * W], wait=False)
            sp.dma_start(gate_raw[:, :, 0:16], w_in[0][:, :, 3072:3088]).then_inc(gate_w_loaded, 16)
            load_x(3)
            load_x(4)
            load_x(5)
            sp.wait_ge(consts, 4)
            for at_p, c in ((0, 0), (32, 8), (64, 4), (96, 12)):
                sp.dma_start(gate_bias[at_p:at_p + 4, :],
                             mlstm_b_gate[0, c:c + 4].rearrange("(p a) -> p a", a=1)).then_inc(bias_loaded, 16)

            for L in range(2):
                q0 = PAIRS * L
                with sp.Fori(1 - L, 6) as i:
                    for s in range(2):
                        load_w(i + q0, s, w_in[L][:, :, bass.ds(i * (2 * W) + s * W, W)])
                with sp.Fori(0, 2) as i:
                    for s in range(2):
                        load_w(i + q0 + POUT, s, w_out[L][:, :, bass.ds(i * (2 * W) + s * W, W)])
                if L == 0:
                    sp.wait_ge(gw_lo, 2)
                    sp.dma_start(gate_raw[:, :, :], w_in[1][:, :, 3072:3104]).then_inc(gate_w_loaded, 16)
                for b, nb in enumerate(BLOCKS):
                    c0 = sum(BLOCKS[:b])
                    with sp.Fori(0, nb // 2) as i:
                        for s in range(2):
                            load_w(i + q0 + PGU[b], s, w_gu[L][:, :, bass.ds(i * W + (s * DFF + c0 * P), W)])
                    with sp.Fori(0, 2) as i:
                        for s in range(2):
                            load_w(i + q0 + PDN[b], s, w_dn[L][:, c0:c0 + nb, bass.ds(i * (2 * W) + s * W, W)])
                    if L == 0 and b == 0:
                        sp.wait_ge(a2_zero, 1)
                        for k in range(3):
                            for d in range(2):
                                p0 = 32 * k + RANK * d
                                sp.dma_start(w_a2_raw[p0:p0 + RANK, d, :], gla_w_a2[0, d]).then_inc(a2_loaded, 16)

            for t in range(TT):
                for hf in range(2):
                    sp.wait_ge(fin_copied[hf], t + 1)
                dst = y_prompt[0, t * P:(t + 1) * P, :] if t < 4 else y_sample[0, (t - 4) * P:(t - 3) * P, :]
                sp.dma_start(dst, y_tok[:, t, :]).then_inc(y_stored, 16)
            sp.wait_ge(y_stored, 16 * TT)

        @block.tensor
        def _(pe):
            def mm(out, lhsT, rhs, start, stop):
                return nc.tensor.matmul(out, lhsT, rhs, start=start, stop=stop)

            def group(out, wh, wl, rh, rl, half, kdim, before=None, k_from=0, last_k=True):
                for k in range(k_from, kdim):
                    if before is not None:
                        before(k)
                    r0, r1 = rh(k)[:, halves[half]], rl(k)[:, halves[half]]
                    mm(out, wh(k), r0, k == 0, False)
                    mm(out, wh(k), r1, False, False)
                    last = mm(out, wl(k), r0, False, k == kdim - 1 and last_k)
                return last

            h_parts = (lambda k: h_hi[:, k, :]), (lambda k: h_lo[:, k, :])
            y_parts_ = (lambda k: y_hi[k]), (lambda k: y_lo[k])
            a_parts = (lambda k: a_hi[:, k, :]), (lambda k: a_lo[:, k, :])

            def tile_begin(q, s):
                pe.wait_ge(w_lo_ready, 2 * q + s + 1)
                pe.wait_ge(taken[s], 4 * q)

            def tile_group(s, g, parts, kdim, before=None):
                half, m = g // 2, g % 2
                cs = slice(m * P, (m + 1) * P)
                last = group(bank[4 * s + g][:, 0:HT], lambda k: w_hi[s][:, k, cs], lambda k: w_lo[s][:, k, cs],
                             *parts, half, kdim, before)
                last.then_inc(mm_done, 1)
                return last

            def tile_seq(q, s, parts, kdim, before=(None,) * 4, hook=None):
                hook = hook or {}
                tile_begin(q, s)
                for g in range(4):
                    last = tile_group(s, g, parts, kdim, before[g])
                    if g in hook:
                        hook[g]()

            def sum_squares(e, half):
                if e == 0:
                    pe.wait_ge(sq_acc, 8 * (half + 1))
                else:
                    pe.wait_ge(sq_acc, 16 * e + 14 + 2 * half)
                mm(bank[3 * half][:, 0:HT], ones[:, :], sq_sum[:, half, :], True, True).then_inc(ss_done, 1)

            def parts_of(e, half):
                def before(k):
                    pe.wait_ge(lo_ready, NORM_S[e] + 8 * half + k + 1)
                return before

            pe.wait_ge(consts, 4)
            pe.wait_ge(vec_loaded, 16 * 8)
            nc.tensor.transpose(bank[7][:, 0:64], vec_rows[:, :], ident[0:64, 0:64]).then_inc(vec_t, 1)

            def x_chunks(half):
                for t in range(3):
                    pe.wait_ge(x_loaded[3 * half + t], 16)
                for c in range(KC):
                    j = 8 * half + c
                    if j == 7:
                        pe.wait_ge(vec_ready, 1)
                    if j >= 8:
                        pe.wait_ge(x_taken, j - 7)
                    for t in range(3):
                        last = nc.tensor.transpose(bank[j % 8][:, t * P:(t + 1) * P],
                                                   xs[:, 3 * half + t, c * P:(c + 1) * P], ident[:, :])
                    last.then_inc(x_t, 1)

            x_chunks(0)
            sum_squares(0, 0)
            pe.wait_ge(ln_done, 1)
            x_chunks(1)

            def mlstm(q0):
                q1 = q0 + POUT
                pe.wait_ge(taken[0], 4 * q1)
                pe.wait_ge(taken[1], 4 * q1)

                def scores(h, tiles):
                    if h and tiles[0] == 0:
                        pe.wait_ge(p_ready, 12 * (h - 1) + 8)
                        if h >= 2:
                            pe.wait_ge(ht_ready, Y_S[0] + 4 * (h - 1))
                    if h and tiles[0] == 4:
                        pe.wait_ge(fin_done, 12 * (h - 1) + 9)
                    for j in tiles:
                        first, last_t = FIRST_T[j] * P, (LAST_T[j] + 1) * P
                        out = bank[j][:, :] if j < 4 else bank[4][:, (j - 4) * 256:(j - 3) * 256]
                        mm(out, k_of[h][:, j * P:(j + 1) * P], q_of[h][:, first:last_t], True, True
                           ).then_inc(st_ready, 1)

                def maxima(h, piece):
                    n = 3 * h + piece
                    if n:
                        pe.wait_ge(exp_done, 4 * n)
                    for d, cs, at_c in ([(0, slice(0, 512), 0)], [(1, slice(0, 512), 0)],
                                        [(0, slice(512, T), 0), (1, slice(512, T), 256)])[piece]:
                        r = 32 * d + h
                        last = mm(bank[5][:, at_c:at_c + cs.stop - cs.start],
                                  sel[:, r:r + 1].to_broadcast([100, P]), rows_m[:, cs], True, True)
                    last.then_inc(cm_ready, 1)

                def output(h, i):
                    d, t = OUTS[i]
                    n = 12 * h + i
                    b = OUT_BANKS[n]
                    if b in OUT_BANKS[:n]:
                        before = max(m for m in range(n) if OUT_BANKS[m] == b)
                        pe.wait_ge(fin_done, before + 1)
                    pe.wait_ge(p_ready, 12 * h + (t + 1 if i < 4 else 8 if i < 8 else 12))
                    if b == 4:
                        pe.wait_ge(p_ready, 12 * (h + 1))
                    js = range(FIRST_T[t], t + 1) if d == 0 else range(t, LAST_T[t] + 1)
                    for j in js:
                        at_c = OFF[d, j] + t * P - span(d, j)[0]
                        last = mm(bank[b][:, 0:DV + 1], decay[:, h % 2, d, at_c:at_c + P],
                                  v_all[:, h, j, :], j == js[0], j == js[-1])
                    last.then_inc(pv_ready, 1)

                def turn(h, g, b):
                    half, cc = g // 2, g % 2
                    pe.wait_ge(hsn_done, TT * (h + 1))
                    for t in range(3):
                        last = nc.tensor.transpose(bank[b][:, t * P:(t + 1) * P],
                                                   hs_m[:, h % 2, 3 * half + t, cc * P:(cc + 1) * P], ident[:, :])
                    last.then_inc(tr_ready, 1)

                pe.wait_ge(v_ones, 1)
                scores(0, range(TT))
                for piece in range(3):
                    maxima(0, piece)
                for h in range(NH):
                    for i in range(12):
                        output(h, i)
                        if h + 1 < NH and i % 4 == 0:
                            maxima(h + 1, i // 4)
                        if h and i in TURN_AT:
                            pe.wait_ge(p_ready, 12 * h + 8)
                            for g in range(2):
                                turn(h - 1, 2 * TURN_AT.index(i) + g, 2 * TURN_AT.index(i) + g)
                        if h + 1 < NH and i == SCORES_AT:
                            scores(h + 1, range(4))
                    if h + 1 < NH:
                        scores(h + 1, (4, 5))
                pe.wait_ge(ht_ready, Y_S[0] + 4 * (NH - 1))
                return lambda g: turn(NH - 1, g, 4 + g)

            def logit(h, d, half, b):
                mm(bank[b][:, 0:HT], w_a2[:, d, h * DK:(h + 1) * DK], rows_g[:, halves[half]], True, True
                   ).then_inc(z_ready, 1)

            def gla(q0):
                q1 = q0 + POUT
                pe.wait_ge(taken[0], 4 * q1)
                pe.wait_ge(taken[1], 4 * q1)

                def gate_logits(h):
                    if h >= 2:
                        pe.wait_ge(state_step, 8 * (h - 1))
                        pe.wait_ge(a_taken, 3 * (h - 1))
                        pe.wait_ge(kt_taken, 2 * (h - 1))
                        if h >= 3:
                            pe.wait_ge(ht_ready, Y_S[1] + 4 * (h - 2))
                    for d in range(2):
                        for half in range(2):
                            logit(h, d, half, 3 * d + half)

                def chunk_scores(h, g):
                    if g < 2 and h >= 2:
                        pe.wait_ge(ht_ready, Y_S[1] + 4 * (h - 2) + 2)
                    if g == 0 and h:
                        pe.wait_ge(a_taken, 3 * h)
                    if g == 1:
                        pe.wait_ge(z_taken, 4 * min(h + 2, NH))
                    if g == 2:
                        pe.wait_ge(a_taken, 3 * h + 1)
                    for i in range(2):
                        for d in range(2):
                            ts = slice((2 * g + i) * P, (2 * g + i + 1) * P)
                            last = mm(bank[2 + g % 2][:, (2 * i + d) * P:(2 * i + d + 1) * P],
                                      ke[:, h % 2, d, ts], qe[:, h % 2, d, ts], True, True)
                    last.then_inc(a_mm, 1)

                def keys_by_token(h, d):
                    if d == 0:
                        pe.wait_ge(z_taken, 4 * min(h + 2, NH))
                        if h >= 2:
                            pe.wait_ge(ht_ready, Y_S[1] + 4 * (h - 2) + 3)
                    if d == 1 and h:
                        pe.wait_ge(hsn_done, TT * (NH + h))
                    for i, t in enumerate(UPD[d]):
                        last = nc.tensor.transpose(bank[4 + 3 * d][:, i * P:(i + 1) * P],
                                                   ke[:, h % 2, d, t * P:(t + 1) * P], ident[:, :])
                    last.then_inc(kt_ready, 1)

                def updates(h, d):
                    pe.wait_ge(kt_taken, 2 * h + d + 1)
                    if d == 0 and h:
                        pe.wait_ge(hsn_done, TT * (NH + h - 1) + 4)
                    if d == 1:
                        pe.wait_ge(z_taken, 4 * min(h + 2, NH))
                        pe.wait_ge(state_step, 8 * h)
                    for i, t in enumerate(UPD[d]):
                        last = mm(bank[5 - 5 * d + i // 2][:, (i % 2) * DV:(i % 2 + 1) * DV], k_tok[:, d, i, :],
                                  v_all[:, h, t, 0:DV], True, True)
                        if i % 2:
                            last.then_inc(u_ready, 1)

                def outputs(h, g):
                    n = 3 * h + g
                    pe.wait_ge(a_summed, n + 1)
                    if g == 0:
                        pe.wait_ge(state_step, 8 * (h + 1))
                    if g == 2 and h:
                        pe.wait_ge(ht_ready, Y_S[1] + 4 * h)
                    for i in range(2):
                        t = 2 * g + i
                        ts = slice(t * P, (t + 1) * P)
                        ops = [(a_sb[:, g, i, 0, :], v_all[:, h, t, 0:DV])]
                        if t != FIRST_T[t]:
                            ops.append((qe[:, h % 2, 0, ts], s_piv[:, 0, UPD[0].index(t - 1), :]))
                        if t != LAST_T[t]:
                            ops.append((qe[:, h % 2, 1, ts], s_piv[:, 1, UPD[1].index(t + 1), :]))
                        for k, (a, b_) in enumerate(ops):
                            last = mm(bank[5 + g][:, i * DV:(i + 1) * DV], a, b_, k == 0, k == len(ops) - 1)
                    last.then_inc(o_mm, 1)

                def turn(h, g, b):
                    half, cc = g // 2, g % 2
                    pe.wait_ge(hsn_done, TT * (NH + h) + 3 * (half + 1))
                    for t in range(3):
                        last = nc.tensor.transpose(bank[b][:, t * P:(t + 1) * P],
                                                   hs_g[h % 2][:, 3 * half + t, cc * P:(cc + 1) * P], ident[:, :])
                    last.then_inc(tr_ready, 1)

                gate_logits(1)
                for h in range(NH):
                    pe.wait_ge(qk_ready, 4 * (h + 1))
                    chunk_scores(h, 0)
                    chunk_scores(h, 1)
                    for d in range(2):
                        keys_by_token(h, d)
                    chunk_scores(h, 2)
                    if h:
                        pe.wait_ge(a_taken, 3 * h + 2)
                        turn(h - 1, 0, 3)
                    for d in range(2):
                        updates(h, d)
                    if h:
                        pe.wait_ge(a_taken, 3 * h + 3)
                        pe.wait_ge(kt_taken, 2 * h + 2)
                        for g in range(1, 4):
                            turn(h - 1, g, TURN[g])
                    outputs(h, 0)
                    outputs(h, 1)
                    if h + 2 < NH:
                        gate_logits(h + 2)
                    outputs(h, 2)
                pe.wait_ge(a_taken, 3 * NH)
                return lambda g: turn(NH - 1, g, 4 + g)

            for L in range(2):
                q0 = PAIRS * L
                e = 2 * L
                if L == 0:
                    pe.wait_ge(x_taken, 16)
                pe.wait_ge(gw_lo, L + 2)

                def gates(half):
                    group(bank[4 + half][:, 0:HT], lambda k: g_hi[:, k, :], lambda k: g_lo[:, k, :],
                          *h_parts, half, KC, parts_of(e, half)).then_inc(gate_mm, 1)

                gates(0)
                sum_squares(e, 1)
                tile_begin(q0, 0)
                tile_group(0, 0, h_parts, KC)
                tile_group(0, 1, h_parts, KC)
                gates(1)
                tile_group(0, 2, h_parts, KC)
                tile_group(0, 3, h_parts, KC)
                pe.wait_ge(gate_rows, 2 * L + 2)
                tile_seq(q0, 1, h_parts, KC)
                for s in range(2):
                    tile_seq(q0 + PK, s, h_parts, KC)
                if L == 1:
                    pe.wait_ge(a2_split, 2)
                    pe.wait_ge(taken[0], 4 * (q0 + PK) + 4)
                    logit(0, 0, 0, 3)
                    pe.wait_ge(taken[1], 4 * (q0 + PK) + 4)
                    logit(0, 0, 1, 7)
                with pe.Fori(0, 2) as i:
                    for s in range(2):
                        tile_begin(i + q0 + PV_, s)
                        for t in range(TT):
                            out = bank[4 * s + t // 2][:, (t % 2) * W:(t % 2 + 1) * W]
                            ts = slice(t * P, (t + 1) * P)
                            for k in range(KC):
                                mm(out, h_hi[:, k, ts], w_hi[s][:, k, :], k == 0, False)
                                mm(out, h_lo[:, k, ts], w_hi[s][:, k, :], False, False)
                                last = mm(out, h_hi[:, k, ts], w_lo[s][:, k, :], False, k == KC - 1)
                            if t % 2 == 1:
                                last.then_inc(mm_done, 2 if t == TT - 1 else 1)
                if L == 0:
                    pe.wait_ge(gate_act, 4)
                    for t in range(TT):
                        last = nc.tensor.transpose(bank[3 + 4 * (t // 3)][:, (t % 3) * 100:(t % 3 + 1) * 100],
                                                   g_cols[0:100, t * P:(t + 1) * P], ident[0:100, 0:100])
                    last.then_inc(cols_t, 1)
                    pe.wait_ge(cols_ready, 2)
                else:
                    for half in range(2):
                        pe.wait_ge(z_taken, half + 1)
                        logit(0, 1, half, 3 + 4 * half)
                    pe.wait_ge(z_taken, 4)
                with pe.Fori(0, 2) as i:
                    for s in range(2):
                        tile_seq(i + q0 + PO, s, h_parts, KC)
                last_turn = (mlstm if L == 0 else gla)(q0)

                def y_before(half):
                    def before(k):
                        pe.wait_ge(lo_ready, Y_S[L] + 4 * (k // 2) + 2 * half + k % 2 + 1)
                    return before

                q = q0 + POUT
                tile_begin(q, 0)
                for k0, k1 in ((0, KC - 2), (KC - 2, KC)):
                    for g in range(4):
                        if k0 == 0 and g >= 2:
                            last_turn(2 * g - 4)
                            last_turn(2 * g - 3)
                        half, cs = g // 2, slice(g % 2 * P, (g % 2 + 1) * P)
                        last = group(bank[g][:, 0:HT], lambda k: w_hi[0][:, k, cs], lambda k: w_lo[0][:, k, cs],
                                     *y_parts_, half, k1, y_before(half), k0, k1 == KC)
                        if k0:
                            last.then_inc(mm_done, 1)
                pe.wait_ge(ht_ready, Y_S[L] + 4 * NH)
                tile_seq(q, 1, y_parts_, KC)

                def first_sum(q, e):
                    pe.wait_ge(taken[0], 4 * (q + 1))
                    sum_squares(e, 0)

                tile_seq(q + 1, 0, y_parts_, KC)
                tile_seq(q + 1, 1, y_parts_, KC, hook={2: lambda: first_sum(q + 1, e + 1)})

                for b, nb in enumerate(BLOCKS):
                    n_pairs = nb // 2
                    start = 0
                    if b == 0:
                        tile_seq(q0 + PGU[0], 0, h_parts, KC, (parts_of(e + 1, 0), None, parts_of(e + 1, 1), None),
                                 hook={0: lambda: sum_squares(e + 1, 1)})
                        tile_seq(q0 + PGU[0], 1, h_parts, KC)
                        start = 1
                    with pe.Fori(start, n_pairs) as i:
                        for s in range(2):
                            tile_seq(i + q0 + PGU[b], s, h_parts, KC)

                    f0 = 4 * (FFP * L + sum(BLOCKS[:b]) // 2) + 4

                    def a_before(half):
                        def before(k):
                            pe.wait_ge(a_ready, f0 + 4 * (k // 2) + 2 * half + k % 2 + 1)
                        return before

                    q = q0 + PDN[b]
                    if b < 2:
                        with pe.Fori(0, 2) as i:
                            pe.wait_ge(a_ready, f0 + 4 * n_pairs - 3)
                            tile_seq(i + q, 0, a_parts, nb, (a_before(0), None, a_before(1), None))
                            tile_seq(i + q, 1, a_parts, nb)
                    else:
                        tile_seq(q, 0, a_parts, nb, (a_before(0), None, a_before(1), None))
                        tile_seq(q, 1, a_parts, nb)
                        tile_seq(q + 1, 0, a_parts, nb)
                        tile_seq(q + 1, 1, a_parts, nb, hook={2: lambda: first_sum(q + 1, e + 2)})

            sum_squares(4, 1)
            for t in range(TT):
                for hf in range(2):
                    n = 2 * t + hf
                    pe.wait_ge(ht_ready, 96 + 8 * (t // 3) + 4 * hf + 4)
                    if n == 0:
                        pe.wait_ge(taken[1], 8 * PAIRS)
                    if t:
                        pe.wait_ge(fin_copied[hf], t)
                    for c in range(4):
                        last = nc.tensor.transpose(bank[4 + n % 2][:, c * P:(c + 1) * P],
                                                   y_fin[:, 4 * hf + c, t * P:(t + 1) * P], ident[:, :])
                    last.then_inc(fin_t, 1)

        @block.scalar
        def _(act):
            def split(q, s, wait=True):
                act.wait_ge(raw_loaded[s], 16 * (q + 1))
                if wait:
                    act.wait_ge(mm_done, 8 * q + (4 * s - 4))
                nc.scalar.copy(w_hi[s][:, :, :], raw[s][:, :, :]).then_inc(w_hi_ready, 1)

            def high(s, out):
                act.wait_ge(ht_ready, s + 1)
                nc.scalar.copy(out, ht[:, s % 4, :]).then_inc(hi_ready, 1)

            def log_exp_table():
                nc.scalar.preload_act_table_set("natural_log_exp_and_others")

            def norm(e):
                for half in range(2):
                    act.wait_ge(ss_done, 2 * e + half + 1)
                    nc.scalar.activation(rstd[:, half, :], bank[3 * half][:, 0:HT], ACT.Ln,
                                         bias=eps_col[:, 0:1], scale=1.0 / D).then_inc(ln_done, 1)
                    act.wait_ge(ln_done, 2 * e + half + 1)
                    nc.scalar.activation(rstd[:, half, :], rstd[:, half, :], ACT.Exp, scale=-0.5).then_inc(rstd_done, 1)
                    for c in range(KC if e < 4 else 0):
                        high(NORM_S[e] + 8 * half + c, h_hi[:, c, halves[half]])

            def y_high(L, h, g):
                high(Y_S[L] + 4 * h + g, y_hi[2 * h + g % 2][:, halves[g // 2]])

            def take(q, s, g):
                act.wait_ge(mm_done, 8 * q + (4 * s + g + 1))
                return bank[4 * s + g][:, 0:HT]

            def head_norm(h, hs, order, taken):
                for n, t in enumerate(order):
                    taken(t)
                    if n:
                        act.wait_ge(hsq_done, TT * h + n)
                    nc.scalar.activation(junk[:, :], hs[:, t, :], ACT.Square,
                                         accum_out=head_sq[:, h % 2, t:t + 1]).then_inc(hsq_done, 1)
                act.wait_ge(hsq_done, TT * (h + 1))
                nc.scalar.activation(head_rstd[:, h % 2, :], head_sq[:, h % 2, :], ACT.Ln,
                                     bias=eps_col[:, 0:1], scale=1.0 / DV).then_inc(hln_done, 1)
                act.wait_ge(hln_done, h + 1)
                nc.scalar.activation(head_rstd[:, h % 2, :], head_rstd[:, h % 2, :], ACT.Exp,
                                     scale=-0.5).then_inc(hrstd_done, 1)
                act.wait_ge(hrstd_done, h + 1)
                for t in range(TT):
                    nc.scalar.mul(hs[:, t, :], hs[:, t, :], head_rstd[:, h % 2, t:t + 1]).then_inc(hsn_done, 1)

            def mlstm():
                log_exp_table()
                act.wait_ge(cols_ready, 2)

                def decays(h, piece):
                    n = 3 * h + piece
                    act.wait_ge(cm_ready, n + 1)
                    if h >= 2:
                        act.wait_ge(pv_ready, 12 * (h - 1))
                    for d, j in PIECES[piece]:
                        t0, w = span(d, j)
                        c0 = t0 if piece < 2 else t0 - 512 + 256 * d
                        nc.scalar.activation(decay[:, h % 2, d, OFF[d, j]:OFF[d, j] + w], bank[5][:, c0:c0 + w],
                                             ACT.Exp, bias=cols[:, j, 32 * d + h:32 * d + h + 1],
                                             scale=-1.0).then_inc(exp_done, 1)

                for piece in range(3):
                    decays(0, piece)
                for h in range(NH):
                    if h + 1 < NH:
                        decays(h + 1, 0)
                        decays(h + 1, 1)
                    if h:
                        y_high(0, h - 1, 0)
                        y_high(0, h - 1, 1)
                    if h + 1 < NH:
                        decays(h + 1, 2)
                    if h:
                        y_high(0, h - 1, 2)
                        y_high(0, h - 1, 3)
                    order = (3, 2, 1, 0, 5, 4)
                    head_norm(h, hs_m[:, h % 2], order,
                              lambda t: act.wait_ge(fin_done, 12 * h + OUTS.index((1, t)) + 1))
                for g in range(4):
                    y_high(0, NH - 1, g)

            def softplus(h, d, part, z, out):
                n = 2 * h + d
                if part == 0:
                    act.wait_ge(z_taken, 2 * n + 2)
                    nc.scalar.activation(out, z, ACT.Abs).then_inc(z_abs, 1)
                else:
                    act.wait_ge(z_abs, n + 1)
                    nc.scalar.activation(out, out, ACT.Exp, scale=-1.0).then_inc(z_exp, 1)
                    act.wait_ge(z_exp, n + 1)
                    nc.scalar.activation(out, out, ACT.Ln, bias=ones[:, 0:1]).then_inc(z_ln, 1)

            def gla():
                def take_scores(h, g):
                    n = 3 * h + g
                    act.wait_ge(a_mm, n + 1)
                    if h:
                        act.wait_ge(o_mm, n - 2)
                    nc.scalar.copy(a_sb[:, g], bank[2 + g % 2][:, :]).then_inc(a_taken, 1)

                def take_keys(h, d):
                    n = 2 * h + d
                    act.wait_ge(kt_ready, n + 1)
                    if h:
                        act.wait_ge(u_ready, 2 * n - 2)
                    nc.scalar.copy(k_tok[:, d], bank[4 + 3 * d][:, :]).then_inc(kt_taken, 1)

                def exponentials(h, d):
                    sl = h % 2
                    if h:
                        act.wait_ge(state_step, 4 * (2 * h - 1 + d))
                        act.wait_ge(kt_ready, 2 * h)
                    act.wait_ge(step_ready, 2 * (2 * h + d) + 2)
                    nc.scalar.activation(step_exp[:, d], step_log[:, d, 1], ACT.Exp,
                                         scale=1.0 / GLA_TAU).then_inc(e_ready, 1)
                    act.wait_ge(centred, 2 * h + d + 1)
                    sums = bsum if h else b0_sum
                    nc.scalar.activation(qe[:, sl, d, :], sums[:, d, :], ACT.Exp,
                                         scale=1.0 / GLA_TAU).then_inc(e_ready, 1)
                    nc.scalar.activation(ke[:, sl, d, :], sums[:, d, :], ACT.Exp,
                                         scale=-1.0 / GLA_TAU).then_inc(e_ready, 1)

                def first_states(h, d):
                    n = 2 * h + d
                    if h and d == 0:
                        act.wait_ge(o_mm, 3 * h)
                    act.wait_ge(e_ready, 6 * h + 3 * d + 1)
                    for i in (0, 3):
                        act.wait_ge(u_ready, 2 * n + 1 + i // 2)
                        t = UPD[d][i]
                        nc.scalar.mul(s_piv[:, d, i, :], bank[5 - 5 * d + i // 2][:, (i % 2) * DV:(i % 2 + 1) * DV],
                                      step_exp[:, d, t - d:t - d + 1]).then_inc(first_state, 1)

                def output_norm(h, g):
                    n = 3 * h + g
                    ts = slice(2 * g, 2 * g + 2)
                    act.wait_ge(o_mm, n + 1)
                    for i in range(2):
                        act.wait_ge(hsq_done, TT * NH + 2 * n + i)
                        nc.scalar.activation(junk[:, :], bank[5 + g][:, i * DV:(i + 1) * DV], ACT.Square,
                                             accum_out=head_sq[:, h % 2, 2 * g + i:2 * g + i + 1]).then_inc(hsq_done, 1)
                    act.wait_ge(hsq_done, TT * NH + 2 * n + 2)
                    if h >= 2:
                        act.wait_ge(hsn_done, TT * (NH + h - 1))
                    nc.scalar.activation(head_rstd[:, h % 2, ts], head_sq[:, h % 2, ts], ACT.Ln,
                                         bias=eps_col[:, 0:1], scale=1.0 / DV).then_inc(hln_done, 1)
                    act.wait_ge(hln_done, NH + n + 1)
                    nc.scalar.activation(head_rstd[:, h % 2, ts], head_rstd[:, h % 2, ts], ACT.Exp,
                                         scale=-0.5).then_inc(hrstd_done, 1)

                log_exp_table()
                act.wait_ge(mm_done, 8 * (PAIRS + POUT))
                for d in range(2):
                    exponentials(0, d)
                for h in range(NH):
                    z, soft = [[part[:, (h + 1) % 2, d, :] for d in range(2)] for part in (ke, qe)]
                    if h + 1 < NH:
                        if h:
                            act.wait_ge(o_mm, 3 * h)
                        for d in range(2):
                            softplus(h + 1, d, 0, z[d], soft[d])
                    if h:
                        output_norm(h - 1, 2)
                    if h + 1 < NH:
                        softplus(h + 1, 0, 1, z[0], soft[0])
                    take_scores(h, 0)
                    if h + 1 < NH:
                        softplus(h + 1, 1, 1, z[1], soft[1])
                    take_scores(h, 1)
                    for d in range(2):
                        take_keys(h, d)
                    take_scores(h, 2)
                    for d in range(2):
                        first_states(h, d)
                        if h + 1 < NH:
                            exponentials(h + 1, d)
                    if h:
                        for g in range(4):
                            y_high(1, h - 1, g)
                    for d in range(2):
                        output_norm(h, d)
                output_norm(NH - 1, 2)
                for g in range(4):
                    y_high(1, NH - 1, g)

            act.wait_ge(consts, 4)
            split(0, 0, wait=False)
            act.wait_ge(gate_w_loaded, 16)
            act.wait_ge(gw_zero, 1)
            for a in range(2):
                src = gate_raw[:, :, 8 * a:8 * a + 8].rearrange("p k (b r) -> p k b r", b=2)
                dst = g_hi[:, :, :].rearrange("p k (b a r) -> p k b a r", b=2, a=2)[:, :, :, a, 0:4]
                nc.scalar.copy(dst, src).then_inc(gw_hi, 1)
            norm(0)
            for L in range(2):
                q0 = PAIRS * L
                for kind in range(2):
                    q = q0 + kind
                    for s in range(2):
                        if s == 0:
                            split(q, 1, wait=q > 0)
                        else:
                            split(q + 1, 0)
                        for g in range(4):
                            h = 2 * s + g % 2
                            src = take(q, s, g)
                            dst = (k_of if kind else q_of)[h][:, halves[g // 2]]
                            ins = nc.scalar.mul(dst, src, 1.0 if kind else float(DK) ** -0.5)
                            ins.then_inc(taken[s], 1)
                if L == 0:
                    act.wait_ge(gate_rows, 2)
                    nc.scalar.activation(g_soft[64:100, :], g_pre[64:100, :], ACT.Abs).then_inc(gate_act, 1)
                    act.wait_ge(gate_act, 1)
                    nc.scalar.activation(g_soft[64:100, :], g_soft[64:100, :], ACT.Exp, scale=-1.0).then_inc(gate_act, 1)
                    act.wait_ge(gate_act, 2)
                    nc.scalar.activation(g_soft[64:100, :], g_soft[64:100, :], ACT.Ln,
                                         bias=ones[64:100, 0:1]).then_inc(gate_act, 1)
                    act.wait_ge(gate_dve, 11)
                    nc.scalar.activation(g_cols[64:100, :], g_log[0:36, :], ACT.Exp, scale=-1.0).then_inc(gate_act, 1)
                def first_softplus(d):
                    for part in range(2):
                        softplus(0, d, part, ht[:, 0:2, :], ht[:, 2:4, :])

                if L == 1:
                    log_exp_table()
                    first_softplus(0)
                with act.Fori(0, 2) as i:
                    for s in range(2):
                        q = i + q0 + PV_
                        if s == 0:
                            split(q, 1)
                        else:
                            split(q + 1, 0)
                        for g in range(3):
                            act.wait_ge(mm_done, 8 * q + (4 * s + g + 1 + (g == 2)))
                            dst = v_all[:, bass.ds(i * 2 + s, 1), 2 * g:2 * g + 2, 0:DV]
                            src = bank[4 * s + g][:, :].rearrange("p (a t n) -> p a t n", a=1, t=2)
                            nc.scalar.copy(dst, src).then_inc(taken[s], 2 if g == 2 else 1)
                if L == 0:
                    act.wait_ge(cols_ready, 2)
                else:
                    log_exp_table()
                    first_softplus(1)
                with act.Fori(0, 2) as i:
                    for s in range(2):
                        q = i + q0 + PO
                        if s == 0:
                            split(q, 1)
                        else:
                            split(q + 1, 0)
                        for g in range(4):
                            src = take(q, s, g)
                            dst = o_gate[:, bass.ds(i * 4 + (2 * s + g % 2), 1), halves[g // 2]]
                            nc.scalar.activation(dst, src, ACT.Silu if L else ACT.Sigmoid).then_inc(taken[s], 1)
                (gla if L else mlstm)()
                for i in range(2):
                    split(q0 + POUT + i, 1)
                    split(q0 + POUT + i + 1, 0)
                norm(2 * L + 1)
                for b, nb in enumerate(BLOCKS):
                    with act.Fori(0, nb // 2) as i:
                        q = i + q0 + PGU[b]
                        split(q, 1)
                        for g in range(4):
                            act.wait_ge(taken[1], 4 * q + (g - 3))
                            src = take(q, 0, g)
                            nc.scalar.activation(sg[:, g, :], src, ACT.Silu).then_inc(taken[0], 1)
                        split(q + 1, 0)
                    if L == 0 and b == 0:
                        act.wait_ge(gate_w_loaded, 32)
                        act.wait_ge(gw_zero, 2)
                        src = gate_raw[:, :, :].rearrange("p k (b r) -> p k b r", b=1)
                        dst = g_hi[:, :, :].rearrange("p k (b r) -> p k b r", b=4)[:, :, 0:3, :]
                        nc.scalar.copy(dst, src.to_broadcast([P, KC, 3, 2 * RANK])).then_inc(gw_hi, 1)
                    if L == 0 and b == 1:
                        act.wait_ge(a2_loaded, 16 * 6)
                        act.wait_ge(gw_lo, 3)
                        nc.scalar.copy(w_a2[:, :, :], w_a2_raw[:, :, :]).then_inc(a2_split, 1)
                    if b < 2:
                        with act.Fori(0, 2) as i:
                            split(i + q0 + PDN[b], 1)
                            split(i + q0 + PDN[b] + 1, 0)
                    else:
                        for i in range(2):
                            split(q0 + PDN[b] + i, 1)
                            if L == 0 or i == 0:
                                split(q0 + PDN[b] + i + 1, 0)
                norm(2 * L + 2)
            for t in range(TT):
                act.wait_ge(fin_t, 2 * t + 1)
                nc.scalar.copy(y_tok[:, t, 0:512], bank[4][:, :]).then_inc(fin_copied[0], 1)

        @block.vector
        def _(dve):
            V = nc.vector

            def split(q, s):
                dve.wait_ge(w_hi_ready, 2 * q + s + 1)
                V.tensor_tensor(w_lo[s][:, :, :], raw[s][:, :, :], w_hi[s][:, :, :].bitcast(F32),
                                ALU.subtract).then_inc(w_lo_ready, 1)

            def ring(s):
                if s >= 4:
                    dve.wait_ge(lo_ready, s - 3)

            def norm_half(e, half):
                dve.wait_ge(rstd_done, 2 * e + half + 1)
                for c in range(KC):
                    if e < 4:
                        s = NORM_S[e] + 8 * half + c
                        ring(s)
                        out = ht[:, s % 4, :]
                    else:
                        out = y_fin[:, c, halves[half]]
                    V.scalar_tensor_tensor(out=out, in0=xT[:, c, halves[half]], scalar=gain[e][:, c:c + 1],
                                           in1=rstd[:, half, :], op0=ALU.mult, op1=ALU.mult).then_inc(ht_ready, 1)

            def add_residual(q, s, g, c):
                dve.wait_ge(mm_done, 8 * q + (4 * s + g + 1))
                dve.wait_ge(taken[s], 4 * q + g)
                hs = halves[g // 2]
                if isinstance(c, int):
                    x, src = xT[:, c, hs], bank[4 * s + g][:, 0:HT]
                else:
                    x = xT[:, bass.ds(c, 1), hs]
                    src = bank[4 * s + g][:, 0:HT].rearrange("p (a n) -> p a n", a=1)
                V.tensor_tensor(x, x, src, ALU.add).then_inc(taken[s], 1)

            def y_take(L, h, g, b):
                s = Y_S[L] + 4 * h + g
                c = 2 * h + g % 2
                dve.wait_ge(tr_ready, 16 * L + 4 * h + g + 1)
                ring(s)
                V.scalar_tensor_tensor(out=ht[:, s % 4, :], in0=bank[b][:, 0:HT], scalar=head_g[L][:, c:c + 1],
                                       in1=o_gate[:, c, halves[g // 2]], op0=ALU.mult,
                                       op1=ALU.mult).then_inc(ht_ready, 1)

            def mlstm():
                row = (lambda d, h: 32 * d + h)

                def weights(h, k, piece):
                    n = 12 * h + 4 * piece + k
                    d, j = PIECES[piece][k]
                    t0, w = span(d, j)
                    dve.wait_ge(mask_done, n + 1)
                    dve.wait_ge(st_ready, TT * h + (4 if piece < 2 else 6))
                    first = FIRST_T[j] * P
                    src = bank[j][:, t0 - first:t0 - first + w] if j < 4 else \
                        bank[4][:, (j - 4) * 256 + t0 - first:(j - 4) * 256 + t0 - first + w]
                    at_d = decay[:, h % 2, d, OFF[d, j]:OFF[d, j] + w]
                    V.tensor_tensor(at_d, at_d, src, ALU.mult).then_inc(p_ready, 1)

                def denominator(n):
                    d, t = OUTS[n % 12]
                    b, dn = bank[OUT_BANKS[n]], den[:, n % 2, :]
                    r = 64 + row(d, n // 12)

                    def largest():
                        dve.wait_ge(pv_ready, n + 1)
                        if n >= 2:
                            dve.wait_ge(fin_done, n - 1)
                        V.tensor_scalar(dn[:, 0:1], b[:, DV:DV + 1], -1.0, cols[:, t, r:r + 1], ALU.mult, ALU.max
                                        ).then_inc(den_step, 1)

                    def inverse():
                        dve.wait_ge(den_step, 3 * n + 1)
                        V.tensor_scalar(dn[:, 0:1], b[:, DV:DV + 1], dn[:, 0:1], None, ALU.max).then_inc(den_step, 1)
                        dve.wait_ge(den_step, 3 * n + 2)
                        V.reciprocal(dn[:, 1:2], dn[:, 0:1]).then_inc(den_step, 1)

                    return largest, inverse

                def finish(n):
                    d, t = OUTS[n % 12]
                    b, dn = bank[OUT_BANKS[n]], den[:, n % 2, :]
                    out = hs_m[:, n // 12 % 2, t, :]
                    dve.wait_ge(den_step, 3 * n + 3)
                    if d == 0:
                        if n >= 24:
                            dve.wait_ge(tr_ready, 4 * (n // 12 - 1))
                        V.tensor_scalar(out, b[:, 0:DV], dn[:, 1:2], None, ALU.mult).then_inc(fin_done, 1)
                    else:
                        dve.wait_ge(fin_done, 12 * (n // 12) + OUTS.index((0, t)) + 1)
                        V.scalar_tensor_tensor(out=out, in0=b[:, 0:DV], scalar=dn[:, 1:2], in1=out,
                                               op0=ALU.mult, op1=ALU.add).then_inc(fin_done, 1)

                for piece in range(2):
                    for k in range(4):
                        weights(0, k, piece)
                for h in range(NH):
                    for k in range(4):
                        weights(h, k, 2)
                    for i in range(12):
                        n = 12 * h + i
                        largest, inverse = denominator(n)
                        largest()
                        if i:
                            finish(n - 1)
                        inverse()
                        if h and i - 1 in TURN_AT:
                            for g in range(2):
                                g += 2 * TURN_AT.index(i - 1)
                                y_take(0, h - 1, g, g)
                        if h + 1 < NH and i > SCORES_AT:
                            for k in range(2):
                                k += 2 * (i - SCORES_AT - 1)
                                weights(h + 1, k % 4, k // 4)
                    finish(12 * h + 11)
                for g in range(4):
                    y_take(0, NH - 1, g, 4 + g)

            def logits(h, d, banks, out):
                for half in range(2):
                    dve.wait_ge(z_ready, 4 * h + 2 * d + half + 1)
                    V.tensor_scalar(out[half], bank[banks[half]][:, 0:HT],
                                    b_a[:, 4 * d + h:4 * d + h + 1], None, ALU.add).then_inc(z_taken, 1)

            def log_gates(h, d, z, soft, sums):
                dve.wait_ge(z_ln, 2 * h + d + 1)
                V.scalar_tensor_tensor(out=soft, in0=z, scalar=0.0, in1=soft, op0=ALU.min, op1=ALU.subtract
                                       ).then_inc(lg_ready, 1)
                dve.wait_ge(lg_ready, 2 * h + d + 1)
                if h:
                    dve.wait_ge(e_ready, 6 * h)
                for t in range(TT):
                    lo = t * P
                    ts = slice(lo, lo + P) if d == 0 else slice(lo + P - 1, lo - 1 if t else None, -1)
                    V.tensor_tensor_scan(sums[:, ts], ones[:, :], soft[:, ts], 0.0,
                                         ALU.mult, ALU.add).then_inc(scanned, 1)

            def pivots(h, d, sums):
                dve.wait_ge(scanned, TT * (2 * h + d + 1))
                n = 2 * h + d
                b_t = sums.rearrange("p (c t) -> p c t", t=P)
                end = P - 1 if d == 0 else 0
                V.tensor_copy(piv[:, d, :], b_t[:, :, PIVOT]).then_inc(piv_ready, 1)
                dve.wait_ge(piv_ready, n + 1)
                if h:
                    dve.wait_ge(e_ready, 6 * h)
                cur, nxt = slice(d, TT - 1 + d), slice(1 - d, TT - d)
                V.tensor_tensor(step_log[:, d, 0, :], b_t[:, cur, end], piv[:, d, cur], ALU.subtract
                                ).then_inc(step_ready, 1)
                dve.wait_ge(step_ready, 2 * n + 1)
                V.tensor_tensor(step_log[:, d, 1, :], step_log[:, d, 0, :], piv[:, d, nxt], ALU.add
                                ).then_inc(step_ready, 1)
                c = piv[:, d, :].rearrange("p (c a) -> p c a", a=1).to_broadcast([P, TT, P])
                V.tensor_tensor(b_t, b_t, c, ALU.subtract
                                ).then_inc(centred, 1)

            def gla():
                def states(h, d):
                    n = 2 * h + d
                    dve.wait_ge(e_ready, 6 * h + 3 * d + 1)
                    u = [bank[5 - 5 * d + i // 2][:, (i % 2) * DV:(i % 2 + 1) * DV] for i in range(4)]
                    f = [step_exp[:, d, t - d:t - d + 1] for t in UPD[d]]
                    st = state[:, d, :]
                    for i in (1, 2):
                        dve.wait_ge(first_state, 2 * n + i)
                        if i == 2:
                            dve.wait_ge(state_step, 4 * n + 2)
                        V.tensor_tensor(st, s_piv[:, d, i - 1, :], u[i], ALU.add).then_inc(state_step, 1)
                        dve.wait_ge(state_step, 4 * n + 2 * i - 1)
                        V.tensor_scalar(s_piv[:, d, i, :], st, f[i], None, ALU.mult).then_inc(state_step, 1)

                def sum_directions(h, g):
                    n = 3 * h + g
                    dve.wait_ge(a_masked, 2 * n + 2)
                    a = a_sb[:, g]
                    V.tensor_tensor(a[:, :, 0, :], a[:, :, 0, :], a[:, :, 1, :], ALU.add).then_inc(a_summed, 1)

                def take_outputs(h, g):
                    dve.wait_ge(hrstd_done, NH + 3 * h + g + 1)
                    if h >= 2:
                        dve.wait_ge(tr_ready, 16 + 4 * (h - 1))
                    for i in range(2):
                        t = 2 * g + i
                        V.tensor_scalar(hs_g[h % 2][:, t, :], bank[5 + g][:, i * DV:(i + 1) * DV],
                                        head_rstd[:, h % 2, t:t + 1], None, ALU.mult).then_inc(hsn_done, 1)

                def head_logits(h):
                    if h >= 2:
                        dve.wait_ge(kt_ready, 2 * (h - 1))
                    for d in range(2):
                        logits(h, d, (3 * d, 3 * d + 1), [ke[:, h % 2, d, hs] for hs in halves])

                head_logits(1)
                for d in range(2):
                    dve.wait_ge(e_ready, 3 * d + 3)
                    k_of_0 = ke[:, 0, d, :]
                    V.tensor_tensor(k_of_0, k_of_0, k_of[0], ALU.mult).then_inc(qk_ready, 1)
                for h in range(NH):
                    sl = (h + 1) % 2
                    more = h + 1 < NH
                    if h:
                        take_outputs(h - 1, 2)
                    if more:
                        log_gates(h + 1, 0, ke[:, sl, 0, :], qe[:, sl, 0, :], bsum[:, 0, :])
                    for g in range(2):
                        sum_directions(h, g)
                    if more:
                        pivots(h + 1, 0, bsum[:, 0, :])
                    states(h, 0)
                    if more:
                        log_gates(h + 1, 1, ke[:, sl, 1, :], qe[:, sl, 1, :], bsum[:, 1, :])
                    states(h, 1)
                    if more:
                        pivots(h + 1, 1, bsum[:, 1, :])
                    sum_directions(h, 2)
                    if h:
                        for g in range(4):
                            y_take(1, h - 1, g, TURN[g])
                    if h + 2 < NH:
                        head_logits(h + 2)
                    take_outputs(h, 0)
                    take_outputs(h, 1)
                take_outputs(NH - 1, 2)
                for g in range(4):
                    y_take(1, NH - 1, g, 4 + g)

            V.memset(ones[:, :], 1.0).then_inc(consts, 1)
            V.memset(eps_col[:, :], EPS).then_inc(consts, 1)
            dve.wait_ge(consts, 4)
            V.tensor_tensor(sel[:, :], ident[0:100, 0:36], ident[0:100, 64:100], ALU.add)
            dve.wait_ge(vec_t, 1)
            V.tensor_copy(vec[:, :], bank[7][:, 0:64]).then_inc(vec_ready, 1)
            dve.wait_ge(vec_ready, 1)
            for half in range(2):
                for c in range(KC):
                    j = 8 * half + c
                    dve.wait_ge(x_t, j + 1)
                    V.tensor_copy(xT[:, c, halves[half]], bank[j % 8][:, 0:HT]).then_inc(x_taken, 1)
                if half == 0:
                    split(0, 0)
                    for a in range(2):
                        dve.wait_ge(gw_hi, a + 1)
                        src = gate_raw[:, :, 8 * a:8 * a + 8].rearrange("p k (b r) -> p k b r", b=2)
                        hi = g_hi[:, :, :].rearrange("p k (b a r) -> p k b a r", b=2, a=2)[:, :, :, a, 0:4]
                        lo = g_lo[:, :, :].rearrange("p k (b a r) -> p k b a r", b=2, a=2)[:, :, :, a, 0:4]
                        V.tensor_tensor(lo, src, hi.bitcast(F32), ALU.subtract).then_inc(gw_lo, 1)
                    norm_half(0, 0)
            norm_half(0, 1)
            for L in range(2):
                q0 = PAIRS * L
                split(q0, 1)
                for half in range(2):
                    dve.wait_ge(gate_mm, 2 * L + half + 1)
                    if L == 0:
                        dve.wait_ge(bias_loaded, 64)
                        V.tensor_scalar(g_pre[0:100, halves[half]], bank[4 + half][0:100, 0:HT],
                                        gate_bias[0:100, 0:1], None, ALU.add).then_inc(gate_rows, 1)
                    else:
                        src, dst = bank[4 + half][:, 0:HT], rows_g[:, halves[half]]
                        V.tensor_copy(dst, src[0:96, :]).then_inc(rows_hi, 1)
                        dve.wait_ge(rows_hi, half + 3)
                        V.tensor_tensor(dst[64:96, :], src[64:96, :], dst[64:96, :].bitcast(F32), ALU.subtract
                                        ).then_inc(gate_rows, 1)
                split(q0 + 1, 0)
                split(q0 + 1, 1)
                split(q0 + 2, 0)
                if L == 0:
                    n = 0

                    def step(ins):
                        ins.then_inc(gate_dve, 1)

                    one = ones[0:36, 0:1]
                    dve.wait_ge(gate_act, 3)
                    step(V.scalar_tensor_tensor(out=g_log[0:36, :], in0=g_pre[64:100, :], scalar=0.0,
                                                in1=g_soft[64:100, :], op0=ALU.min, op1=ALU.subtract))
                    dve.wait_ge(gate_dve, 1)
                    for p in (slice(0, 36), slice(32, 36)):
                        for n_s, (a, b) in enumerate(((0, SEQS[0]), (SEQS[0], T))):
                            ts = slice(a, b) if p.start == 0 else slice(b - 1, a - 1 if a else None, -1)
                            step(V.tensor_tensor_scan(g_cum[p, ts], ones[p, 0:1].to_broadcast([p.stop - p.start, b - a]),
                                                      g_log[p, ts], 0.0, ALU.mult, ALU.add))
                        dve.wait_ge(gate_dve, 3 if p.start == 0 else 5)
                    dve.wait_ge(gw_zero, 1)
                    step(V.tensor_tensor(g_cols[0:36, :], g_pre[0:36, :], g_cum[0:36, :], ALU.subtract))
                    dve.wait_ge(gate_dve, 6)
                    for p in (slice(0, 36), slice(32, 36)):
                        for a, b in ((0, SEQS[0]), (SEQS[0], T)):
                            ts = slice(a, b) if p.start == 0 else slice(b - 1, a - 1 if a else None, -1)
                            step(V.tensor_tensor_scan(g_soft[p, ts], ones[p, 0:1].to_broadcast([p.stop - p.start, b - a]),
                                                      g_cols[p, ts], M_INIT, ALU.mult, ALU.max))
                        dve.wait_ge(gate_dve, 8 if p.start == 0 else 10)
                    step(V.tensor_tensor(g_log[0:36, :], g_cum[0:36, :], g_soft[0:36, :], ALU.add))
                    V.memset(rows_m[32:64, :].bitcast(mybir.dt.uint32), 0).then_inc(rows_hi, 1)
                    dve.wait_ge(rows_hi, 1)
                    V.tensor_copy(rows_m[0:36, :], g_soft[0:36, :]).then_inc(rows_hi, 1)
                    dve.wait_ge(rows_hi, 2)
                    V.tensor_tensor(rows_m[64:100, :], g_soft[0:36, :], rows_m[0:36, :].bitcast(F32), ALU.subtract)
                    V.memset(v_all[:, :, :, DV:DV + 1], 1.0).then_inc(v_ones, 1)
                def first_gates(d):
                    flat = ht[:, :, :].rearrange("p a n -> p (a n)")
                    log_gates(0, d, flat[:, 0:T], flat[:, T:2 * T], b0_sum[:, d, :])
                    pivots(0, d, b0_sum[:, d, :])

                if L == 1:
                    logits(0, 0, (3, 7), [ht[:, 0, :], ht[:, 1, :]])
                    first_gates(0)
                with dve.Fori(0, 2) as i:
                    split(i + q0 + PV_, 1)
                    split(i + q0 + PV_ + 1, 0)
                if L == 0:
                    dve.wait_ge(cols_t, 1)
                    for k in range(2):
                        V.tensor_copy(cols[:, 3 * k:3 * k + 3, :],
                                      bank[3 + 4 * k][:, 0:300].rearrange("p (t r) -> p t r", t=3)).then_inc(cols_ready, 1)
                else:
                    dve.wait_ge(scanned, TT)
                    logits(0, 1, (3, 7), [ht[:, 0, :], ht[:, 1, :]])
                    first_gates(1)
                with dve.Fori(0, 2) as i:
                    split(i + q0 + PO, 1)
                    split(i + q0 + PO + 1, 0)
                (gla if L else mlstm)()

                def last_pair(q, c, e, more):
                    split(q, 1)
                    for g in range(4):
                        add_residual(q, 0, g, c + g % 2)
                    if more:
                        split(q + 1, 0)
                    for g in range(3):
                        add_residual(q, 1, g, c + 2 + g % 2)
                    norm_half(e, 0)
                    add_residual(q, 1, 3, c + 3)
                    norm_half(e, 1)

                def pair(q, c):
                    split(q, 1)
                    for g in range(4):
                        add_residual(q, 0, g, c + g % 2)
                    split(q + 1, 0)
                    for g in range(4):
                        add_residual(q, 1, g, c + (2 + g % 2))

                pair(q0 + POUT, 0)
                last_pair(q0 + POUT + 1, 4, 2 * L + 1, True)
                for b, nb in enumerate(BLOCKS):
                    with dve.Fori(0, nb // 2) as i:
                        q = i + q0 + PGU[b]
                        f = i + (FFP * L + sum(BLOCKS[:b]) // 2)
                        split(q, 1)
                        split(q + 1, 0)
                        for g in range(4):
                            dve.wait_ge(mm_done, 8 * q + (4 + g + 1))
                            dve.wait_ge(taken[0], 4 * q + (g + 1))
                            dve.wait_ge(a_ready, 4 * f + (g + 1))
                            V.tensor_tensor(at[:, g, :], sg[:, g, :], bank[4 + g][:, 0:HT], ALU.mult
                                            ).then_inc(taken[1], 1)
                    if L == 0 and b == 0:
                        dve.wait_ge(gw_hi, 3)
                        src = gate_raw[:, :, :].rearrange("p k (b r) -> p k b r", b=1)
                        hi = g_hi[:, :, :].rearrange("p k (b r) -> p k b r", b=4)[:, :, 0:3, :]
                        lo = g_lo[:, :, :].rearrange("p k (b r) -> p k b r", b=4)[:, :, 0:3, :]
                        V.tensor_tensor(lo, src.to_broadcast([P, KC, 3, 2 * RANK]), hi.bitcast(F32), ALU.subtract
                                        ).then_inc(gw_lo, 1)
                    if L == 0 and b == 1:
                        dve.wait_ge(a2_split, 1)
                        w = w_a2[32:64, :, :]
                        V.tensor_tensor(w, w_a2_raw[32:64, :, :], w.bitcast(F32), ALU.subtract).then_inc(a2_split, 1)
                    if b < 2:
                        with dve.Fori(0, 2) as i:
                            pair(i + q0 + PDN[b], i * 4)
                    else:
                        pair(q0 + PDN[b], 0)
                        last_pair(q0 + PDN[b] + 1, 4, 2 * L + 2, L == 0)
            for t in range(TT):
                dve.wait_ge(fin_t, 2 * t + 2)
                V.tensor_copy(y_tok[:, t, 512:D], bank[5][:, :]).then_inc(fin_copied[1], 1)

        @block.gpsimd
        def _(pool):
            G = nc.gpsimd

            sq_steps = [1]

            def square(src, first, half, n):
                if first:
                    G.tensor_tensor(sq_sum[:, half, :], src, src, ALU.mult).then_inc(sq_acc, 1)
                    return
                pool.wait_ge(sq_acc, n)
                G.tensor_tensor(sq_new[:, :], src, src, ALU.mult).then_inc(sq_mul, 1)
                sq_steps[0] += 1
                pool.wait_ge(sq_mul, sq_steps[0])
                G.tensor_tensor(sq_sum[:, half, :], sq_sum[:, half, :], sq_new[:, :], ALU.add).then_inc(sq_acc, 1)

            def low(s, out, hi):
                pool.wait_ge(hi_ready, s + 1)
                G.tensor_tensor(out, ht[:, s % 4, :], hi.bitcast(F32), ALU.subtract).then_inc(lo_ready, 1)

            def norm_low(e, half):
                for c in range(KC if e < 4 else 0):
                    low(NORM_S[e] + 8 * half + c, h_lo[:, c, halves[half]], h_hi[:, c, halves[half]])

            def y_low(L, h, g):
                c, hs = 2 * h + g % 2, halves[g // 2]
                low(Y_S[L] + 4 * h + g, y_lo[c][:, hs], y_hi[c][:, hs])

            def squares(q, e):
                for n in range(16):
                    i, s, g = n // 8, n // 4 % 2, n % 4
                    c = 4 * i + 2 * s + g % 2
                    if n == 15:
                        norm_low(e, 0)
                    if c == 0:
                        pool.wait_ge(ss_done, 2 * (e - 1) + g // 2 + 1)
                    pool.wait_ge(taken[s], 4 * (q + i) + g + 1)
                    square(xT[:, c, halves[g // 2]], c == 0, g // 2, 16 * e + n)
                norm_low(e, 1)

            def causal(ap, d, tiles, done):
                sign = 1 if d == 0 else -1
                pat = [[sign, P]] if tiles == 1 else [[0, tiles], [sign, P]]
                G.affine_select(out=ap, in_=ap, pattern=pat, compare_op=ALU.is_ge, fill=0.0, base=0,
                                channel_multiplier=-sign).then_inc(done, 1)

            def mlstm():
                def masks(h, piece):
                    for k, (d, j) in enumerate(PIECES[piece]):
                        pool.wait_ge(exp_done, 12 * h + 4 * piece + k + 1)
                        c = OFF[d, j] + (0 if d == 0 else span(d, j)[1] - P)
                        causal(decay[:, h % 2, d, c:c + P], d, 1, mask_done)

                for piece in range(3):
                    masks(0, piece)
                for h in range(NH):
                    if h + 1 < NH:
                        masks(h + 1, 0)
                        masks(h + 1, 1)
                    if h:
                        y_low(0, h - 1, 0)
                        y_low(0, h - 1, 1)
                    if h + 1 < NH:
                        masks(h + 1, 2)
                    if h:
                        y_low(0, h - 1, 2)
                        y_low(0, h - 1, 3)
                for g in range(4):
                    y_low(0, NH - 1, g)

            def gla():
                def scale_qk(h, d):
                    for i, (part, of) in enumerate(((qe, q_of), (ke, k_of))[:2 if h else 1]):
                        pool.wait_ge(e_ready, 6 * h + 3 * d + i + 2)
                        p = part[:, h % 2, d, :]
                        G.tensor_tensor(p, p, of[h], ALU.mult).then_inc(qk_ready, 1)

                def masks(h, g):
                    n = 3 * h + g
                    pool.wait_ge(a_taken, n + 1)
                    for d in range(2):
                        causal(a_sb[:, g, :, d, :], d, 2, a_masked)

                for d in range(2):
                    scale_qk(0, d)
                for h in range(NH):
                    for g in range(3):
                        masks(h, g)
                    if h + 1 < NH:
                        scale_qk(h + 1, 0)
                        scale_qk(h + 1, 1)
                    if h:
                        for g in range(4):
                            y_low(1, h - 1, g)
                for g in range(4):
                    y_low(1, NH - 1, g)

            G.memset(ident[:, :], 0.0).then_inc(sq_mul, 1)
            pool.wait_ge(sq_mul, 1)
            G.affine_select(out=ident[:, :], in_=ident[:, :], compare_op=ALU.not_equal, fill=1.0, base=0,
                            pattern=[[-1, P]], channel_multiplier=1).then_inc(consts, 1)
            G.memset(gate_bias[:, :], 0.0).then_inc(consts, 1)
            G.memset(den[:, :], 0.0).then_inc(a_ready, 4)
            G.memset(g_cols[:, :], 0.0)
            G.memset(g_hi[:, :, :].bitcast(mybir.dt.uint32), 0)
            G.memset(g_lo[:, :, :].bitcast(mybir.dt.uint32), 0).then_inc(gw_zero, 1)
            for half in range(2):
                for c in range(KC):
                    n = 8 * half + c
                    pool.wait_ge(x_taken, n + 1)
                    square(xT[:, c, halves[half]], c == 0, half, n)
                norm_low(0, half)
            for L in range(2):
                q0 = PAIRS * L
                (gla if L else mlstm)()
                squares(q0 + POUT, 2 * L + 1)
                for b, nb in enumerate(BLOCKS):
                    with pool.Fori(0, nb // 2) as i:
                        q = i + q0 + PGU[b]
                        f = i + (FFP * L + sum(BLOCKS[:b]) // 2)
                        for g in range(4):
                            c = bass.ds(i * 2 + g % 2, 1)
                            hs = halves[g // 2]
                            src = at[:, g:g + 1, :]
                            pool.wait_ge(taken[1], 4 * q + (g + 1))
                            G.tensor_copy(a_hi[:, c, hs], src).then_inc(a_hi_done, 1)
                            pool.wait_ge(a_hi_done, 4 * f + (g + 1))
                            G.tensor_tensor(a_lo[:, c, hs], src, a_hi[:, c, hs].bitcast(F32),
                                            ALU.subtract).then_inc(a_ready, 1)
                    if L == 0 and b == 0:
                        G.memset(g_hi[:, :, :].bitcast(mybir.dt.uint32), 0)
                        G.memset(g_lo[:, :, :].bitcast(mybir.dt.uint32), 0).then_inc(gw_zero, 1)
                        G.memset(w_a2_raw[:, :, :], 0.0).then_inc(a2_zero, 1)
                squares(q0 + PDN[2], 2 * L + 2)


_INS = ["x_prompt", "x_sample", "norm_mix_g", "norm_ffn_g", "norm_final_g", "mlstm_w_in", "mlstm_b_gate",
        "mlstm_head_g", "mlstm_w_out", "gla_w_in", "gla_w_a2", "gla_b_a", "gla_head_g", "gla_w_out",
        "ffn_w_gu", "ffn_w_down"]
_OUTS = [(1, SEQS[0], D), (1, SEQS[1], D)]


def kernel(**inputs):
    import numpy as _np
    import concourse.bacc as _bacc
    from concourse.bass_utils import run_bass_kernel_spmd as _run

    nc = _bacc.Bacc("TRN2", target_bir_lowering=False, num_devices=1, dynamic_dma_scratch_size=1024)
    arrays, args = {}, []
    for name in _INS:
        a = _np.ascontiguousarray(inputs[name])
        arrays[f"in_{name}_dram"] = a
        args.append(nc.dram_tensor(f"in_{name}_dram", a.shape, mybir.dt.from_np(a.dtype), kind="ExternalInput").ap())
    for i, shape in enumerate(_OUTS):
        args.append(nc.dram_tensor(f"out_{i}_dram", shape, F32, kind="ExternalOutput").ap())
    build(nc, *args)
    r = _run(nc, [arrays], core_ids=[0])
    return tuple(r.results[0][f"out_{i}_dram"] for i in range(len(_OUTS)))
```

```python
from contextlib import ExitStack

import concourse.bass as bass
from concourse import mybir

F32 = mybir.dt.float32
F32R = mybir.dt.float32r
ALU = mybir.AluOpType
ACT = mybir.ActivationFunctionType

P = 128
SEQS = (512, 256)
T = sum(SEQS)
HT = T // 2
TT = T // P
D = 1024
KC = D // P
NH = 4
DK = 128
DV = 256
QK = NH * DK
DFF = 2816
W = 256
EPS = 1e-6
M_INIT = -1e30
GLA_TAU = 16.0
RANK = 16
PIVOT = P // 2 - 1
BLOCKS = (8, 8, 6)
PAIRS = 25
PQ, PK, PVAL, PO, POUT = 0, 1, 2, 4, 6
PGU, PDN = (8, 14, 20), (12, 18, 23)
FFP = sum(BLOCKS) // 2
X_BANK = [(1, 2, 3, 4, 5, 6, 7, 1), (5, 6, 7, 2, 3, 5, 6, 7)]
NORM_S = (0, 32, 48, 80)
Y_S = (16, 64)
FIRST_T = (0, 0, 0, 0, 4, 4)
LAST_T = (3, 3, 3, 3, 5, 5)
OUTS = [(0, 0), (0, 1), (0, 2), (0, 3), (1, 3), (1, 2), (1, 1), (1, 0), (0, 4), (0, 5), (1, 5), (1, 4)]
TURN_AT, SCORES_AT = (4, 6), 7
OUT_BANKS = [b if b == 4 or h % 2 == 0 else 13 - b
             for h in range(NH) for b in (6, 7, 4, 6, 7, 4, 6, 7, 4, 6, 7, 6)]
PIECES = [[(0, j) for j in range(4)], [(1, j) for j in range(4)], [(0, 4), (0, 5), (1, 4), (1, 5)]]
UPD = ((0, 1, 2, 4), (3, 2, 1, 5))
TURN = (3, 2, 4, 7)


def span(d, j):
    if d == 0:
        return j * P, (LAST_T[j] + 1 - j) * P
    return FIRST_T[j] * P, (j + 1 - FIRST_T[j]) * P


def offsets():
    out, at = {}, [0, 0]
    for d in range(2):
        for j in range(TT):
            out[d, j] = at[d]
            at[d] += span(d, j)[1]
    assert at[0] == at[1]
    return out, at[0]


OFF, PW = offsets()


def build(nc, x_prompt, x_sample, norm_mix_g, norm_ffn_g, norm_final_g,
          mlstm_w_in, mlstm_b_gate, mlstm_head_g, mlstm_w_out,
          gla_w_in, gla_w_a2, gla_b_a, gla_head_g, gla_w_out,
          ffn_w_gu, ffn_w_down, y_prompt, y_sample):
    w_in = [w[0].rearrange("(k p) n -> p k n", p=P) for w in (mlstm_w_in, gla_w_in)]
    w_out = [w[0].rearrange("(k p) n -> p k n", p=P) for w in (mlstm_w_out, gla_w_out)]
    w_gu = [ffn_w_gu[i].rearrange("(k p) n -> p k n", p=P) for i in range(2)]
    w_dn = [ffn_w_down[i].rearrange("(k p) n -> p k n", p=P) for i in range(2)]

    with ExitStack() as ctx:
        def sb(name, shape, dt=F32, to=ctx):
            return to.enter_context(nc.sbuf_tensor(name, shape, dt))

        def sem(name):
            return ctx.enter_context(nc.semaphore(name))

        xT = sb("xT", [P, KC, T])
        raw = [sb(f"raw{s}", [P, KC, W]) for s in range(2)]
        w_hi = [sb(f"w_hi{s}", [P, KC, W], F32R) for s in range(2)]
        w_lo = [sb(f"w_lo{s}", [P, KC, W], F32R) for s in range(2)]
        ht = sb("ht", [P, 4, HT])
        with ExitStack() as r:
            hs_g1 = sb("hs_g1", [P, TT, DV], F32, r)
            junk = sb("junk", [P, DV], F32, r)
        with ExitStack() as r:
            b0_sum = sb("b0_sum", [P, 2, T], F32, r)
        rstd = sb("rstd", [P, 2, HT])
        sq_sum = sb("sq_sum", [P, 2, HT])
        sq_new = sb("sq_new", [P, HT])
        with ExitStack() as r:
            rows_g = sb("rows_g", [96, T], F32R, r)
        rows_m = sb("rows_m", [100, T], F32R)
        sel = sb("sel", [100, 36], F32R)
        ones = sb("ones", [P, P])
        ident = sb("ident", [P, P])
        with ExitStack() as r:
            vec_rows = sb("vec_rows", [64, P], F32, r)
            cols = sb("cols", [P, TT, 100], F32, r)
            gate_raw = sb("gate_raw", [P, KC, 2 * RANK], F32, r)
        w_a2 = sb("w_a2", [96, 2, QK], F32R)
        vec = sb("vec", [P, 64])
        gate_bias = sb("gate_bias", [P, 1])
        head_sq = sb("head_sq", [P, 2, TT])
        head_rstd = sb("head_rstd", [P, 2, TT])
        den = sb("den", [P, 2, 2])
        eps_col = sb("eps_col", [P, 1])
        x_sq = sb("x_sq", [P, TT])
        rms = sb("rms", [P, 2, TT])

        with ExitStack() as r:
            h_hi = sb("h_hi", [P, KC, T], F32R, r)
            h_lo = sb("h_lo", [P, KC, T], F32R, r)
        with ExitStack() as r:
            y_fin = sb("y_fin", [P, KC, T], F32, r)
            y_tok = sb("y_tok", [P, TT, D], F32, r)
        with ExitStack() as r:
            decay = sb("decay", [P, 2, 2, PW], F32, r)
            hs_m = sb("hs_m", [P, 2, TT, DV], F32, r)
        region_h = ctx.enter_context(ExitStack())
        qe = sb("qe", [P, 2, 2, T], F32, region_h)
        ke = sb("ke", [P, 2, 2, T], F32, region_h)
        bsum = sb("bsum", [P, 2, T], F32, region_h)
        k_tok = sb("k_tok", [P, 2, 4, P], F32, region_h)
        state = sb("state", [P, 2, DV], F32, region_h)
        s_piv = sb("s_piv", [P, 2, 4, DV], F32, region_h)
        hs_g = [sb("hs_g0", [P, TT, DV], F32, region_h), hs_g1]
        a_sb = sb("a_sb", [P, 3, 2, 2, P], F32, region_h)
        piv = sb("piv", [P, 2, TT], F32, region_h)
        step_log = sb("step_log", [P, 2, 2, TT - 1], F32, region_h)
        step_exp = sb("step_exp", [P, 2, TT - 1], F32, region_h)

        HR = 2 * T + TT * (DV + 1)
        with ExitStack() as r:
            xs = sb("xs", [P, TT, D], F32, r)
        with ExitStack() as r:
            y_parts = sb("y_parts", [P, NH, HR], F32R, r)
        with ExitStack() as r:
            a_hi = sb("a_hi", [P, 8, T], F32R, r)
            a_lo = sb("a_lo", [P, 8, T], F32R, r)
        qkv = sb("qkv", [P, NH, HR])

        with ExitStack() as r:
            g_hi = sb("g_hi", [P, KC, P], F32R, r)
            g_lo = sb("g_lo", [P, KC, P], F32R, r)
            with ExitStack() as r2:
                g_pre = sb("g_pre", [100, T], F32, r2)
                g_soft = sb("g_soft", [100, T], F32, r2)
                g_log = sb("g_log", [64, T], F32, r2)
                g_cum = sb("g_cum", [64, T], F32, r2)
                g_cols = sb("g_cols", [P, T], F32, r2)
            with ExitStack() as r2:
                sg = sb("sg", [P, 4, HT], F32, r2)
                at = sb("at", [P, 4, HT], F32, r2)
                w_a2_raw = sb("w_a2_raw", [96, 2, QK], F32, r2)
        o_gate = sb("o_gate", [P, KC, T])

        bank = [ctx.enter_context(nc.psum_tensor(f"bank{i}", [P, 512], F32)) for i in range(8)]

        q_of = [qkv[:, h, 0:T] for h in range(NH)]
        k_of = [qkv[:, h, T:2 * T] for h in range(NH)]
        v_all = qkv[:, :, 2 * T:HR].rearrange("p h (t n) -> p h t n", t=TT)
        y_hi = [y_parts[:, c // 2, (c % 2) * T:(c % 2 + 1) * T] for c in range(KC)]
        y_lo = [y_parts[:, c // 2, (2 + c % 2) * T:(3 + c % 2) * T] for c in range(KC)]
        gain = [vec[:, 8 * e:8 * e + 8] for e in range(5)]
        head_g = [vec[:, 40:48], vec[:, 48:56]]
        b_a = vec[:, 56:64]

        x_loaded = [sem(f"x_loaded{t}") for t in range(TT)]
        vec_loaded, bias_loaded, a2_loaded = sem("vec_loaded"), sem("bias_loaded"), sem("a2_loaded")
        gate_w_loaded = sem("gate_w_loaded")
        raw_loaded = [sem(f"raw_loaded{s}") for s in range(2)]
        y_stored = sem("y_stored")
        consts = sem("consts")
        vec_t, vec_ready = sem("vec_t"), sem("vec_ready")
        w_hi_ready, w_lo_ready = sem("w_hi_ready"), sem("w_lo_ready")
        mm_done = [sem(f"mm_done{s}") for s in range(2)]
        taken = [sem(f"taken{s}") for s in range(2)]
        x_t, x_taken = sem("x_t"), sem("x_taken")
        x_sq_done, x_diag = sem("x_sq_done"), sem("x_diag")
        sq_mul, sq_acc = sem("sq_mul"), sem("sq_acc")
        ss_done, ln_done, rstd_done = sem("ss_done"), sem("ln_done"), sem("rstd_done")
        ht_ready, hi_ready, lo_ready = sem("ht_ready"), sem("hi_ready"), sem("lo_ready")
        gw_zero, gw_hi, gw_lo = sem("gw_zero"), sem("gw_hi"), sem("gw_lo")
        gate_mm, gate_rows = sem("gate_mm"), sem("gate_rows")
        gate_act, gate_dve = sem("gate_act"), sem("gate_dve")
        cols_t, cols_ready = sem("cols_t"), sem("cols_ready")
        v_ones = sem("v_ones")
        a_hi_done, a_ready = sem("a_hi_done"), sem("a_ready")
        st_ready, cm_ready, exp_done, mask_done, p_ready = (
            sem("st_ready"), sem("cm_ready"), sem("exp_done"), sem("mask_done"), sem("p_ready"))
        pv_ready, den_step, fin_done = sem("pv_ready"), sem("den_step"), sem("fin_done")
        hsq_done, hln_done, hrstd_done, hsn_done, tr_ready = (
            sem("hsq_done"), sem("hln_done"), sem("hrstd_done"), sem("hsn_done"), sem("tr_ready"))
        z_ready, z_taken, z_abs, z_exp, z_ln, lg_ready = (
            sem("z_ready"), sem("z_taken"), sem("z_abs"), sem("z_exp"), sem("z_ln"), sem("lg_ready"))
        scanned, piv_ready, step_ready, centred, e_ready, qk_ready = (
            sem("scanned"), sem("piv_ready"), sem("step_ready"), sem("centred"), sem("e_ready"), sem("qk_ready"))
        a_mm, a_taken, a_masked, a_summed = sem("a_mm"), sem("a_taken"), sem("a_masked"), sem("a_summed")
        a2_zero, a2_split, rows_hi = sem("a2_zero"), sem("a2_split"), sem("rows_hi")
        kt_ready, kt_taken, u_ready, first_state, state_step = (
            sem("kt_ready"), sem("kt_taken"), sem("u_ready"), sem("first_state"), sem("state_step"))
        o_mm = sem("o_mm")
        fin_scaled, last_sq, tok_sum, rms_done, rms_inv, fin_t = (
            sem("fin_scaled"), sem("last_sq"), sem("tok_sum"), sem("rms_done"), sem("rms_inv"), sem("fin_t"))
        fin_copied = [sem(f"fin_copied{i}") for i in range(2)]

        halves = [slice(0, HT), slice(HT, T)]
        block = ctx.enter_context(nc.Block())

        @block.sync
        def _(sp):
            def load_x(t):
                src = x_prompt[0, t * P:(t + 1) * P, :] if t < 4 else x_sample[0, (t - 4) * P:(t - 3) * P, :]
                sp.dma_start(xs[:, t, :], src).then_inc(x_loaded[t], 16)

            load_x(0)
            load_x(1)
            load_x(2)
            srcs = [norm_mix_g[0], norm_ffn_g[0], norm_mix_g[1], norm_ffn_g[1], norm_final_g,
                    mlstm_head_g[0], gla_head_g[0]]
            for i, src in enumerate(srcs):
                sp.dma_start(vec_rows[8 * i:8 * i + 8, :], src.rearrange("(c p) -> c p", p=P)).then_inc(vec_loaded, 16)
            sp.dma_start(vec_rows[56:64, :], gla_b_a[0].rearrange("d (h p) -> (d h) p", p=P)).then_inc(vec_loaded, 16)

            def load_w(q, s, src, wait=True):
                if wait:
                    sp.wait_ge(w_lo_ready, 2 * q + s - 1)
                sp.dma_start(raw[s][:, 0:src.shape[1], :], src).then_inc(raw_loaded[s], 16)

            sp.dma_start(gate_raw[:, :, 0:16], w_in[0][:, :, 3072:3088]).then_inc(gate_w_loaded, 16)
            load_w(0, 0, w_in[0][:, :, 0:W], wait=False)
            load_x(3)
            load_x(4)
            load_x(5)
            load_w(0, 1, w_in[0][:, :, W:2 * W], wait=False)
            sp.wait_ge(consts, 4)
            for at_p, c in ((0, 0), (32, 8), (64, 4), (96, 12)):
                sp.dma_start(gate_bias[at_p:at_p + 4, :],
                             mlstm_b_gate[0, c:c + 4].rearrange("(p a) -> p a", a=1)).then_inc(bias_loaded, 16)

            for L in range(2):
                q0 = PAIRS * L
                with sp.Fori(1 - L, 6) as i:
                    for s in range(2):
                        load_w(i + q0, s, w_in[L][:, :, bass.ds(i * (2 * W) + s * W, W)])
                with sp.Fori(0, 2) as i:
                    for s in range(2):
                        load_w(i + q0 + POUT, s, w_out[L][:, :, bass.ds(i * (2 * W) + s * W, W)])
                if L == 0:
                    sp.wait_ge(gw_lo, 2)
                    sp.dma_start(gate_raw[:, :, :], w_in[1][:, :, 3072:3104]).then_inc(gate_w_loaded, 16)
                for b, nb in enumerate(BLOCKS):
                    c0 = sum(BLOCKS[:b])
                    with sp.Fori(0, nb // 2) as i:
                        for s in range(2):
                            load_w(i + q0 + PGU[b], s, w_gu[L][:, :, bass.ds(i * W + (s * DFF + c0 * P), W)])
                    with sp.Fori(0, 2) as i:
                        for s in range(2):
                            load_w(i + q0 + PDN[b], s, w_dn[L][:, c0:c0 + nb, bass.ds(i * (2 * W) + s * W, W)])
                    if L == 0 and b == 0:
                        sp.wait_ge(a2_zero, 1)
                        for k in range(3):
                            for d in range(2):
                                p0 = 32 * k + RANK * d
                                sp.dma_start(w_a2_raw[p0:p0 + RANK, d, :], gla_w_a2[0, d]).then_inc(a2_loaded, 16)

            for t in range(TT):
                for hf in range(2):
                    sp.wait_ge(fin_copied[hf], t + 1)
                dst = y_prompt[0, t * P:(t + 1) * P, :] if t < 4 else y_sample[0, (t - 4) * P:(t - 3) * P, :]
                sp.dma_start(dst, y_tok[:, t, :]).then_inc(y_stored, 16)
            sp.wait_ge(y_stored, 16 * TT)

        @block.tensor
        def _(pe):
            def mm(out, lhsT, rhs, start, stop):
                return nc.tensor.matmul(out, lhsT, rhs, start=start, stop=stop)

            def side_by_side(groups, parts, half, kdim, before=None, k_from=0, k_end=True):
                r_hi, r_lo = parts
                lasts = []
                for k in range(k_from, kdim):
                    if before is not None:
                        before(k)
                    r0, r1 = r_hi(k)[:, halves[half]], r_lo(k)[:, halves[half]]
                    end = k == kdim - 1 and k_end
                    for out, wh, wl in groups:
                        mm(out, wh(k), r0, k == 0, False)
                        mm(out, wh(k), r1, False, False)
                        last = mm(out, wl(k), r0, False, end)
                        if end:
                            lasts.append(last)
                return lasts

            h_of = (lambda k: h_hi[:, k, :]), (lambda k: h_lo[:, k, :])
            y_of = (lambda k: y_hi[k]), (lambda k: y_lo[k])
            a_of = (lambda k: a_hi[:, k, :]), (lambda k: a_lo[:, k, :])

            def tile_begin(q, s):
                pe.wait_ge(w_lo_ready, 2 * q + s + 1)
                pe.wait_ge(taken[s], 4 * q)

            def of_tile(s, g):
                cs = slice(g % 2 * P, (g % 2 + 1) * P)
                return bank[4 * s + g][:, 0:HT], lambda k: w_hi[s][:, k, cs], lambda k: w_lo[s][:, k, cs]

            def tile_group(s, g, parts, kdim, before=None):
                last, = side_by_side([of_tile(s, g)], parts, g // 2, kdim, before)
                last.then_inc(mm_done[s], 1)

            def tile_seq(q, s, parts, kdim, before=(None,) * 4, hook=None):
                hook = hook or {}
                tile_begin(q, s)
                for g in range(4):
                    tile_group(s, g, parts, kdim, before[g])
                    if g in hook:
                        hook[g]()

            def sum_squares(e, half):
                if e == 0:
                    pe.wait_ge(x_diag, 3 * (half + 1))
                else:
                    pe.wait_ge(sq_acc, 16 * e - 2 + 2 * half)
                mm(bank[3 * half][:, 0:HT], ones[:, :], sq_sum[:, half, :], True, True).then_inc(ss_done, 1)

            def parts_of(e, half):
                def before(k):
                    pe.wait_ge(lo_ready, NORM_S[e] + 8 * half + k + 1)
                return before

            pe.wait_ge(consts, 4)
            pe.wait_ge(vec_loaded, 16 * 8)
            nc.tensor.transpose(bank[7][:, 0:64], vec_rows[:, :], ident[0:64, 0:64]).then_inc(vec_t, 1)

            def x_chunks(half):
                for t in range(3):
                    pe.wait_ge(x_loaded[3 * half + t], 16)
                for c in range(KC):
                    j = 8 * half + c
                    if j == 6:
                        pe.wait_ge(vec_ready, 1)
                    if j == 7:
                        pe.wait_ge(x_taken, 1)
                    if half:
                        pe.wait_ge(x_taken, max(8, j - 4))
                    for t in range(3):
                        last = nc.tensor.transpose(bank[X_BANK[half][c]][:, t * P:(t + 1) * P],
                                                   xs[:, 3 * half + t, c * P:(c + 1) * P], ident[:, :])
                    last.then_inc(x_t, 1)
                    if j == 3:
                        sum_squares(0, 0)

            x_chunks(0)
            x_chunks(1)

            def mlstm(q0):
                q1 = q0 + POUT
                pe.wait_ge(taken[0], 4 * q1)
                pe.wait_ge(taken[1], 4 * q1 - 2)

                def scores(h, tiles):
                    if h and tiles[0] == 0:
                        pe.wait_ge(p_ready, 12 * (h - 1) + 8)
                        if h >= 2:
                            pe.wait_ge(ht_ready, Y_S[0] + 4 * (h - 1))
                    if h and tiles[0] == 4:
                        pe.wait_ge(fin_done, 12 * (h - 1) + 9)
                    for j in tiles:
                        first, last_t = FIRST_T[j] * P, (LAST_T[j] + 1) * P
                        out = bank[j][:, :] if j < 4 else bank[4][:, (j - 4) * 256:(j - 3) * 256]
                        mm(out, k_of[h][:, j * P:(j + 1) * P], q_of[h][:, first:last_t], True, True
                           ).then_inc(st_ready, 1)

                def maxima(h, piece):
                    n = 3 * h + piece
                    if n:
                        pe.wait_ge(exp_done, 4 * n)
                    for d, cs, at_c in ([(0, slice(0, 512), 0)], [(1, slice(0, 512), 0)],
                                        [(0, slice(512, T), 0), (1, slice(512, T), 256)])[piece]:
                        r = 32 * d + h
                        last = mm(bank[5][:, at_c:at_c + cs.stop - cs.start],
                                  sel[:, r:r + 1].to_broadcast([100, P]), rows_m[:, cs], True, True)
                    last.then_inc(cm_ready, 1)

                def output(h, i):
                    d, t = OUTS[i]
                    n = 12 * h + i
                    b = OUT_BANKS[n]
                    if b in OUT_BANKS[:n]:
                        before = max(m for m in range(n) if OUT_BANKS[m] == b)
                        pe.wait_ge(fin_done, before + 1)
                    pe.wait_ge(p_ready, 12 * h + (t + 1 if i < 4 else 8 if i < 8 else 12))
                    if b == 4:
                        pe.wait_ge(p_ready, 12 * (h + 1))
                    js = range(FIRST_T[t], t + 1) if d == 0 else range(t, LAST_T[t] + 1)
                    for j in js:
                        at_c = OFF[d, j] + t * P - span(d, j)[0]
                        last = mm(bank[b][:, 0:DV + 1], decay[:, h % 2, d, at_c:at_c + P],
                                  v_all[:, h, j, :], j == js[0], j == js[-1])
                    last.then_inc(pv_ready, 1)

                def turn(h, g, b):
                    half, cc = g // 2, g % 2
                    pe.wait_ge(hsn_done, TT * (h + 1))
                    for t in range(3):
                        last = nc.tensor.transpose(bank[b][:, t * P:(t + 1) * P],
                                                   hs_m[:, h % 2, 3 * half + t, cc * P:(cc + 1) * P], ident[:, :])
                    last.then_inc(tr_ready, 1)

                pe.wait_ge(v_ones, 1)
                maxima(0, 0)
                scores(0, range(4))
                maxima(0, 1)
                scores(0, (4, 5))
                maxima(0, 2)
                pe.wait_ge(taken[1], 4 * q1)
                for h in range(NH):
                    for i in range(12):
                        output(h, i)
                        if h + 1 < NH and i % 4 == 0:
                            maxima(h + 1, i // 4)
                        if h and i in TURN_AT:
                            pe.wait_ge(p_ready, 12 * h + 8)
                            for g in range(2):
                                turn(h - 1, 2 * TURN_AT.index(i) + g, 2 * TURN_AT.index(i) + g)
                        if h + 1 < NH and i == SCORES_AT:
                            scores(h + 1, range(4))
                    if h + 1 < NH:
                        scores(h + 1, (4, 5))
                pe.wait_ge(ht_ready, Y_S[0] + 4 * (NH - 1))
                return lambda g: turn(NH - 1, g, 4 + g)

            def logit(h, d, half, b):
                mm(bank[b][:, 0:HT], w_a2[:, d, h * DK:(h + 1) * DK], rows_g[:, halves[half]], True, True
                   ).then_inc(z_ready, 1)

            def gla(q0):
                q1 = q0 + POUT
                pe.wait_ge(taken[0], 4 * q1)
                pe.wait_ge(taken[1], 4 * q1 - 3)

                def gate_logits(h):
                    if h >= 2:
                        pe.wait_ge(state_step, 8 * (h - 1))
                        pe.wait_ge(a_taken, 3 * (h - 1))
                        pe.wait_ge(kt_taken, 2 * (h - 1))
                        if h >= 3:
                            pe.wait_ge(ht_ready, Y_S[1] + 4 * (h - 2))
                    for d in range(2):
                        for half in range(2):
                            logit(h, d, half, 3 * d + half)

                def chunk_scores(h, g):
                    if g < 2 and h >= 2:
                        pe.wait_ge(ht_ready, Y_S[1] + 4 * (h - 2) + 2)
                    if g == 0 and h:
                        pe.wait_ge(a_taken, 3 * h)
                    if g == 1:
                        pe.wait_ge(z_taken, 4 * min(h + 2, NH))
                    if g == 2:
                        pe.wait_ge(a_taken, 3 * h + 1)
                    for i in range(2):
                        for d in range(2):
                            ts = slice((2 * g + i) * P, (2 * g + i + 1) * P)
                            last = mm(bank[2 + g % 2][:, (2 * i + d) * P:(2 * i + d + 1) * P],
                                      ke[:, h % 2, d, ts], qe[:, h % 2, d, ts], True, True)
                    last.then_inc(a_mm, 1)

                def keys_by_token(h, d):
                    if d == 0:
                        pe.wait_ge(z_taken, 4 * min(h + 2, NH))
                        if h >= 2:
                            pe.wait_ge(ht_ready, Y_S[1] + 4 * (h - 2) + 3)
                    if d == 1 and h:
                        pe.wait_ge(hsn_done, TT * (NH + h))
                    for i, t in enumerate(UPD[d]):
                        last = nc.tensor.transpose(bank[4 + 3 * d][:, i * P:(i + 1) * P],
                                                   ke[:, h % 2, d, t * P:(t + 1) * P], ident[:, :])
                    last.then_inc(kt_ready, 1)

                def updates(h, d):
                    pe.wait_ge(kt_taken, 2 * h + d + 1)
                    if d == 0 and h:
                        pe.wait_ge(hsn_done, TT * (NH + h - 1) + 4)
                    if d == 1:
                        pe.wait_ge(z_taken, 4 * min(h + 2, NH))
                        pe.wait_ge(state_step, 8 * h)
                    for i, t in enumerate(UPD[d]):
                        last = mm(bank[5 - 5 * d + i // 2][:, (i % 2) * DV:(i % 2 + 1) * DV], k_tok[:, d, i, :],
                                  v_all[:, h, t, 0:DV], True, True)
                        if i % 2:
                            last.then_inc(u_ready, 1)

                def outputs(h, g):
                    n = 3 * h + g
                    pe.wait_ge(a_summed, n + 1)
                    if g == 0:
                        pe.wait_ge(state_step, 8 * (h + 1))
                    if g == 2 and h:
                        pe.wait_ge(ht_ready, Y_S[1] + 4 * h)
                    for i in range(2):
                        t = 2 * g + i
                        ts = slice(t * P, (t + 1) * P)
                        ops = [(a_sb[:, g, i, 0, :], v_all[:, h, t, 0:DV])]
                        if t != FIRST_T[t]:
                            ops.append((qe[:, h % 2, 0, ts], s_piv[:, 0, UPD[0].index(t - 1), :]))
                        if t != LAST_T[t]:
                            ops.append((qe[:, h % 2, 1, ts], s_piv[:, 1, UPD[1].index(t + 1), :]))
                        for k, (a, b_) in enumerate(ops):
                            last = mm(bank[5 + g][:, i * DV:(i + 1) * DV], a, b_, k == 0, k == len(ops) - 1)
                    last.then_inc(o_mm, 1)

                def turn(h, g, b):
                    half, cc = g // 2, g % 2
                    pe.wait_ge(hsn_done, TT * (NH + h) + 3 * (half + 1))
                    for t in range(3):
                        last = nc.tensor.transpose(bank[b][:, t * P:(t + 1) * P],
                                                   hs_g[h % 2][:, 3 * half + t, cc * P:(cc + 1) * P], ident[:, :])
                    last.then_inc(tr_ready, 1)

                gate_logits(1)
                pe.wait_ge(taken[1], 4 * q1)
                for h in range(NH):
                    pe.wait_ge(qk_ready, 4 * (h + 1))
                    chunk_scores(h, 0)
                    chunk_scores(h, 1)
                    for d in range(2):
                        keys_by_token(h, d)
                    chunk_scores(h, 2)
                    if h:
                        pe.wait_ge(a_taken, 3 * h + 2)
                        turn(h - 1, 0, 3)
                    for d in range(2):
                        updates(h, d)
                    if h:
                        pe.wait_ge(a_taken, 3 * h + 3)
                        pe.wait_ge(kt_taken, 2 * h + 2)
                        for g in range(1, 4):
                            turn(h - 1, g, TURN[g])
                    outputs(h, 0)
                    outputs(h, 1)
                    if h + 2 < NH:
                        gate_logits(h + 2)
                    outputs(h, 2)
                pe.wait_ge(a_taken, 3 * NH)
                return lambda g: turn(NH - 1, g, 4 + g)

            for L in range(2):
                q0 = PAIRS * L
                e = 2 * L
                pe.wait_ge(gw_lo, L + 2)

                def gates_and(half, gs=()):
                    gates = (bank[4 + half][:, 0:HT], lambda k: g_hi[:, k, :], lambda k: g_lo[:, k, :])
                    of_half = parts_of(e, half)

                    def before(k):
                        if L == 0 and half == 0 and k == 2:
                            pe.wait_ge(x_taken, 13)
                            sum_squares(0, 1)
                        of_half(k)

                    lasts = side_by_side([gates] + [of_tile(0, g) for g in gs], h_of, half, KC, before)
                    lasts[0].then_inc(gate_mm, 1)
                    for last in lasts[1:]:
                        last.then_inc(mm_done[0], 1)

                tile_begin(q0, 0)
                if L == 0:
                    pe.wait_ge(x_taken, 8)
                    pe.wait_ge(ln_done, 1)
                gates_and(0, (0, 1))
                if L == 1:
                    sum_squares(e, 1)
                tile_begin(q0, 1)
                pe.wait_ge(gate_rows, 2 * L + 1)
                tile_group(1, 0, h_of, KC)
                if L == 0:
                    pe.wait_ge(x_taken, 16)
                    pe.wait_ge(ln_done, 2)
                gates_and(1, (2, 3))
                pe.wait_ge(gate_rows, 2 * L + 2)
                for g in range(1, 4):
                    tile_group(1, g, h_of, KC)
                for s in range(2):
                    tile_seq(q0 + PK, s, h_of, KC)
                if L == 1:
                    pe.wait_ge(a2_split, 2)
                    pe.wait_ge(taken[0], 4 * (q0 + PK) + 4)
                    logit(0, 0, 0, 3)
                    pe.wait_ge(taken[1], 4 * (q0 + PK) + 4)
                    logit(0, 0, 1, 7)
                with pe.Fori(0, 2) as i:
                    for s in range(2):
                        tile_begin(i + q0 + PVAL, s)
                        for t in range(TT):
                            out = bank[4 * s + t // 2][:, (t % 2) * W:(t % 2 + 1) * W]
                            ts = slice(t * P, (t + 1) * P)
                            for k in range(KC):
                                mm(out, h_hi[:, k, ts], w_hi[s][:, k, :], k == 0, False)
                                mm(out, h_lo[:, k, ts], w_hi[s][:, k, :], False, False)
                                last = mm(out, h_hi[:, k, ts], w_lo[s][:, k, :], False, k == KC - 1)
                            if t % 2 == 1:
                                last.then_inc(mm_done[s], 2 if t == TT - 1 else 1)
                if L == 0:
                    pe.wait_ge(gate_act, 4)
                    for t in range(TT):
                        last = nc.tensor.transpose(bank[3 + 4 * (t // 3)][:, (t % 3) * 100:(t % 3 + 1) * 100],
                                                   g_cols[0:100, t * P:(t + 1) * P], ident[0:100, 0:100])
                    last.then_inc(cols_t, 1)
                    pe.wait_ge(cols_ready, 2)
                else:
                    for half in range(2):
                        pe.wait_ge(z_taken, half + 1)
                        logit(0, 1, half, 3 + 4 * half)
                    pe.wait_ge(z_taken, 4)
                with pe.Fori(0, 2) as i:
                    for s in range(2):
                        tile_seq(i + q0 + PO, s, h_of, KC)
                last_turn = (mlstm if L == 0 else gla)(q0)

                def y_before(half):
                    def before(k):
                        pe.wait_ge(lo_ready, Y_S[L] + 4 * (k // 2) + 2 * half + k % 2 + 1)
                    return before

                q = q0 + POUT
                tile_begin(q, 0)
                for k0, k1 in ((0, KC - 2), (KC - 2, KC)):
                    for g in range(4):
                        if k0 == 0 and g >= 2:
                            last_turn(2 * g - 4)
                            last_turn(2 * g - 3)
                        lasts = side_by_side([of_tile(0, g)], y_of, g // 2, k1, y_before(g // 2), k0, k1 == KC)
                        for last in lasts:
                            last.then_inc(mm_done[0], 1)
                pe.wait_ge(ht_ready, Y_S[L] + 4 * NH)
                tile_seq(q, 1, y_of, KC)

                def first_sum(q, e):
                    pe.wait_ge(taken[0], 4 * (q + 1))
                    sum_squares(e, 0)

                tile_seq(q + 1, 0, y_of, KC)
                tile_seq(q + 1, 1, y_of, KC, hook={2: lambda: first_sum(q + 1, e + 1)})

                for b, nb in enumerate(BLOCKS):
                    n_pairs = nb // 2
                    start = 0
                    if b == 0:
                        q = q0 + PGU[0]
                        for half in range(2):
                            for s in range(2):
                                if half == 0:
                                    tile_begin(q, s)
                                gs = (2 * half, 2 * half + 1)
                                if s == 0:
                                    for last in side_by_side([of_tile(0, g) for g in gs], h_of, half, KC,
                                                             parts_of(e + 1, half)):
                                        last.then_inc(mm_done[0], 1)
                                else:
                                    tile_group(1, gs[0], h_of, KC)
                                    if half == 0:
                                        sum_squares(e + 1, 1)
                                    tile_group(1, gs[1], h_of, KC)
                        start = 1
                    with pe.Fori(start, n_pairs) as i:
                        for s in range(2):
                            tile_seq(i + q0 + PGU[b], s, h_of, KC)

                    f0 = 4 * (FFP * L + sum(BLOCKS[:b]) // 2) + 4

                    def a_before(half):
                        def before(k):
                            pe.wait_ge(a_ready, f0 + 4 * (k // 2) + 2 * half + k % 2 + 1)
                        return before

                    q = q0 + PDN[b]
                    if b < 2:
                        with pe.Fori(0, 2) as i:
                            pe.wait_ge(a_ready, f0 + 4 * n_pairs - 3)
                            tile_seq(i + q, 0, a_of, nb, (a_before(0), None, a_before(1), None))
                            tile_seq(i + q, 1, a_of, nb)
                    else:
                        tile_seq(q, 0, a_of, nb, (a_before(0), None, a_before(1), None))
                        tile_seq(q, 1, a_of, nb)
                        tile_seq(q + 1, 0, a_of, nb)
                        if L == 0:
                            tile_seq(q + 1, 1, a_of, nb, hook={2: lambda: first_sum(q + 1, e + 2)})
                        else:
                            tile_seq(q + 1, 1, a_of, nb)

            pe.wait_ge(taken[0], 8 * PAIRS)
            for half in range(2):
                pe.wait_ge(sq_acc, 62 + half)
                if half == 1:
                    pe.wait_ge(last_sq, 1)
                for t in range(3 * half, 3 * half + 3):
                    ts = slice((t - 3 * half) * P, (t - 3 * half + 1) * P)
                    out = bank[0 if half == 0 else 5][:, t:t + 1]
                    last = mm(out, sq_sum[:, half, ts], ones[:, 0:1], True, half == 0)
                    if half == 1:
                        last = mm(out, sq_new[:, ts], ones[:, 0:1], False, True)
                last.then_inc(tok_sum, 1)
                for t in range(3 * half, 3 * half + 3):
                    for hf in range(2):
                        n = 2 * t + hf
                        pe.wait_ge(fin_scaled, 12 + half * 2 + 2 if hf else 12)
                        if n == 3:
                            pe.wait_ge(taken[1], 8 * PAIRS)
                        if n >= 4:
                            pe.wait_ge(fin_copied[n % 2], (n - 4) // 2 + 1)
                        for c in range(4):
                            last = nc.tensor.transpose(bank[1 + n % 4][:, c * P:(c + 1) * P],
                                                       y_fin[:, 4 * hf + c, t * P:(t + 1) * P], ident[:, :])
                        last.then_inc(fin_t, 1)

        @block.scalar
        def _(act):
            def split(q, s, wait=True):
                act.wait_ge(raw_loaded[s], 16 * (q + 1))
                if wait:
                    act.wait_ge(mm_done[s], 4 * q)
                nc.scalar.copy(w_hi[s][:, :, :], raw[s][:, :, :]).then_inc(w_hi_ready, 1)

            def high(s, out):
                act.wait_ge(ht_ready, s + 1)
                nc.scalar.copy(out, ht[:, s % 4, :]).then_inc(hi_ready, 1)

            def log_exp_table():
                nc.scalar.preload_act_table_set("natural_log_exp_and_others")

            def norm_rstd(e, half):
                act.wait_ge(ss_done, 2 * e + half + 1)
                nc.scalar.activation(rstd[:, half, :], bank[3 * half][:, 0:HT], ACT.Ln,
                                     bias=eps_col[:, 0:1], scale=1.0 / D).then_inc(ln_done, 1)
                act.wait_ge(ln_done, 2 * e + half + 1)
                nc.scalar.activation(rstd[:, half, :], rstd[:, half, :], ACT.Exp, scale=-0.5).then_inc(rstd_done, 1)

            def norm_high(e, half, chunks=range(KC)):
                for c in chunks:
                    high(NORM_S[e] + 8 * half + c, h_hi[:, c, halves[half]])

            def norm(e, q):
                norm_rstd(e, 0)
                norm_high(e, 0)
                split(q, 1)
                norm_rstd(e, 1)
                norm_high(e, 1)

            def y_high(L, h, g):
                high(Y_S[L] + 4 * h + g, y_hi[2 * h + g % 2][:, halves[g // 2]])

            def take(q, s, g):
                act.wait_ge(mm_done[s], 4 * q + (g + 1))
                return bank[4 * s + g][:, 0:HT]

            def head_norm(h, hs, order, taken):
                for n, t in enumerate(order):
                    taken(t)
                    if n:
                        act.wait_ge(hsq_done, TT * h + n)
                    nc.scalar.activation(junk[:, :], hs[:, t, :], ACT.Square,
                                         accum_out=head_sq[:, h % 2, t:t + 1]).then_inc(hsq_done, 1)
                act.wait_ge(hsq_done, TT * (h + 1))
                nc.scalar.activation(head_rstd[:, h % 2, :], head_sq[:, h % 2, :], ACT.Ln,
                                     bias=eps_col[:, 0:1], scale=1.0 / DV).then_inc(hln_done, 1)
                act.wait_ge(hln_done, h + 1)
                nc.scalar.activation(head_rstd[:, h % 2, :], head_rstd[:, h % 2, :], ACT.Exp,
                                     scale=-0.5).then_inc(hrstd_done, 1)
                act.wait_ge(hrstd_done, h + 1)
                for t in range(TT):
                    nc.scalar.mul(hs[:, t, :], hs[:, t, :], head_rstd[:, h % 2, t:t + 1]).then_inc(hsn_done, 1)

            def mlstm():
                log_exp_table()
                act.wait_ge(cols_ready, 2)

                def decays(h, piece):
                    n = 3 * h + piece
                    act.wait_ge(cm_ready, n + 1)
                    if h >= 2:
                        act.wait_ge(pv_ready, 12 * (h - 1))
                    for d, j in PIECES[piece]:
                        t0, w = span(d, j)
                        c0 = t0 if piece < 2 else t0 - 512 + 256 * d
                        nc.scalar.activation(decay[:, h % 2, d, OFF[d, j]:OFF[d, j] + w], bank[5][:, c0:c0 + w],
                                             ACT.Exp, bias=cols[:, j, 32 * d + h:32 * d + h + 1],
                                             scale=-1.0).then_inc(exp_done, 1)

                for piece in range(3):
                    decays(0, piece)
                for h in range(NH):
                    if h + 1 < NH:
                        decays(h + 1, 0)
                        decays(h + 1, 1)
                    if h:
                        y_high(0, h - 1, 0)
                        y_high(0, h - 1, 1)
                    if h + 1 < NH:
                        decays(h + 1, 2)
                    if h:
                        y_high(0, h - 1, 2)
                        y_high(0, h - 1, 3)
                    order = (3, 2, 1, 0, 5, 4)
                    if h == NH - 1:
                        split(POUT, 1)
                    head_norm(h, hs_m[:, h % 2], order,
                              lambda t: act.wait_ge(fin_done, 12 * h + OUTS.index((1, t)) + 1))
                for g in range(4):
                    y_high(0, NH - 1, g)

            def softplus(h, d, out):
                n = 2 * h + d
                act.wait_ge(z_abs, n + 1)
                nc.scalar.activation(out, out, ACT.Exp).then_inc(z_exp, 1)
                act.wait_ge(z_exp, n + 1)
                nc.scalar.activation(out, out, ACT.Ln, bias=ones[:, 0:1]).then_inc(z_ln, 1)

            def gla():
                def take_scores(h, g):
                    n = 3 * h + g
                    act.wait_ge(a_mm, n + 1)
                    if h:
                        act.wait_ge(o_mm, n - 2)
                    nc.scalar.copy(a_sb[:, g], bank[2 + g % 2][:, :]).then_inc(a_taken, 1)

                def take_keys(h, d):
                    n = 2 * h + d
                    act.wait_ge(kt_ready, n + 1)
                    if h:
                        act.wait_ge(u_ready, 2 * n - 2)
                    nc.scalar.copy(k_tok[:, d], bank[4 + 3 * d][:, :]).then_inc(kt_taken, 1)

                def exponentials(h, d):
                    sl = h % 2
                    if h:
                        act.wait_ge(state_step, 4 * (2 * h - 1 + d))
                        act.wait_ge(kt_ready, 2 * h)
                    act.wait_ge(step_ready, 2 * (2 * h + d) + 2)
                    nc.scalar.activation(step_exp[:, d], step_log[:, d, 1], ACT.Exp,
                                         scale=1.0 / GLA_TAU).then_inc(e_ready, 1)
                    act.wait_ge(centred, 2 * h + d + 1)
                    sums = bsum if h else b0_sum
                    nc.scalar.activation(qe[:, sl, d, :], sums[:, d, :], ACT.Exp,
                                         scale=1.0 / GLA_TAU).then_inc(e_ready, 1)
                    nc.scalar.activation(ke[:, sl, d, :], sums[:, d, :], ACT.Exp,
                                         scale=-1.0 / GLA_TAU).then_inc(e_ready, 1)

                def first_states(h, d):
                    n = 2 * h + d
                    if h and d == 0:
                        act.wait_ge(o_mm, 3 * h)
                    act.wait_ge(e_ready, 6 * h + 3 * d + 1)
                    for i in (0, 3):
                        act.wait_ge(u_ready, 2 * n + 1 + i // 2)
                        t = UPD[d][i]
                        nc.scalar.mul(s_piv[:, d, i, :], bank[5 - 5 * d + i // 2][:, (i % 2) * DV:(i % 2 + 1) * DV],
                                      step_exp[:, d, t - d:t - d + 1]).then_inc(first_state, 1)

                def output_norm(h, g):
                    n = 3 * h + g
                    ts = slice(2 * g, 2 * g + 2)
                    act.wait_ge(o_mm, n + 1)
                    for i in range(2):
                        act.wait_ge(hsq_done, TT * NH + 2 * n + i)
                        nc.scalar.activation(junk[:, :], bank[5 + g][:, i * DV:(i + 1) * DV], ACT.Square,
                                             accum_out=head_sq[:, h % 2, 2 * g + i:2 * g + i + 1]).then_inc(hsq_done, 1)
                    act.wait_ge(hsq_done, TT * NH + 2 * n + 2)
                    if h >= 2:
                        act.wait_ge(hsn_done, TT * (NH + h - 1))
                    nc.scalar.activation(head_rstd[:, h % 2, ts], head_sq[:, h % 2, ts], ACT.Ln,
                                         bias=eps_col[:, 0:1], scale=1.0 / DV).then_inc(hln_done, 1)
                    act.wait_ge(hln_done, NH + n + 1)
                    nc.scalar.activation(head_rstd[:, h % 2, ts], head_rstd[:, h % 2, ts], ACT.Exp,
                                         scale=-0.5).then_inc(hrstd_done, 1)

                log_exp_table()
                for s in range(2):
                    act.wait_ge(mm_done[s], 4 * (PAIRS + POUT))
                for d in range(2):
                    exponentials(0, d)
                for h in range(NH):
                    soft = [qe[:, (h + 1) % 2, d, :] for d in range(2)]
                    if h:
                        output_norm(h - 1, 2)
                    if h + 1 < NH:
                        softplus(h + 1, 0, soft[0])
                    take_scores(h, 0)
                    take_scores(h, 1)
                    take_keys(h, 0)
                    take_keys(h, 1)
                    if h + 1 < NH:
                        softplus(h + 1, 1, soft[1])
                    take_scores(h, 2)
                    for d in range(2):
                        first_states(h, d)
                    if h + 1 < NH:
                        for d in range(2):
                            exponentials(h + 1, d)
                    if h:
                        for g in range(4):
                            y_high(1, h - 1, g)
                    if h == NH - 1:
                        split(PAIRS + POUT, 1)
                    for d in range(2):
                        output_norm(h, d)
                output_norm(NH - 1, 2)
                for g in range(4):
                    y_high(1, NH - 1, g)

            def input_squares(half):
                for t in range(3 * half, 3 * half + 3):
                    act.wait_ge(x_loaded[t], 16)
                    if t:
                        act.wait_ge(x_sq_done, t)
                    nc.scalar.activation(w_hi[1][:, 0:D // W, :], xs[:, t, :].rearrange("p (k n) -> p k n", n=W),
                                         ACT.Square, accum_out=x_sq[:, t:t + 1]).then_inc(x_sq_done, 1)

            act.wait_ge(consts, 4)
            input_squares(0)
            act.wait_ge(gate_w_loaded, 16)
            act.wait_ge(gw_zero, 1)
            for a in range(2):
                src = gate_raw[:, :, 8 * a:8 * a + 8].rearrange("p k (b r) -> p k b r", b=2)
                dst = g_hi[:, :, :].rearrange("p k (b a r) -> p k b a r", b=2, a=2)[:, :, :, a, 0:4]
                nc.scalar.copy(dst, src).then_inc(gw_hi, 1)
            norm_rstd(0, 0)
            split(0, 0, wait=False)
            norm_high(0, 0, range(4))
            input_squares(1)
            norm_high(0, 0, range(4, 8))
            act.wait_ge(x_sq_done, TT)
            split(0, 1, wait=False)
            norm_rstd(0, 1)
            norm_high(0, 1)
            for L in range(2):
                q0 = PAIRS * L
                for kind in range(2):
                    q = q0 + kind
                    for s in range(2):
                        for g in range(4):
                            h = 2 * s + g % 2
                            src = take(q, s, g)
                            dst = (k_of if kind else q_of)[h][:, halves[g // 2]]
                            ins = nc.scalar.mul(dst, src, 1.0 if kind else float(DK) ** -0.5)
                            ins.then_inc(taken[s], 1)
                            if s == 1 and g == 0:
                                split(q + 1, 0)
                    if kind == 0:
                        split(q + 1, 1)
                if L == 0:
                    act.wait_ge(gate_rows, 2)
                    nc.scalar.activation(g_soft[64:100, :], g_pre[64:100, :], ACT.Abs).then_inc(gate_act, 1)
                    act.wait_ge(gate_act, 1)
                    nc.scalar.activation(g_soft[64:100, :], g_soft[64:100, :], ACT.Exp, scale=-1.0).then_inc(gate_act, 1)
                    act.wait_ge(gate_act, 2)
                    nc.scalar.activation(g_soft[64:100, :], g_soft[64:100, :], ACT.Ln,
                                         bias=ones[64:100, 0:1]).then_inc(gate_act, 1)
                    act.wait_ge(gate_dve, 11)
                    nc.scalar.activation(g_cols[64:100, :], g_log[0:36, :], ACT.Exp, scale=-1.0).then_inc(gate_act, 1)
                if L == 1:
                    log_exp_table()
                    softplus(0, 0, ht[:, 2:4, :])
                with act.Fori(0, 2) as i:
                    for s in range(2):
                        q = i + q0 + PVAL
                        if s == 0:
                            split(q, 1)
                        else:
                            split(q + 1, 0)
                        for g in range(3):
                            act.wait_ge(mm_done[s], 4 * q + (g + 1 + (g == 2)))
                            dst = v_all[:, bass.ds(i * 2 + s, 1), 2 * g:2 * g + 2, 0:DV]
                            src = bank[4 * s + g][:, :].rearrange("p (a t n) -> p a t n", a=1, t=2)
                            nc.scalar.copy(dst, src).then_inc(taken[s], 2 if g == 2 else 1)
                if L == 0:
                    act.wait_ge(cols_ready, 2)
                else:
                    log_exp_table()
                    softplus(0, 1, ht[:, 2:4, :])
                with act.Fori(0, 2) as i:
                    for s in range(2):
                        q = i + q0 + PO
                        if s == 0:
                            split(q, 1)
                        else:
                            split(q + 1, 0)
                        for g in range(4):
                            src = take(q, s, g)
                            dst = o_gate[:, bass.ds(i * 4 + (2 * s + g % 2), 1), halves[g // 2]]
                            nc.scalar.activation(dst, src, ACT.Silu if L else ACT.Sigmoid).then_inc(taken[s], 1)
                (gla if L else mlstm)()
                split(q0 + POUT + 1, 0)
                split(q0 + POUT + 1, 1)
                split(q0 + PGU[0], 0)
                norm(2 * L + 1, q0 + PGU[0])
                for b, nb in enumerate(BLOCKS):
                    with act.Fori(0, nb // 2) as i:
                        q = i + q0 + PGU[b]
                        for g in range(4):
                            act.wait_ge(taken[1], 4 * q + (g - 3))
                            src = take(q, 0, g)
                            nc.scalar.activation(sg[:, g, :], src, ACT.Silu).then_inc(taken[0], 1)
                        split(q + 1, 0)
                        split(q + 1, 1)
                    if L == 0 and b == 0:
                        act.wait_ge(gate_w_loaded, 32)
                        act.wait_ge(gw_zero, 2)
                        src = gate_raw[:, :, :].rearrange("p k (b r) -> p k b r", b=1)
                        dst = g_hi[:, :, :].rearrange("p k (b r) -> p k b r", b=4)[:, :, 0:3, :]
                        nc.scalar.copy(dst, src.to_broadcast([P, KC, 3, 2 * RANK])).then_inc(gw_hi, 1)
                    if L == 0 and b == 1:
                        act.wait_ge(a2_loaded, 16 * 6)
                        act.wait_ge(gw_lo, 3)
                        nc.scalar.copy(w_a2[:, :, :], w_a2_raw[:, :, :]).then_inc(a2_split, 1)
                    if b < 2:
                        with act.Fori(0, 2) as i:
                            for s in range(2):
                                split(i + q0 + PDN[b] + 1, s)
                    else:
                        split(q0 + PDN[b] + 1, 0)
                        split(q0 + PDN[b] + 1, 1)
                        if L == 0:
                            split(PAIRS, 0)
                if L == 0:
                    norm(2, PAIRS)
            nc.scalar.preload_act_table(ACT.Sqrt)
            act.wait_ge(sq_acc, 63)
            for half in range(2):
                if half == 1:
                    act.wait_ge(taken[1], 8 * PAIRS)
                    nc.scalar.activation(sq_new[:, :], xT[:, KC - 1, halves[1]], ACT.Square).then_inc(last_sq, 1)
                ts = slice(3 * half, 3 * half + 3)
                act.wait_ge(tok_sum, half + 1)
                nc.scalar.activation(rms[:, 0, ts], bank[0 if half == 0 else 5][:, ts], ACT.Sqrt,
                                     bias=eps_col[:, 0:1], scale=1.0 / D).then_inc(rms_done, 1)
                for t in range(3 * half, 3 * half + 3):
                    act.wait_ge(rms_inv, half + 1)
                    act.wait_ge(fin_t, 2 * t + 1)
                    nc.scalar.mul(y_tok[:, t, 0:512], bank[1 + 2 * t % 4][:, :], rms[:, 1, t:t + 1]
                                  ).then_inc(fin_copied[0], 1)

        @block.vector
        def _(dve):
            V = nc.vector

            def split(q, s):
                dve.wait_ge(w_hi_ready, 2 * q + s + 1)
                V.tensor_tensor(w_lo[s][:, :, :], raw[s][:, :, :], w_hi[s][:, :, :].bitcast(F32),
                                ALU.subtract).then_inc(w_lo_ready, 1)

            def ring(s):
                if s >= 4:
                    dve.wait_ge(lo_ready, s - 3)

            def norm_half(e, half, chunks=range(KC)):
                dve.wait_ge(rstd_done, 2 * e + half + 1)
                for c in chunks:
                    s = NORM_S[e] + 8 * half + c
                    ring(s)
                    V.scalar_tensor_tensor(out=ht[:, s % 4, :], in0=xT[:, c, halves[half]], scalar=gain[e][:, c:c + 1],
                                           in1=rstd[:, half, :], op0=ALU.mult, op1=ALU.mult).then_inc(ht_ready, 1)

            def add_residual(q, s, g, c):
                dve.wait_ge(mm_done[s], 4 * q + (g + 1))
                dve.wait_ge(taken[s], 4 * q + g)
                hs = halves[g // 2]
                if isinstance(c, int):
                    x, src = xT[:, c, hs], bank[4 * s + g][:, 0:HT]
                else:
                    x = xT[:, bass.ds(c, 1), hs]
                    src = bank[4 * s + g][:, 0:HT].rearrange("p (a n) -> p a n", a=1)
                V.tensor_tensor(x, x, src, ALU.add).then_inc(taken[s], 1)

            def y_take(L, h, g, b):
                s = Y_S[L] + 4 * h + g
                c = 2 * h + g % 2
                dve.wait_ge(tr_ready, 16 * L + 4 * h + g + 1)
                ring(s)
                V.scalar_tensor_tensor(out=ht[:, s % 4, :], in0=bank[b][:, 0:HT], scalar=head_g[L][:, c:c + 1],
                                       in1=o_gate[:, c, halves[g // 2]], op0=ALU.mult,
                                       op1=ALU.mult).then_inc(ht_ready, 1)

            def mlstm():
                row = (lambda d, h: 32 * d + h)

                def weights(h, k, piece):
                    n = 12 * h + 4 * piece + k
                    d, j = PIECES[piece][k]
                    t0, w = span(d, j)
                    dve.wait_ge(mask_done, n + 1)
                    dve.wait_ge(st_ready, TT * h + (j + 1 if j < 4 else TT))
                    first = FIRST_T[j] * P
                    src = bank[j][:, t0 - first:t0 - first + w] if j < 4 else \
                        bank[4][:, (j - 4) * 256 + t0 - first:(j - 4) * 256 + t0 - first + w]
                    at_d = decay[:, h % 2, d, OFF[d, j]:OFF[d, j] + w]
                    V.tensor_tensor(at_d, at_d, src, ALU.mult).then_inc(p_ready, 1)

                def denominator(n):
                    d, t = OUTS[n % 12]
                    b, dn = bank[OUT_BANKS[n]], den[:, n % 2, :]
                    r = 64 + row(d, n // 12)

                    def largest():
                        dve.wait_ge(pv_ready, n + 1)
                        if n >= 2:
                            dve.wait_ge(fin_done, n - 1)
                        V.tensor_scalar(dn[:, 0:1], b[:, DV:DV + 1], -1.0, cols[:, t, r:r + 1], ALU.mult, ALU.max
                                        ).then_inc(den_step, 1)

                    def inverse():
                        dve.wait_ge(den_step, 3 * n + 1)
                        V.tensor_scalar(dn[:, 0:1], b[:, DV:DV + 1], dn[:, 0:1], None, ALU.max).then_inc(den_step, 1)
                        dve.wait_ge(den_step, 3 * n + 2)
                        V.reciprocal(dn[:, 1:2], dn[:, 0:1]).then_inc(den_step, 1)

                    return largest, inverse

                def finish(n):
                    d, t = OUTS[n % 12]
                    b, dn = bank[OUT_BANKS[n]], den[:, n % 2, :]
                    out = hs_m[:, n // 12 % 2, t, :]
                    dve.wait_ge(den_step, 3 * n + 3)
                    if d == 0:
                        if n >= 24:
                            dve.wait_ge(tr_ready, 4 * (n // 12 - 1))
                        V.tensor_scalar(out, b[:, 0:DV], dn[:, 1:2], None, ALU.mult).then_inc(fin_done, 1)
                    else:
                        dve.wait_ge(fin_done, 12 * (n // 12) + OUTS.index((0, t)) + 1)
                        V.scalar_tensor_tensor(out=out, in0=b[:, 0:DV], scalar=dn[:, 1:2], in1=out,
                                               op0=ALU.mult, op1=ALU.add).then_inc(fin_done, 1)

                for piece in range(2):
                    for k in range(4):
                        weights(0, k, piece)
                for h in range(NH):
                    for k in range(4):
                        weights(h, k, 2)
                    for i in range(12):
                        n = 12 * h + i
                        if h and i - 1 in TURN_AT:
                            for g in range(2):
                                g += 2 * TURN_AT.index(i - 1)
                                y_take(0, h - 1, g, g)
                        largest, inverse = denominator(n)
                        after_scores = h + 1 < NH and i == SCORES_AT + 1
                        if after_scores:
                            finish(n - 1)
                            for k in range(4):
                                weights(h + 1, k, 0)
                        largest()
                        if i and not after_scores:
                            finish(n - 1)
                        inverse()
                        if h + 1 < NH and i > SCORES_AT + 1:
                            for k in ((0, 1), (2,), (3,))[i - SCORES_AT - 2]:
                                weights(h + 1, k, 1)
                    finish(12 * h + 11)
                split(POUT, 1)
                for g in range(4):
                    y_take(0, NH - 1, g, 4 + g)

            def logits(h, d, banks, out):
                for half in range(2):
                    dve.wait_ge(z_ready, 4 * h + 2 * d + half + 1)
                    V.tensor_scalar(out[half], bank[banks[half]][:, 0:HT],
                                    b_a[:, 4 * d + h:4 * d + h + 1], None, ALU.add).then_inc(z_taken, 1)

            def minus_abs(h, d, z, out):
                dve.wait_ge(z_taken, 2 * (2 * h + d) + 2)
                V.scalar_tensor_tensor(out=out, in0=z, scalar=-1.0, in1=z, op0=ALU.mult, op1=ALU.min
                                       ).then_inc(z_abs, 1)

            def log_gates(h, d, z, soft, sums):
                dve.wait_ge(z_ln, 2 * h + d + 1)
                V.scalar_tensor_tensor(out=soft, in0=z, scalar=0.0, in1=soft, op0=ALU.min, op1=ALU.subtract
                                       ).then_inc(lg_ready, 1)
                dve.wait_ge(lg_ready, 2 * h + d + 1)
                if h:
                    dve.wait_ge(e_ready, 6 * h)
                for t in range(TT):
                    lo = t * P
                    ts = slice(lo, lo + P) if d == 0 else slice(lo + P - 1, lo - 1 if t else None, -1)
                    V.tensor_tensor_scan(sums[:, ts], ones[:, :], soft[:, ts], 0.0,
                                         ALU.mult, ALU.add).then_inc(scanned, 1)

            def pivots(h, d, sums):
                dve.wait_ge(scanned, TT * (2 * h + d + 1))
                n = 2 * h + d
                b_t = sums.rearrange("p (c t) -> p c t", t=P)
                end = P - 1 if d == 0 else 0
                V.tensor_copy(piv[:, d, :], b_t[:, :, PIVOT]).then_inc(piv_ready, 1)
                dve.wait_ge(piv_ready, n + 1)
                if h:
                    dve.wait_ge(e_ready, 6 * h)
                cur, nxt = slice(d, TT - 1 + d), slice(1 - d, TT - d)
                V.tensor_tensor(step_log[:, d, 0, :], b_t[:, cur, end], piv[:, d, cur], ALU.subtract
                                ).then_inc(step_ready, 1)
                dve.wait_ge(step_ready, 2 * n + 1)
                V.tensor_tensor(step_log[:, d, 1, :], step_log[:, d, 0, :], piv[:, d, nxt], ALU.add
                                ).then_inc(step_ready, 1)
                c = piv[:, d, :].rearrange("p (c a) -> p c a", a=1).to_broadcast([P, TT, P])
                V.tensor_tensor(b_t, b_t, c, ALU.subtract
                                ).then_inc(centred, 1)

            def gla():
                def states(h, d):
                    n = 2 * h + d
                    dve.wait_ge(e_ready, 6 * h + 3 * d + 1)
                    u = [bank[5 - 5 * d + i // 2][:, (i % 2) * DV:(i % 2 + 1) * DV] for i in range(4)]
                    f = [step_exp[:, d, t - d:t - d + 1] for t in UPD[d]]
                    st = state[:, d, :]
                    for i in (1, 2):
                        dve.wait_ge(first_state, 2 * n + i)
                        if i == 2:
                            dve.wait_ge(state_step, 4 * n + 2)
                        V.tensor_tensor(st, s_piv[:, d, i - 1, :], u[i], ALU.add).then_inc(state_step, 1)
                        dve.wait_ge(state_step, 4 * n + 2 * i - 1)
                        V.tensor_scalar(s_piv[:, d, i, :], st, f[i], None, ALU.mult).then_inc(state_step, 1)

                def sum_directions(h, g):
                    n = 3 * h + g
                    dve.wait_ge(a_masked, 2 * n + 2)
                    a = a_sb[:, g]
                    V.tensor_tensor(a[:, :, 0, :], a[:, :, 0, :], a[:, :, 1, :], ALU.add).then_inc(a_summed, 1)

                def take_outputs(h, g):
                    dve.wait_ge(hrstd_done, NH + 3 * h + g + 1)
                    if h >= 2:
                        dve.wait_ge(tr_ready, 16 + 4 * (h - 1))
                    for i in range(2):
                        t = 2 * g + i
                        V.tensor_scalar(hs_g[h % 2][:, t, :], bank[5 + g][:, i * DV:(i + 1) * DV],
                                        head_rstd[:, h % 2, t:t + 1], None, ALU.mult).then_inc(hsn_done, 1)

                def head_logits(h, ds=range(2)):
                    if h >= 2:
                        dve.wait_ge(kt_ready, 2 * (h - 1))
                    for d in ds:
                        logits(h, d, (3 * d, 3 * d + 1), [ke[:, h % 2, d, hs] for hs in halves])

                for d in range(2):
                    dve.wait_ge(e_ready, 3 * d + 3)
                    k_of_0 = ke[:, 0, d, :]
                    V.tensor_tensor(k_of_0, k_of_0, k_of[0], ALU.mult).then_inc(qk_ready, 1)
                    head_logits(1, (d,))
                for h in range(NH):
                    sl = (h + 1) % 2
                    more = h + 1 < NH
                    if more:
                        if h:
                            dve.wait_ge(o_mm, 3 * h)
                        for d in range(2):
                            minus_abs(h + 1, d, ke[:, sl, d, :], qe[:, sl, d, :])
                    if h:
                        take_outputs(h - 1, 2)
                    if more:
                        log_gates(h + 1, 0, ke[:, sl, 0, :], qe[:, sl, 0, :], bsum[:, 0, :])
                    for g in range(2):
                        sum_directions(h, g)
                    if more:
                        pivots(h + 1, 0, bsum[:, 0, :])
                    for d in range(2):
                        states(h, d)
                    sum_directions(h, 2)
                    if more:
                        log_gates(h + 1, 1, ke[:, sl, 1, :], qe[:, sl, 1, :], bsum[:, 1, :])
                        pivots(h + 1, 1, bsum[:, 1, :])
                    if h:
                        for g in range(4):
                            y_take(1, h - 1, g, TURN[g])
                    if h + 2 < NH:
                        head_logits(h + 2)
                    if not more:
                        split(PAIRS + POUT, 1)
                    take_outputs(h, 0)
                    take_outputs(h, 1)
                take_outputs(NH - 1, 2)
                for g in range(4):
                    y_take(1, NH - 1, g, 4 + g)

            V.memset(ones[:, :], 1.0).then_inc(consts, 1)
            V.memset(eps_col[:, :], EPS).then_inc(consts, 1)
            dve.wait_ge(consts, 4)
            V.tensor_tensor(sel[:, :], ident[0:100, 0:36], ident[0:100, 64:100], ALU.add)
            dve.wait_ge(vec_t, 1)
            V.tensor_copy(vec[:, :], bank[7][:, 0:64]).then_inc(vec_ready, 1)
            dve.wait_ge(vec_ready, 1)

            def input_sums(half):
                for t in range(3):
                    dve.wait_ge(x_sq_done, 3 * half + t + 1)
                    V.tensor_scalar(sq_sum[:, half, t * P:(t + 1) * P], ident[:, :],
                                    x_sq[:, 3 * half + t:3 * half + t + 1], None, ALU.mult).then_inc(x_diag, 1)

            def input_chunks(half, chunks=range(KC)):
                for c in chunks:
                    dve.wait_ge(x_t, 8 * half + c + 1)
                    V.tensor_copy(xT[:, c, halves[half]], bank[X_BANK[half][c]][:, 0:HT]).then_inc(x_taken, 1)

            input_sums(0)
            input_chunks(0)
            for a in range(2):
                dve.wait_ge(gw_hi, a + 1)
                src = gate_raw[:, :, 8 * a:8 * a + 8].rearrange("p k (b r) -> p k b r", b=2)
                hi = g_hi[:, :, :].rearrange("p k (b a r) -> p k b a r", b=2, a=2)[:, :, :, a, 0:4]
                lo = g_lo[:, :, :].rearrange("p k (b a r) -> p k b a r", b=2, a=2)[:, :, :, a, 0:4]
                V.tensor_tensor(lo, src, hi.bitcast(F32), ALU.subtract).then_inc(gw_lo, 1)
            dve.wait_ge(x_taken, 8)
            norm_half(0, 0, range(4))
            input_chunks(1, range(3))
            split(0, 0)
            norm_half(0, 0, range(4, 6))
            input_chunks(1, range(3, 5))
            input_sums(1)
            norm_half(0, 0, range(6, 8))
            input_chunks(1, range(5, 8))
            dve.wait_ge(x_taken, 16)
            split(0, 1)
            norm_half(0, 1, range(4))

            def gates_taken(L, half):
                dve.wait_ge(gate_mm, 2 * L + half + 1)
                if L == 0:
                    dve.wait_ge(bias_loaded, 64)
                    V.tensor_scalar(g_pre[0:100, halves[half]], bank[4 + half][0:100, 0:HT],
                                    gate_bias[0:100, 0:1], None, ALU.add).then_inc(gate_rows, 1)
                else:
                    src, dst = bank[4 + half][:, 0:HT], rows_g[:, halves[half]]
                    V.tensor_copy(dst, src[0:96, :]).then_inc(rows_hi, 1)
                    dve.wait_ge(rows_hi, half + 3)
                    V.tensor_tensor(dst[64:96, :], src[64:96, :], dst[64:96, :].bitcast(F32), ALU.subtract
                                    ).then_inc(gate_rows, 1)

            for L in range(2):
                q0 = PAIRS * L
                if L == 0:
                    gates_taken(0, 0)
                    norm_half(0, 1, range(4, 8))
                gates_taken(L, 1)
                split(q0 + 1, 0)
                split(q0 + 1, 1)
                split(q0 + 2, 0)
                if L == 0:
                    def step(ins):
                        ins.then_inc(gate_dve, 1)

                    one = ones[0:36, 0:1]
                    dve.wait_ge(gate_act, 3)
                    step(V.scalar_tensor_tensor(out=g_log[0:36, :], in0=g_pre[64:100, :], scalar=0.0,
                                                in1=g_soft[64:100, :], op0=ALU.min, op1=ALU.subtract))
                    dve.wait_ge(gate_dve, 1)
                    for p in (slice(0, 36), slice(32, 36)):
                        for n_s, (a, b) in enumerate(((0, SEQS[0]), (SEQS[0], T))):
                            ts = slice(a, b) if p.start == 0 else slice(b - 1, a - 1 if a else None, -1)
                            step(V.tensor_tensor_scan(g_cum[p, ts], ones[p, 0:1].to_broadcast([p.stop - p.start, b - a]),
                                                      g_log[p, ts], 0.0, ALU.mult, ALU.add))
                        dve.wait_ge(gate_dve, 3 if p.start == 0 else 5)
                    dve.wait_ge(gw_zero, 1)
                    step(V.tensor_tensor(g_cols[0:36, :], g_pre[0:36, :], g_cum[0:36, :], ALU.subtract))
                    dve.wait_ge(gate_dve, 6)
                    for p in (slice(0, 36), slice(32, 36)):
                        for a, b in ((0, SEQS[0]), (SEQS[0], T)):
                            ts = slice(a, b) if p.start == 0 else slice(b - 1, a - 1 if a else None, -1)
                            step(V.tensor_tensor_scan(g_soft[p, ts], ones[p, 0:1].to_broadcast([p.stop - p.start, b - a]),
                                                      g_cols[p, ts], M_INIT, ALU.mult, ALU.max))
                        dve.wait_ge(gate_dve, 8 if p.start == 0 else 10)
                    step(V.tensor_tensor(g_log[0:36, :], g_cum[0:36, :], g_soft[0:36, :], ALU.add))
                    V.memset(rows_m[32:64, :].bitcast(mybir.dt.uint32), 0).then_inc(rows_hi, 1)
                    dve.wait_ge(rows_hi, 1)
                    V.tensor_copy(rows_m[0:36, :], g_soft[0:36, :]).then_inc(rows_hi, 1)
                    dve.wait_ge(rows_hi, 2)
                    V.tensor_tensor(rows_m[64:100, :], g_soft[0:36, :], rows_m[0:36, :].bitcast(F32), ALU.subtract)
                    V.memset(v_all[:, :, :, DV:DV + 1], 1.0).then_inc(v_ones, 1)
                def first_gates(d):
                    flat = ht[:, :, :].rearrange("p a n -> p (a n)")
                    minus_abs(0, d, flat[:, 0:T], flat[:, T:2 * T])
                    log_gates(0, d, flat[:, 0:T], flat[:, T:2 * T], b0_sum[:, d, :])
                    pivots(0, d, b0_sum[:, d, :])

                if L == 1:
                    logits(0, 0, (3, 7), [ht[:, 0, :], ht[:, 1, :]])
                    first_gates(0)
                with dve.Fori(0, 2) as i:
                    split(i + q0 + PVAL, 1)
                    split(i + (q0 + PVAL + 1), 0)
                if L == 0:
                    dve.wait_ge(cols_t, 1)
                    for k in range(2):
                        V.tensor_copy(cols[:, 3 * k:3 * k + 3, :],
                                      bank[3 + 4 * k][:, 0:300].rearrange("p (t r) -> p t r", t=3)).then_inc(cols_ready, 1)
                else:
                    dve.wait_ge(scanned, TT)
                    logits(0, 1, (3, 7), [ht[:, 0, :], ht[:, 1, :]])
                    first_gates(1)
                with dve.Fori(0, 2) as i:
                    split(i + q0 + PO, 1)
                    split(i + (q0 + PO + 1), 0)
                (gla if L else mlstm)()

                def last_pair(q, c, e):
                    for g in range(4):
                        add_residual(q, 0, g, c + g % 2)
                    split(q + 1, 0)
                    for g in range(3):
                        add_residual(q, 1, g, c + 2 + g % 2)
                    norm_half(e, 0)
                    add_residual(q, 1, 3, c + 3)
                    split(q + 1, 1)
                    if e == 2:
                        gates_taken(1, 0)
                    norm_half(e, 1)

                def final_pair(q):
                    def scaled(c, half):
                        V.tensor_scalar(y_fin[:, c, halves[half]], xT[:, c, halves[half]], gain[4][:, c:c + 1], None,
                                        ALU.mult).then_inc(fin_scaled, 1)

                    for g in range(4):
                        add_residual(q, 0, g, 4 + g % 2)
                    dve.wait_ge(taken[0], 4 * q + 4)
                    for half in range(2):
                        for c in range(6):
                            scaled(c, half)
                    for g in range(4):
                        add_residual(q, 1, g, 6 + g % 2)
                        dve.wait_ge(taken[1], 4 * q + g + 1)
                        scaled(6 + g % 2, g // 2)

                def pair(q, c):
                    for g in range(4):
                        add_residual(q, 0, g, c + g % 2)
                    split(q + 1, 0)
                    for g in range(4):
                        add_residual(q, 1, g, c + (2 + g % 2))
                    split(q + 1, 1)

                pair(q0 + POUT, 0)
                last_pair(q0 + POUT + 1, 4, 2 * L + 1)
                for b, nb in enumerate(BLOCKS):
                    with dve.Fori(0, nb // 2) as i:
                        q = i + q0 + PGU[b]
                        f = i + (FFP * L + sum(BLOCKS[:b]) // 2)
                        split(q + 1, 0)
                        for g in range(4):
                            dve.wait_ge(mm_done[1], 4 * q + (g + 1))
                            dve.wait_ge(taken[0], 4 * q + (g + 1))
                            dve.wait_ge(a_ready, 4 * f + (g + 1))
                            V.tensor_tensor(at[:, g, :], sg[:, g, :], bank[4 + g][:, 0:HT], ALU.mult
                                            ).then_inc(taken[1], 1)
                        split(q + 1, 1)
                    if L == 0 and b == 0:
                        dve.wait_ge(gw_hi, 3)
                        src = gate_raw[:, :, :].rearrange("p k (b r) -> p k b r", b=1)
                        hi = g_hi[:, :, :].rearrange("p k (b r) -> p k b r", b=4)[:, :, 0:3, :]
                        lo = g_lo[:, :, :].rearrange("p k (b r) -> p k b r", b=4)[:, :, 0:3, :]
                        V.tensor_tensor(lo, src.to_broadcast([P, KC, 3, 2 * RANK]), hi.bitcast(F32), ALU.subtract
                                        ).then_inc(gw_lo, 1)
                    if L == 0 and b == 1:
                        dve.wait_ge(a2_split, 1)
                        w = w_a2[32:64, :, :]
                        V.tensor_tensor(w, w_a2_raw[32:64, :, :], w.bitcast(F32), ALU.subtract).then_inc(a2_split, 1)
                    if b < 2:
                        with dve.Fori(0, 2) as i:
                            pair(i + q0 + PDN[b], i * 4)
                    else:
                        pair(q0 + PDN[b], 0)
                        if L == 0:
                            last_pair(q0 + PDN[b] + 1, 4, 2)
                        else:
                            final_pair(q0 + PDN[b] + 1)
            for half in range(2):
                ts = slice(3 * half, 3 * half + 3)
                dve.wait_ge(rms_done, half + 1)
                V.reciprocal(rms[:, 1, ts], rms[:, 0, ts]).then_inc(rms_inv, 1)
                dve.wait_ge(rms_inv, half + 1)
                for t in range(3 * half, 3 * half + 3):
                    dve.wait_ge(fin_t, 2 * t + 2)
                    V.tensor_scalar(y_tok[:, t, 512:D], bank[1 + (2 * t + 1) % 4][:, :], rms[:, 1, t:t + 1], None,
                                    ALU.mult).then_inc(fin_copied[1], 1)

        @block.gpsimd
        def _(pool):
            G = nc.gpsimd

            sq_steps = [1]

            def square(src, first, half, n):
                if first:
                    G.tensor_tensor(sq_sum[:, half, :], src, src, ALU.mult).then_inc(sq_acc, 1)
                    return
                pool.wait_ge(sq_acc, n)
                G.tensor_tensor(sq_new[:, :], src, src, ALU.mult).then_inc(sq_mul, 1)
                sq_steps[0] += 1
                pool.wait_ge(sq_mul, sq_steps[0])
                G.tensor_tensor(sq_sum[:, half, :], sq_sum[:, half, :], sq_new[:, :], ALU.add).then_inc(sq_acc, 1)

            def low(s, out, hi):
                pool.wait_ge(hi_ready, s + 1)
                G.tensor_tensor(out, ht[:, s % 4, :], hi.bitcast(F32), ALU.subtract).then_inc(lo_ready, 1)

            def norm_low(e, half):
                for c in range(KC):
                    low(NORM_S[e] + 8 * half + c, h_lo[:, c, halves[half]], h_hi[:, c, halves[half]])

            def y_low(L, h, g):
                c, hs = 2 * h + g % 2, halves[g // 2]
                low(Y_S[L] + 4 * h + g, y_lo[c][:, hs], y_hi[c][:, hs])

            def squares(q, e):
                for n in range(16 if e < 4 else 15):
                    i, s, g = n // 8, n // 4 % 2, n % 4
                    c = 4 * i + 2 * s + g % 2
                    if n == 15:
                        norm_low(e, 0)
                    if c == 0:
                        pool.wait_ge(ss_done, 2 * (e - 1) + g // 2 + 1)
                    pool.wait_ge(taken[s], 4 * (q + i) + g + 1)
                    square(xT[:, c, halves[g // 2]], c == 0, g // 2, 16 * (e - 1) + n)
                if e < 4:
                    norm_low(e, 1)

            def causal(ap, d, tiles, done):
                sign = 1 if d == 0 else -1
                pat = [[sign, P]] if tiles == 1 else [[0, tiles], [sign, P]]
                G.affine_select(out=ap, in_=ap, pattern=pat, compare_op=ALU.is_ge, fill=0.0, base=0,
                                channel_multiplier=-sign).then_inc(done, 1)

            def mlstm():
                def masks(h, piece):
                    for k, (d, j) in enumerate(PIECES[piece]):
                        pool.wait_ge(exp_done, 12 * h + 4 * piece + k + 1)
                        c = OFF[d, j] + (0 if d == 0 else span(d, j)[1] - P)
                        causal(decay[:, h % 2, d, c:c + P], d, 1, mask_done)

                for piece in range(3):
                    masks(0, piece)
                for h in range(NH):
                    if h + 1 < NH:
                        masks(h + 1, 0)
                        masks(h + 1, 1)
                    if h:
                        y_low(0, h - 1, 0)
                        y_low(0, h - 1, 1)
                    if h + 1 < NH:
                        masks(h + 1, 2)
                    if h:
                        y_low(0, h - 1, 2)
                        y_low(0, h - 1, 3)
                for g in range(4):
                    y_low(0, NH - 1, g)

            def gla():
                def scale_qk(h, d):
                    for i, (part, of) in enumerate(((qe, q_of), (ke, k_of))[:2 if h else 1]):
                        pool.wait_ge(e_ready, 6 * h + 3 * d + i + 2)
                        p = part[:, h % 2, d, :]
                        G.tensor_tensor(p, p, of[h], ALU.mult).then_inc(qk_ready, 1)

                def masks(h, g):
                    n = 3 * h + g
                    pool.wait_ge(a_taken, n + 1)
                    for d in range(2):
                        causal(a_sb[:, g, :, d, :], d, 2, a_masked)

                for d in range(2):
                    scale_qk(0, d)
                for h in range(NH):
                    for g in range(3):
                        masks(h, g)
                    if h + 1 < NH:
                        scale_qk(h + 1, 0)
                        scale_qk(h + 1, 1)
                    if h:
                        for g in range(4):
                            y_low(1, h - 1, g)
                for g in range(4):
                    y_low(1, NH - 1, g)

            G.memset(ident[:, :], 0.0).then_inc(sq_mul, 1)
            pool.wait_ge(sq_mul, 1)
            G.affine_select(out=ident[:, :], in_=ident[:, :], compare_op=ALU.not_equal, fill=1.0, base=0,
                            pattern=[[-1, P]], channel_multiplier=1).then_inc(consts, 1)
            G.memset(gate_bias[:, :], 0.0).then_inc(consts, 1)
            G.memset(den[:, :], 0.0).then_inc(a_ready, 4)
            G.memset(g_cols[:, :], 0.0)
            G.memset(g_hi[:, :, :].bitcast(mybir.dt.uint32), 0)
            G.memset(g_lo[:, :, :].bitcast(mybir.dt.uint32), 0).then_inc(gw_zero, 1)
            for half in range(2):
                norm_low(0, half)
            for L in range(2):
                q0 = PAIRS * L
                (gla if L else mlstm)()
                squares(q0 + POUT, 2 * L + 1)
                for b, nb in enumerate(BLOCKS):
                    with pool.Fori(0, nb // 2) as i:
                        q = i + q0 + PGU[b]
                        f = i + (FFP * L + sum(BLOCKS[:b]) // 2)
                        for g in range(4):
                            c = bass.ds(i * 2 + g % 2, 1)
                            hs = halves[g // 2]
                            src = at[:, g:g + 1, :]
                            pool.wait_ge(taken[1], 4 * q + (g + 1))
                            G.tensor_copy(a_hi[:, c, hs], src).then_inc(a_hi_done, 1)
                            pool.wait_ge(a_hi_done, 4 * f + (g + 1))
                            G.tensor_tensor(a_lo[:, c, hs], src, a_hi[:, c, hs].bitcast(F32),
                                            ALU.subtract).then_inc(a_ready, 1)
                    if L == 0 and b == 0:
                        G.memset(g_hi[:, :, :].bitcast(mybir.dt.uint32), 0)
                        G.memset(g_lo[:, :, :].bitcast(mybir.dt.uint32), 0).then_inc(gw_zero, 1)
                        G.memset(w_a2_raw[:, :, :], 0.0).then_inc(a2_zero, 1)
                squares(q0 + PDN[2], 2 * L + 2)


_INS = ["x_prompt", "x_sample", "norm_mix_g", "norm_ffn_g", "norm_final_g", "mlstm_w_in", "mlstm_b_gate",
        "mlstm_head_g", "mlstm_w_out", "gla_w_in", "gla_w_a2", "gla_b_a", "gla_head_g", "gla_w_out",
        "ffn_w_gu", "ffn_w_down"]
_OUTS = [(1, SEQS[0], D), (1, SEQS[1], D)]


def kernel(**inputs):
    import numpy as _np
    import concourse.bacc as _bacc
    from concourse.bass_utils import run_bass_kernel_spmd as _run

    nc = _bacc.Bacc("TRN2", target_bir_lowering=False, num_devices=1, dynamic_dma_scratch_size=1024)
    arrays, args = {}, []
    for name in _INS:
        a = _np.ascontiguousarray(inputs[name])
        arrays[f"in_{name}_dram"] = a
        args.append(nc.dram_tensor(f"in_{name}_dram", a.shape, mybir.dt.from_np(a.dtype), kind="ExternalInput").ap())
    for i, shape in enumerate(_OUTS):
        args.append(nc.dram_tensor(f"out_{i}_dram", shape, F32, kind="ExternalOutput").ap())
    build(nc, *args)
    r = _run(nc, [arrays], core_ids=[0])
    return tuple(r.results[0][f"out_{i}_dram"] for i in range(len(_OUTS)))
```
